# Optimizing a Trainium2 kernel written in Bass

```python
import numpy as np
import jax
import jax.numpy as jnp
from jax import lax

D_MODEL = 1024
BATCH = 1
SEQ = 512
DEPTH = 2

CHUNK = 64
MEM_LEN = 256
EPS = 1e-6
RET_HEADS = 4
RET_QK_DIM = 128
RET_V_DIM = 256
RET_QK = RET_HEADS * RET_QK_DIM
RET_V = RET_HEADS * RET_V_DIM
ROPE_THETA = 10000.0
SSM_INNER = 2 * D_MODEL
SSM_HEAD_DIM = 64
SSM_HEADS = SSM_INNER // SSM_HEAD_DIM
SSM_GROUPS = 8
SSM_HEADS_PER_GROUP = SSM_HEADS // SSM_GROUPS
SSM_STATE = 128
SSM_CONV = 4
SSM_BC = SSM_GROUPS * SSM_STATE
SSM_CONV_DIM = SSM_INNER + 2 * SSM_BC
N_BRANCH = 2
IN_SIZES = (RET_QK, RET_QK, RET_V, RET_V, SSM_INNER, SSM_CONV_DIM, SSM_HEADS, N_BRANCH * D_MODEL)
IN_DIM = RET_QK + RET_QK + RET_V + RET_V + SSM_INNER + SSM_CONV_DIM + SSM_HEADS + N_BRANCH * D_MODEL
XA_HEADS = 4
XA_HEAD_DIM = D_MODEL // XA_HEADS
D_FF = 4 * D_MODEL

kernel_name = 'hybrid_retention_ssd_xattn_trunk'

def _rms(x):
    xf = x.astype(jnp.float32)
    return (xf * lax.rsqrt(jnp.mean(xf * xf, axis=-1, keepdims=True) + EPS)).astype(x.dtype)

def _rmsnorm(x, w):
    return _rms(x) * w

def _rope(t, cos, sin):
    t1, t2 = jnp.split(t, 2, axis=-1)
    return jnp.concatenate([t1 * cos - t2 * sin, t1 * sin + t2 * cos], axis=-1)

def _causal_conv(x, w, bias):
    c = x.shape[-1]
    out = lax.conv_general_dilated(
        x, w[:, None, :].astype(x.dtype), window_strides=(1,), padding=[(SSM_CONV - 1, 0)],
        dimension_numbers=('NWC', 'WIO', 'NWC'), feature_group_count=c)
    return out + bias

def _chunk_scan(ret_q, ret_k, ret_v, ssm_x, ssm_dt, ssm_b, ssm_c, ssm_a):
    b, s = ret_q.shape[:2]
    n_chunks = s // CHUNK

    def to_chunks(t):
        t = t.astype(jnp.float32).reshape((b, n_chunks, CHUNK) + t.shape[2:])
        return jnp.moveaxis(t, 1, 0)

    idx = jnp.arange(CHUNK, dtype=jnp.float32)
    log_gamma = jnp.log1p(-(2.0 ** (-5.0 - jnp.arange(RET_HEADS, dtype=jnp.float32))))
    rel = jnp.abs(idx[:, None] - idx[None, :])
    ret_intra = jnp.exp(log_gamma[:, None, None] * rel)
    ret_q_decay = jnp.exp(log_gamma[None, :] * (idx[:, None] + 1.0))[..., None]
    ret_k_decay = jnp.exp(log_gamma[None, :] * (CHUNK - 1.0 - idx[:, None]))[..., None]
    ret_chunk_decay = jnp.exp(log_gamma * CHUNK)
    a = ssm_a.astype(jnp.float32)

    def step(carry, inp):
        s_ret, h_ssm = carry
        q, k, v, xs, dt, bm, cm = inp
        sc = jnp.einsum('blhd,bmhd->bhlm', q, k) * ret_intra
        y_ret = (jnp.einsum('bhlm,bmhe->blhe', sc, v)
                 + jnp.einsum('blhd,bhde->blhe', q * ret_q_decay, s_ret))
        s_ret = (s_ret * ret_chunk_decay[None, :, None, None]
                 + jnp.einsum('blhd,blhe->bhde', k * ret_k_decay, v))
        cum = jnp.cumsum(dt * a, axis=1)
        cum_h = jnp.moveaxis(cum, 1, -1)
        seg = jnp.exp(-jnp.abs(cum_h[..., :, None] - cum_h[..., None, :]))
        cb = jnp.einsum('blgn,bmgn->bglm', cm, bm)
        xdt = xs * dt[..., None]
        y_ssm = (jnp.einsum('bghlm,bmghp->blghp', cb[:, :, None] * seg, xdt)
                 + jnp.einsum('blgn,bghpn->blghp', cm, h_ssm) * jnp.exp(cum)[..., None])
        cum_last = cum[:, -1]
        h_ssm = (h_ssm * jnp.exp(cum_last)[..., None, None]
                 + jnp.einsum('bmgn,bmghp->bghpn', bm,
                              xdt * jnp.exp(cum_last[:, None] - cum)[..., None]))
        return (s_ret, h_ssm), (y_ret, y_ssm)

    init = (jnp.zeros((b, RET_HEADS, RET_QK_DIM, RET_V_DIM), jnp.float32),
            jnp.zeros((b, SSM_GROUPS, SSM_HEADS_PER_GROUP, SSM_HEAD_DIM, SSM_STATE), jnp.float32))
    xs_in = tuple(to_chunks(t) for t in (ret_q, ret_k, ret_v, ssm_x, ssm_dt, ssm_b, ssm_c))
    _, (y_ret, y_ssm) = lax.scan(step, init, xs_in)

    def from_chunks(t):
        t = jnp.moveaxis(t, 0, 1)
        return t.reshape((b, s) + t.shape[3:])

    return from_chunks(y_ret), from_chunks(y_ssm)

def _hybrid_mixer(u, cos, sin, w_in, b_gate, conv_w, conv_b, dt_bias, a_log, d_skip,
                  ssm_norm, w_br_ret, w_br_ssm, w_out):
    b, s, _ = u.shape
    proj = u @ w_in
    offsets = [int(o) for o in np.cumsum(IN_SIZES)[:-1]]
    q, k, v, g, z, xbc, dt, gates = jnp.split(proj, offsets, axis=-1)
    q = _rope(q.reshape(b, s, RET_HEADS, RET_QK_DIM), cos, sin)
    k = _rope(k.reshape(b, s, RET_HEADS, RET_QK_DIM), cos, sin) * (RET_QK_DIM ** -0.5)
    v = v.reshape(b, s, RET_HEADS, RET_V_DIM)
    xbc = jax.nn.silu(_causal_conv(xbc, conv_w, conv_b))
    xs, bm, cm = jnp.split(xbc, [SSM_INNER, SSM_INNER + SSM_BC], axis=-1)
    xs = xs.reshape(b, s, SSM_GROUPS, SSM_HEADS_PER_GROUP, SSM_HEAD_DIM)
    bm = bm.reshape(b, s, SSM_GROUPS, SSM_STATE)
    cm = cm.reshape(b, s, SSM_GROUPS, SSM_STATE)
    dt = jax.nn.softplus(dt.astype(jnp.float32) + dt_bias.astype(jnp.float32))
    dt = dt.reshape(b, s, SSM_GROUPS, SSM_HEADS_PER_GROUP)
    ssm_a = -jnp.exp(a_log.astype(jnp.float32)).reshape(SSM_GROUPS, SSM_HEADS_PER_GROUP)
    y_ret, y_ssm = _chunk_scan(q, k, v, xs, dt, bm, cm, ssm_a)
    y_ret = _rms(y_ret.astype(u.dtype)).reshape(b, s, RET_V) * jax.nn.silu(g)
    y_ssm = y_ssm.astype(u.dtype) + xs * d_skip.reshape(SSM_GROUPS, SSM_HEADS_PER_GROUP, 1)
    y_ssm = y_ssm.reshape(b, s, SSM_INNER) * jax.nn.silu(z)
    y_ssm = _rms(y_ssm.reshape(b, s, SSM_GROUPS, SSM_INNER // SSM_GROUPS)).reshape(b, s, SSM_INNER) * ssm_norm
    gate_ret, gate_ssm = jnp.split(jax.nn.sigmoid(gates + b_gate), N_BRANCH, axis=-1)
    merged = gate_ret * (y_ret @ w_br_ret) + gate_ssm * (y_ssm @ w_br_ssm)
    return merged @ w_out

def _cross_attention(h, mem_n, wq, wkv, wo):
    b, s, _ = h.shape
    m = mem_n.shape[1]
    q = (h @ wq).reshape(b, s, XA_HEADS, XA_HEAD_DIM)
    k, v = jnp.split(mem_n @ wkv, 2, axis=-1)
    k = k.reshape(b, m, XA_HEADS, XA_HEAD_DIM)
    v = v.reshape(b, m, XA_HEADS, XA_HEAD_DIM)
    scores = jnp.einsum('bshd,bmhd->bhsm', q, k).astype(jnp.float32) * (XA_HEAD_DIM ** -0.5)
    p = jax.nn.softmax(scores, axis=-1).astype(v.dtype)
    o = jnp.einsum('bhsm,bmhd->bshd', p, v).reshape(b, s, D_MODEL)
    return o @ wo

def _sq_relu_mlp(h, w1, w2):
    return jnp.square(jax.nn.relu(h @ w1)) @ w2

def setup_inputs(seed: int = 0) -> dict:
    key = jax.random.key(seed)
    ks = jax.random.split(key, 32)

    def nrm(k, shape, scale):
        return jax.random.normal(k, shape, jnp.float32) * scale

    def gain(k, shape):
        return 1.0 + nrm(k, shape, 0.02)

    L = DEPTH
    x = nrm(ks[0], (BATCH, SEQ, D_MODEL), 1.0)
    mem = nrm(ks[1], (BATCH, MEM_LEN, D_MODEL), 1.0)
    offset = jax.random.randint(ks[2], (BATCH, 1), 0, 8192, dtype=jnp.int32)
    positions = offset + jnp.arange(SEQ, dtype=jnp.int32)[None, :]
    dt0 = jnp.exp(jax.random.uniform(ks[3], (L, SSM_HEADS), jnp.float32)
                  * (jnp.log(0.1) - jnp.log(0.001)) + jnp.log(0.001))
    dt_bias = dt0 + jnp.log(-jnp.expm1(-dt0))
    a_log = jnp.log(jax.random.uniform(ks[4], (L, SSM_HEADS), jnp.float32, 1.0, 16.0))
    return {
        'x': x,
        'mem': mem,
        'positions': positions,
        'norm_mix': gain(ks[5], (L, D_MODEL)),
        'w_in': nrm(ks[6], (L, D_MODEL, IN_DIM), D_MODEL ** -0.5),
        'b_gate': nrm(ks[7], (L, N_BRANCH * D_MODEL), 0.01),
        'conv_w': nrm(ks[8], (L, SSM_CONV, SSM_CONV_DIM), SSM_CONV ** -0.5),
        'conv_b': nrm(ks[9], (L, SSM_CONV_DIM), 0.01),
        'dt_bias': dt_bias,
        'a_log': a_log,
        'd_skip': gain(ks[10], (L, SSM_HEADS)),
        'ssm_norm': gain(ks[11], (L, SSM_INNER)),
        'w_br_ret': nrm(ks[12], (L, RET_V, D_MODEL), RET_V ** -0.5),
        'w_br_ssm': nrm(ks[13], (L, SSM_INNER, D_MODEL), SSM_INNER ** -0.5),
        'w_out': nrm(ks[14], (L, D_MODEL, D_MODEL), D_MODEL ** -0.5),
        'norm_xa': gain(ks[15], (L, D_MODEL)),
        'norm_mem': gain(ks[16], (L, D_MODEL)),
        'xa_wq': nrm(ks[17], (L, D_MODEL, D_MODEL), D_MODEL ** -0.5),
        'xa_wkv': nrm(ks[18], (L, D_MODEL, 2 * D_MODEL), D_MODEL ** -0.5),
        'xa_wo': nrm(ks[19], (L, D_MODEL, D_MODEL), D_MODEL ** -0.5),
        'norm_mlp': gain(ks[20], (L, D_MODEL)),
        'mlp_w1': nrm(ks[21], (L, D_MODEL, D_FF), D_MODEL ** -0.5),
        'mlp_w2': nrm(ks[22], (L, D_FF, D_MODEL), D_FF ** -0.5),
        'norm_final': gain(ks[23], (D_MODEL,)),
    }

def reference(x, mem, positions, norm_mix, w_in, b_gate, conv_w, conv_b, dt_bias, a_log,
              d_skip, ssm_norm, w_br_ret, w_br_ssm, w_out, norm_xa, norm_mem, xa_wq, xa_wkv,
              xa_wo, norm_mlp, mlp_w1, mlp_w2, norm_final):
    inv_freq = ROPE_THETA ** (-jnp.arange(0, RET_QK_DIM, 2, dtype=jnp.float32) / RET_QK_DIM)
    ang = positions.astype(jnp.float32)[..., None] * inv_freq
    cos = jnp.cos(ang)[:, :, None, :].astype(x.dtype)
    sin = jnp.sin(ang)[:, :, None, :].astype(x.dtype)
    for l in range(DEPTH):
        x = x + _hybrid_mixer(_rmsnorm(x, norm_mix[l]), cos, sin, w_in[l], b_gate[l],
                              conv_w[l], conv_b[l], dt_bias[l], a_log[l], d_skip[l],
                              ssm_norm[l], w_br_ret[l], w_br_ssm[l], w_out[l])
        x = x + _cross_attention(_rmsnorm(x, norm_xa[l]), _rmsnorm(mem, norm_mem[l]),
                                 xa_wq[l], xa_wkv[l], xa_wo[l])
        x = x + _sq_relu_mlp(_rmsnorm(x, norm_mlp[l]), mlp_w1[l], mlp_w2[l])
    return _rmsnorm(x, norm_final)


_drawn_inputs = setup_inputs


def setup_inputs(seed=0):
    import zlib

    import numpy as np

    out = dict(_drawn_inputs(seed))
    spreads = {}
    factors = {'b_gate': 8.0,
     'conv_b': 5.482,
     'd_skip': 6.969,
     'ssm_norm': 4.434,
     'norm_xa': 8.0,
     'norm_mem': 8.0,
     'norm_final': 8.386,
     'norm_mlp': 3.348}
    for name, (base, spread) in spreads.items():
        noise = np.random.default_rng([zlib.crc32(name.encode()), seed]).standard_normal(out[name].shape)
        drawn = base * np.exp(spread * noise) if base else spread * noise
        out[name] = jnp.asarray(drawn.astype(out[name].dtype))
    for name, factor in factors.items():
        out[name] = (out[name] * factor).astype(out[name].dtype)
    return out
```

```python
from contextlib import ExitStack, contextmanager

import numpy as np

import concourse.bass as bass
from concourse import mybir

F32 = mybir.dt.float32
F32R = mybir.dt.float32r
I32 = mybir.dt.int32
ALU = mybir.AluOpType
ACT = mybir.ActivationFunctionType
AX = mybir.AxisListType.X

P = 128
D = 1024
S = 512
KT = D // P
DEPTH = 2
MEM = 256
CHUNK = 64
NBLK = S // P
EPS = 1e-6
RET_HEADS = 4
RET_QK = 512
RET_V = 1024
SSM_INNER = 2048
SSM_HEADS = 32
GROUPS = 8
HPG = SSM_HEADS // GROUPS
HD = SSM_INNER // SSM_HEADS
BC = 1024
D_FF = 4096
FFQ = D_FF // D

O_Q = 0
O_K = O_Q + RET_QK
O_V = O_K + RET_QK
O_G = O_V + RET_V
O_Z = O_G + RET_V
O_XS = O_Z + SSM_INNER
O_B = O_XS + SSM_INNER
O_C = O_B + BC
O_DT = O_C + BC
O_GATE = O_DT + SSM_HEADS

UNITS = 2 + GROUPS * 6 + KT * 3 + RET_HEADS * 6 + KT * 2 + KT + 4 * 6 + KT + FFQ * 2 * KT
AHEAD = 2

L_MIX, L_XA, L_MEM, L_MLP, L_GATE, L_ALOG, L_DTB = 0, 8, 16, 24, 32, 48, 80
LPN = 81
G_TAP, G_BIAS, G_SKIP, G_NORM = 0, 16, 20, 22
GPN = 24

TWO_PI = 2 * np.pi
C1 = 6.28125
C2 = float(np.float32(np.round((TWO_PI - C1) * 2**21) / 2**21))
C3 = float(np.float32(TWO_PI - C1 - C2))
MAGIC = 1.5 * 2.0**23


class Counts:

    def __init__(self, engine, per, always):
        self.engine, self.per, self.always = engine, per, always
        self.n, self.active, self.loops = {}, [], 0

    def now(self, sem):
        value = self.n.get(sem.name, 0)
        for index, counts in self.active:
            if counts.get(sem.name, 0):
                value = index * counts[sem.name] + value
        return value

    def next(self, sem, by=1):
        self.n[sem.name] = self.n.get(sem.name, 0) + by
        return self.now(sem)

    @contextmanager
    def loop(self, eng, times):
        self.loops += 1
        label = (self.engine, self.loops)
        before = dict(self.n)
        if self.active:
            eng.sem_inc(self.always, 1)
        with eng.Fori(0, times) as index:
            self.active.append((index, self.per.get(label, {})))
            yield index
            self.active.pop()
        once = {s: v - before.get(s, 0) for s, v in self.n.items()}
        self.per[label] = once
        self.n = {s: before.get(s, 0) + times * v for s, v in once.items()}


def program(nc, a, per):
    with ExitStack() as ctx:
        def sb(name, shape, dt=F32, stack=ctx):
            return stack.enter_context(nc.sbuf_tensor(name, shape, dt))

        def sem(name):
            return ctx.enter_context(nc.semaphore(name))

        x = sb("x", [P, KT, S])
        u_hi, u_lo = sb("u_hi", [P, KT, S], F32R), sb("u_lo", [P, KT, S], F32R)
        raw = sb("raw", [P, 2, KT, P])
        w_hi, w_lo = sb("w_hi", [P, 2, KT, P], F32R), sb("w_lo", [P, 2, KT, P], F32R)
        mem = sb("mem_t", [P, KT, MEM])
        cos_sb, sin_sb = sb("cos_sb", [P, S]), sb("sin_sb", [P, S])
        decay = sb("decay", [P, RET_HEADS, S])
        ident, upto, mask = sb("ident", [P, P]), sb("upto", [P, P]), sb("mask", [P, P])
        ones = sb("ones", [P, P])
        eps_t = sb("eps_t", [P, 1])
        lp = sb("lp", [P, LPN])
        fin_w = sb("fin_w", [P, KT])
        half_gate = sb("half_gate", [P, 2 * KT])
        a_pos = sb("a_pos", [P, SSM_HEADS])
        gp = sb("gp", [P, GPN])
        gp_half = sb("gp_half", [P, G_SKIP])
        freq = sb("freq", [P, 4])
        t2 = sb("t2", [P, 2, S])
        e2 = sb("e2", [P, 2, S])
        rstd, acc_sq = sb("rstd", [P, S]), sb("acc_sq", [P, S])
        tok = sb("tok", [P, 4, NBLK, SSM_HEADS])
        small = sb("small", [P, 8])

        with ExitStack() as ssm:
            b_t, c_t = sb("b_t", [P, S], F32, ssm), sb("c_t", [P, S], F32, ssm)
            xs_t, z_t = sb("xs_t", [P, 2, S], F32, ssm), sb("z_t", [P, 2, S], F32, ssm)
            b_tok = sb("b_tok", [P, P], F32, ssm)
            xdt, xdt_dec = sb("xdt", [P, HPG, HD], F32, ssm), sb("xdt_dec", [P, HPG, HD], F32, ssm)
            row = sb("row", [P, 2, HPG, P], F32, ssm)
            seg, c_dec = sb("seg", [P, HPG, P], F32, ssm), sb("c_dec", [P, HPG, P], F32, ssm)
            cb_m = sb("cb_m", [P, P], F32, ssm)
            state = sb("state", [P, HPG, HD], F32, ssm)
            dt_w = sb("dt_w", [SSM_HEADS, 5, S], F32, ssm)
            ys_hi, ys_lo = sb("ys_hi", [P, 2 * KT, S], F32R, ssm), sb("ys_lo", [P, 2 * KT, S], F32R, ssm)
        merge = sb("merge", [P, KT, S])
        mem_hi, mem_lo = sb("mem_hi", [P, KT, MEM], F32R), sb("mem_lo", [P, KT, MEM], F32R)
        with ExitStack() as mix:
            yr_hi, yr_lo = sb("yr_hi", [P, KT, S], F32R, mix), sb("yr_lo", [P, KT, S], F32R, mix)
            with ExitStack() as ret:
                q_t, k_t = sb("q_t", [P, S], F32, ret), sb("k_t", [P, S], F32, ret)
                v_t, g_t = sb("v_t", [P, 2, S], F32, ret), sb("g_t", [P, 2, S], F32, ret)
                v_tok = sb("v_tok", [P, NBLK, 2 * P], F32, ret)
                score = sb("score", [P, NBLK, S], F32, ret)
            m_hi, m_lo = sb("m_hi", [P, KT, S], F32R, mix), sb("m_lo", [P, KT, S], F32R, mix)
        with ExitStack() as xa:
            o_hi, o_lo = sb("o_hi", [P, KT, S], F32R, xa), sb("o_lo", [P, KT, S], F32R, xa)
            xk, xv = sb("xk", [P, 2, MEM], F32, xa), sb("xv", [P, 2, MEM], F32, xa)
            xv_tok = sb("xv_tok", [P, 2, 2 * P], F32, xa)
            xq = sb("xq", [P, 2, S], F32, xa)
            prob = sb("prob", [P, 2, MEM], F32, xa)
            prob_t = sb("prob_t", [P, 2, S], F32, xa)
        h_hi, h_lo = sb("h_hi", [P, KT, S], F32R), sb("h_lo", [P, KT, S], F32R)

        acc = [ctx.enter_context(nc.psum_tensor(f"acc{i}", [P, S], F32)) for i in range(2)]
        tp = ctx.enter_context(nc.psum_tensor("tp", [P, S], F32))
        pr = [ctx.enter_context(nc.psum_tensor(f"pr{i}", [P, S], F32)) for i in range(2)]
        yp = [ctx.enter_context(nc.psum_tensor(f"yp{i}", [P, S], F32)) for i in range(2)]
        ss = ctx.enter_context(nc.psum_tensor("ss", [P, S], F32))
        cum_dram = nc.dram_tensor("cum_scratch", [GROUPS, HPG, S], F32, kind="Internal").ap()

        passed = sem("passed")
        const_in = sem("const_in")
        x_in = sem("x_in")
        lp_in, gp_in = sem("lp_in"), sem("gp_in")
        raw_in = [sem("raw_in0"), sem("raw_in1")]
        hi_ready, lo_ready, unit_done = sem("hi_ready"), sem("lo_ready"), sem("unit_done")
        acc_free = [sem("acc_free0"), sem("acc_free1")]
        dve_step, act_step, pool_step = sem("dve_step"), sem("act_step"), sem("pool_step")
        x_tile = sem("x_tile")
        sq_ready, sum_ready = sem("sq_ready"), sem("sum_ready")
        ss_ready, ss_free, rstd_ready = sem("ss_ready"), sem("ss_free"), sem("rstd_ready")
        tmp_ready, hi_tile, pair_ready = sem("tmp_ready"), sem("hi_tile"), sem("pair_ready")
        consts_ready = sem("consts_ready")
        angle_ready, trig_ready = sem("angle_ready"), sem("trig_ready")
        lp_ready, lp_free = sem("lp_ready"), sem("lp_free")
        gp_free = sem("gp_free")
        dt_abs, dt_exp, dt_done = sem("dt_abs"), sem("dt_exp"), sem("dt_done")
        dt_turned, dta_ready, cum_ready = sem("dt_turned"), sem("dta_ready"), sem("cum_ready")
        tok_part, tok_ready, cum_rows, cum_out = sem("tok_part"), sem("tok_ready"), sem("cum_rows"), sem("cum_out")
        row_in, row_free = [sem("row_in0"), sem("row_in1")], sem("row_free")
        lin_ready, act_ready, silu_ready = sem("lin_ready"), sem("act_ready"), sem("silu_ready")
        turned, tp_free = sem("turned"), sem("tp_free")
        cb_ready, cb_free = sem("cb_ready"), sem("cb_free")
        diff_ready, seg_ready, cdec_ready = sem("diff_ready"), sem("seg_ready"), sem("cdec_ready")
        blk_ready, y_blk = sem("blk_ready"), sem("y_blk")
        dec_ready, st_sum, st_ready = sem("dec_ready"), sem("st_sum"), sem("st_ready")
        xa_ready = sem("xa_ready")
        y_free, out_ready = sem("y_free"), sem("out_ready")
        e_free = sem("e_free")
        gate_ready, gated = sem("gate_ready"), sem("gated")
        v_ready, sc_ready, sc_free, sc_done = sem("v_ready"), sem("sc_ready"), sem("sc_free"), sem("sc_done")
        vtok_ready, head_y = sem("vtok_ready"), sem("head_y")
        max_ready, prob_raw, prob_ready = sem("max_ready"), sem("prob_raw"), sem("prob_ready")
        probt_ready, evac_hi = sem("probt_ready"), sem("evac_hi")
        relu_ready = sem("relu_ready")
        final_ready, final_out, out_done = sem("final_ready"), sem("final_out"), sem("out_done")

        block = ctx.enter_context(nc.Block())

        @block.sync
        def _(sp):
            sp.dma_start(raw[:, 0], a["stream"][0]).then_inc(raw_in[0], 16)
            sp.dma_start(x[:], a["x"]).then_inc(x_in, 16)
            sp.dma_start(mem[:], a["mem"]).then_inc(x_in, 16)
            sp.dma_start(raw[:, 1], a["stream"][1]).then_inc(raw_in[1], 16)
            with sp.Fori(1, (DEPTH * UNITS + AHEAD) // 2) as i:
                for s in range(2):
                    sp.wait_ge(lo_ready, i * 2 + (s - 1))
                    sp.dma_start(raw[:, s], a["stream"][bass.ds(i * 2 + s, 1)].rearrange("a p k c -> p (a k) c")).then_inc(raw_in[s], 16)

        @block.gpsimd
        def _(pool):
            c = Counts("pool", per, passed)
            pool.memset(ones[:], 1.0).then_inc(pool_step, 1)
            pool.memset(eps_t[:], EPS).then_inc(pool_step, 1)
            pool.wait_ge(pool_step, c.next(pool_step, 2))
            pool.dma_start(freq[:], a["freq"]).then_inc(const_in, 16)
            pool.dma_start(e2[:, 0].bitcast(I32), a["pos"].partition_broadcast(P)).then_inc(const_in, 16)
            pool.dma_start(ident[:], a["ident"]).then_inc(const_in, 16)
            pool.dma_start(upto[:], a["upto"]).then_inc(const_in, 16)
            pool.dma_start(mask[:], a["mask"]).then_inc(const_in, 16)
            pool.dma_start(fin_w[:], a["fin_w"]).then_inc(const_in, 16)
            pool.dma_start(decay[:], a["decay"]).then_inc(const_in, 16)
            pool.wait_ge(const_in, 7 * 16)
            pool.sem_inc(consts_ready, 1)
            with c.loop(pool, DEPTH) as l:
                pool.wait_ge(lp_free, c.next(lp_free))
                pool.dma_start(lp[:], a["lp"][bass.ds(l, 1)].rearrange("a p n -> p (a n)")).then_inc(lp_in, 16)
                with c.loop(pool, GROUPS) as g:
                    pool.wait_ge(gp_free, c.next(gp_free))
                    pool.dma_start(gp[:], a["gp"][bass.ds(l * GROUPS + g, 1)].rearrange("a p n -> p (a n)")).then_inc(gp_in, 16)
                    for b in range(NBLK):
                        if b == 0:
                            pool.wait_ge(cum_out, l * 16 + 16)
                        pool.wait_ge(row_free, c.next(row_free))
                        pool.dma_start(row[:, b % 2], cum_dram[bass.ds(g, 1), :, b * P:(b + 1) * P]
                                       .rearrange("a h s -> (a h) s").partition_broadcast(P)).then_inc(row_in[b % 2], 16)

        @block.tensor
        def _(pe):
            c = Counts("pe", per, passed)

            def unit(s, bank, hi, lo, first=True, last=True, width=S, tiles=None):
                pe.wait_ge(hi_ready, c.next(hi_ready))
                if first:
                    pe.wait_ge(acc_free[bank], c.next(acc_free[bank]))
                out = acc[bank][:, 0:width]
                for k in range(KT):
                    if tiles is not None:
                        pe.wait_ge(pair_ready, tiles + (k + 1))
                    pe.matmul(out, w_hi[:, s, k], hi[:, k, 0:width], start=first and k == 0, stop=False)
                    pe.matmul(out, w_hi[:, s, k], lo[:, k, 0:width], start=False, stop=False)
                pe.wait_ge(lo_ready, c.next(lo_ready))
                for k in range(KT):
                    mm = pe.matmul(out, w_lo[:, s, k], hi[:, k, 0:width], start=False, stop=last and k == KT - 1)
                mm.then_inc(unit_done, 1)

            def sum_of_squares():
                pe.wait_ge(sum_ready, c.next(sum_ready))
                pe.wait_ge(ss_free, c.next(ss_free))
                pe.matmul(ss[:], ones[:], acc_sq[:], start=True, stop=True).then_inc(ss_ready, 1)

            def norm():
                sum_of_squares()
                base = c.now(pair_ready)
                c.next(pair_ready, KT)
                return base

            def dt_rows():
                pe.wait_ge(dt_done, c.next(dt_done))
                pe.wait_ge(tp_free, c.next(tp_free))
                pe.sem_inc(passed, 1)
                for b in range(NBLK):
                    t = pe.transpose(tp[:, b * SSM_HEADS:(b + 1) * SSM_HEADS], dt_w[:, 0, b * P:(b + 1) * P],
                                     ident[0:SSM_HEADS, 0:SSM_HEADS])
                t.then_inc(dt_turned, 1)
                pe.wait_ge(dta_ready, c.next(dta_ready))
                dta = t2[:, 0, 0:P]
                pe.matmul(pr[0][:, 0:P], upto[:], dta, start=True, stop=True)
                pe.matmul(pr[0][:, P:2 * P], ones[:], dta, start=True, stop=True)
                for b in range(NBLK):
                    mm = pe.matmul(pr[1][0:SSM_HEADS, b * P:(b + 1) * P], dta[:, b * SSM_HEADS:(b + 1) * SSM_HEADS], upto[:],
                                   start=True, stop=True)
                mm.then_inc(cum_ready, 1)

            def scan_group():
                pe.wait_ge(silu_ready, c.next(silu_ready, 6))
                for b in range(NBLK):
                    at = slice(b * P, (b + 1) * P)
                    pe.wait_ge(tp_free, c.next(tp_free))
                    pe.transpose(tp[:, 0:P], b_t[:, at], ident[:])
                    pe.transpose(tp[:, P:2 * P], xs_t[:, 0, at], ident[:])
                    pe.transpose(tp[:, 2 * P:3 * P], xs_t[:, 1, at], ident[:]).then_inc(turned, 1)
                    pe.wait_ge(cb_free, c.next(cb_free))
                    pe.matmul(pr[0][:, 0:P], b_t[:, at], c_t[:, at], start=True, stop=True).then_inc(cb_ready, 1)
                    pe.wait_ge(blk_ready, c.next(blk_ready))
                    if b == 0:
                        pe.wait_ge(y_free, c.next(y_free))
                    else:
                        pe.wait_ge(cdec_ready, c.next(cdec_ready))
                        pe.wait_ge(st_ready, c.next(st_ready))
                    for h in range(HPG):
                        out = yp[h // 2][h % 2 * HD:(h % 2 + 1) * HD, at]
                        mm = pe.matmul(out, xdt[:, h], seg[:, h], start=True, stop=b == 0)
                        if b:
                            mm = pe.matmul(out, state[:, h], c_dec[:, h], start=False, stop=True)
                    mm.then_inc(y_blk, 1)
                    if b < NBLK - 1:
                        pe.wait_ge(dec_ready, c.next(dec_ready))
                        pe.matmul(pr[1][:, 0:HPG * HD], b_tok[:], xdt_dec[:].rearrange("p h d -> p (h d)"),
                                  start=True, stop=True).then_inc(st_sum, 1)
                sum_of_squares()

            def retention_head():
                c.next(silu_ready, 2)
                for t in range(2):
                    pe.wait_ge(v_ready, c.next(v_ready))
                    pe.wait_ge(tp_free, c.next(tp_free))
                    for b in range(NBLK):
                        mm = pe.transpose(tp[:, b * P:(b + 1) * P], v_t[:, t, b * P:(b + 1) * P], ident[:])
                    mm.then_inc(turned, 1)
                for i in range(NBLK):
                    pe.wait_ge(sc_free, c.next(sc_free))
                    pe.matmul(pr[i % 2][:, 0:S - i * P], k_t[:, i * P:(i + 1) * P], q_t[:, i * P:S],
                              start=True, stop=True).then_inc(sc_ready, 1)
                pe.wait_ge(vtok_ready, c.next(vtok_ready, 2))
                pe.wait_ge(y_free, c.next(y_free))
                for i in range(NBLK):
                    pe.wait_ge(sc_done, c.next(sc_done))
                    for t in range(2):
                        mm = pe.matmul(yp[t][:, i * P:S], v_tok[:, i, t * P:(t + 1) * P], score[:, i, 0:S - i * P],
                                       start=i == 0, stop=i == NBLK - 1)
                mm.then_inc(head_y, 1)
                sum_of_squares()

            def attention_head():
                for t in range(2):
                    pe.wait_ge(v_ready, c.next(v_ready))
                    pe.wait_ge(tp_free, c.next(tp_free))
                    for m in range(2):
                        mm = pe.transpose(tp[:, m * P:(m + 1) * P], xv[:, t, m * P:(m + 1) * P], ident[:])
                    mm.then_inc(turned, 1)
                pe.wait_ge(xa_ready, c.next(xa_ready, 4))

                def turn():
                    pe.wait_ge(prob_ready, c.next(prob_ready))
                    pe.wait_ge(tp_free, c.next(tp_free))
                    for m in range(2):
                        mm = pe.transpose(tp[:, m * P:(m + 1) * P], prob[:, (i - 1) % 2, m * P:(m + 1) * P], ident[:])
                    mm.then_inc(turned, 1)

                for i in range(NBLK + 1):
                    if i < NBLK:
                        pe.wait_ge(sc_free, c.next(sc_free))
                        for k in range(2):
                            mm = pe.matmul(pr[i % 2][:, 0:MEM], xq[:, k, i * P:(i + 1) * P], xk[:, k],
                                           start=k == 0, stop=k == 1)
                        mm.then_inc(sc_ready, 1)
                    if i:
                        turn()
                pe.wait_ge(probt_ready, c.next(probt_ready, NBLK))
                pe.wait_ge(vtok_ready, c.next(vtok_ready, 2))
                pe.wait_ge(y_free, c.next(y_free))
                for t in range(2):
                    for m in range(2):
                        mm = pe.matmul(yp[t][:], xv_tok[:, m, t * P:(t + 1) * P], prob_t[:, m], start=m == 0, stop=m == 1)
                mm.then_inc(head_y, 1)

            def plain_units(hi, lo, tiles):
                with c.loop(pe, KT // 2):
                    unit(0, 0, hi, lo, tiles=tiles)
                    unit(1, 1, hi, lo)

            pe.wait_ge(consts_ready, 1)
            c.next(silu_ready, 2)
            with c.loop(pe, DEPTH):
                tiles = norm()
                unit(0, 0, u_hi, u_lo, tiles=tiles)
                pe.wait_ge(hi_ready, c.next(hi_ready))
                pe.wait_ge(lo_ready, c.next(lo_ready))
                pe.wait_ge(acc_free[1], c.next(acc_free[1]))
                pe.matmul(acc[1][:, 0:P], w_hi[:, 1, 0], w_lo[:, 1, 0], start=True, stop=True).then_inc(unit_done, 1)
                dt_rows()
                with c.loop(pe, GROUPS):
                    for j in range(6):
                        unit(j % 2, j % 2, u_hi, u_lo)
                    scan_group()
                base = c.now(pair_ready)
                c.next(pair_ready, 2 * KT)
                with c.loop(pe, KT // 2):
                    for j in range(2):
                        unit(j, 0, u_hi, u_lo)
                        unit(1 - j, 1, ys_hi[:, 0:KT], ys_lo[:, 0:KT], last=False, tiles=base)
                        unit(j, 1, ys_hi[:, KT:2 * KT], ys_lo[:, KT:2 * KT], first=False, tiles=base + KT)
                with c.loop(pe, RET_HEADS):
                    for j in range(6):
                        unit(j % 2, j % 2, u_hi, u_lo)
                    retention_head()
                base = c.now(pair_ready)
                c.next(pair_ready, KT)
                with c.loop(pe, KT):
                    unit(0, 0, u_hi, u_lo)
                    unit(1, 1, yr_hi, yr_lo, tiles=base)
                base = c.now(pair_ready)
                c.next(pair_ready, KT)
                plain_units(m_hi, m_lo, base)
                mem_tiles = norm()
                tiles = norm()
                with c.loop(pe, 4):
                    for j in range(4):
                        unit(j % 2, j % 2, mem_hi, mem_lo, width=MEM, tiles=mem_tiles)
                    for j in range(2):
                        unit(j, j, u_hi, u_lo, tiles=tiles)
                    attention_head()
                base = c.now(pair_ready)
                c.next(pair_ready, KT)
                plain_units(o_hi, o_lo, base)
                tiles = norm()
                with c.loop(pe, FFQ):
                    plain_units(u_hi, u_lo, tiles)
                    base = c.now(pair_ready)
                    c.next(pair_ready, KT)
                    plain_units(h_hi, h_lo, base)
            sum_of_squares()

        @block.scalar
        def _(act):
            c = Counts("act", per, passed)

            def then(ins, signal=act_step):
                ins.then_inc(signal, 1)
                act.wait_ge(signal, c.next(signal))

            def split(s):
                act.wait_ge(raw_in[s], c.next(raw_in[s], 16))
                then(act.activation(w_hi[:, s], raw[:, s], ACT.Copy), hi_ready)

            def step(s, before=None, after=None):
                act.wait_ge(unit_done, c.next(unit_done))
                if before:
                    before()
                split(s)
                if after:
                    after()

            def rms(scale):
                act.wait_ge(ss_ready, c.next(ss_ready))
                then(act.activation(acc_sq[:], ss[:], ACT.Ln, bias=eps_t[:], scale=scale), ss_free)
                then(act.activation(rstd[:], acc_sq[:], ACT.Exp, scale=-0.5), rstd_ready)

            def norm(src, width, ready):
                for k in range(KT):
                    if ready is not None:
                        act.wait_ge(ready, c.next(ready))
                    act.wait_ge(sum_ready, c.next(sum_ready)) if 0 else None
                    then(act.activation(sq(k)[:, 0:width], src[:, k], ACT.Square), sq_ready)

            def sq(k):
                return t2[:, k % 2]

            def high_parts(n, dst, width=S):
                for k in range(n):
                    act.wait_ge(tmp_ready, c.next(tmp_ready))
                    then(act.activation(dst(k), t2[:, k % 2, 0:width], ACT.Copy), hi_tile)

            def full_norm(src, width, ready, dst):
                for k in range(KT):
                    if ready is not None:
                        act.wait_ge(ready, c.next(ready))
                    act.wait_ge(gated, c.next(gated))
                    then(act.activation(t2[:, k % 2, 0:width], src[:, k], ACT.Square), sq_ready)
                rms(1.0 / D)
                if dst is not None:
                    high_parts(KT, lambda k: dst[:, k, 0:width], width)

            c.next(ss_free)
            act.wait_ge(pool_step, 2)
            act.wait_ge(angle_ready, 1)
            then(act.activation(t2[:, 1], t2[:, 0], ACT.Sin))
            then(act.activation(sin_sb[0:64], t2[0:64, 1], ACT.Copy))
            then(act.activation(sin_sb[64:128], t2[0:64, 1], ACT.Copy, scale=-1.0))
            then(act.activation(cos_sb[0:64], t2[64:128, 1], ACT.Copy))
            then(act.activation(cos_sb[64:128], t2[64:128, 1], ACT.Copy), trig_ready)
            for s in range(2):
                split(s)

            def conv_unit(s, j, taps):
                def before():
                    act.wait_ge(silu_ready, c.next(silu_ready))
                    then(act.activation(t2[:, s], acc[s][:], ACT.Identity, bias=gp_half[:, G_BIAS + j:G_BIAS + j + 1],
                                        scale=gp_half[:, G_TAP + 4 * j + 3:G_TAP + 4 * j + 4]), lin_ready)

                def after():
                    act.wait_ge(act_ready, c.next(act_ready))
                    then(act.activation(e2[:, s], t2[:, s], ACT.Tanh), gate_ready)
                step(s, before, after)

            def silu_unit(s):
                def before():
                    act.wait_ge(silu_ready, c.next(silu_ready))
                    then(act.activation(e2[:, s], acc[s][:], ACT.Tanh, scale=0.5), gate_ready)
                step(s, before)

            with c.loop(act, DEPTH) as l:
                full_norm(x, S, x_tile, u_hi)
                act.wait_ge(lp_ready, c.next(lp_ready))
                then(act.activation(a_pos[:], lp[:, L_ALOG:L_ALOG + SSM_HEADS], ACT.Exp), tok_part)

                def dt_before():
                    act.wait_ge(dt_abs, c.next(dt_abs))
                    then(act.activation(dt_w[:, 1], dt_w[:, 0], ACT.Abs))
                    then(act.activation(dt_w[:, 2], dt_w[:, 1], ACT.Exp, scale=-1.0), dt_exp)
                step(0, None, dt_before)
                step(1)
                act.wait_ge(cum_ready, c.next(cum_ready))
                then(act.activation(dt_w[:, 4], pr[1][0:SSM_HEADS, :], ACT.Copy), cum_rows)
                act.dma_start(cum_dram.rearrange("g h s -> (g h) s"), dt_w[:, 4]).then_inc(cum_out, 16)
                act.wait_ge(cum_out, c.next(cum_out, 16))
                act.wait_ge(tok_ready, c.next(tok_ready))
                then(act.activation(tok[:, 2], tok[:, 2], ACT.Exp))
                then(act.activation(tok[:, 3], tok[:, 3], ACT.Exp), tok_part)

                with c.loop(act, GROUPS) as g:
                    for j in range(4):
                        if j == 0:
                            act.wait_ge(gp_free, c.next(gp_free)) if 0 else None
                            act.wait_ge(lp_ready, c.next(lp_ready))
                        conv_unit(j % 2, j, None)
                    for j in range(2):
                        silu_unit(j)
                    for b in range(NBLK):
                        act.wait_ge(row_in[b % 2], c.next(row_in[b % 2], 16))
                        if b:
                            act.wait_ge(y_blk, c.now(y_blk))
                            then(act.activation(c_dec[:], row[:, b % 2], ACT.Exp))
                            act.wait_ge(diff_ready, c.next(diff_ready))
                            then(act.activation(seg[:], seg[:], ACT.Abs))
                        else:
                            act.wait_ge(diff_ready, c.next(diff_ready))
                            then(act.activation(seg[:], seg[:], ACT.Abs))
                        then(act.activation(seg[:], seg[:], ACT.Exp, scale=-1.0), seg_ready)
                        act.wait_ge(y_blk, c.next(y_blk))
                    act.wait_ge(out_ready, c.next(out_ready))
                    for t in range(2):
                        then(act.activation(z_t[:, t], xs_t[:, t], ACT.Square), sq_ready)
                    rms(1.0 / (SSM_INNER // GROUPS))
                    high_parts(2, lambda t: ys_hi[:, bass.ds(g * 2 + t, 1)].rearrange("p a s -> p (a s)"))

                def gate_unit(s, n, col):
                    def before():
                        act.wait_ge(e_free, c.next(e_free))
                        then(act.activation(e2[:, n], acc[0][:], ACT.Tanh, bias=half_gate[:, bass.ds(col, 1)], scale=0.5), gate_ready)
                    step(s, before)

                with c.loop(act, KT // 2) as i:
                    for j in range(2):
                        gate_unit(j, j, i * 2 + (j + KT))
                        step(1 - j)
                        step(j)
                with c.loop(act, RET_HEADS) as h:
                    step(0)
                    step(1)
                    for t in range(2):
                        def before():
                            then(act.activation(v_t[:, t], acc[t][:], ACT.Copy), v_ready)
                        step(t, before)
                    for t in range(2):
                        silu_unit(t)
                    act.wait_ge(head_y, c.next(head_y))
                    for t in range(2):
                        then(act.activation(v_t[:, t], yp[t][:], ACT.Copy))
                        then(act.activation(t2[:, t], v_t[:, t], ACT.Square), sq_ready)
                    rms(1.0 / (RET_V // RET_HEADS))
                    high_parts(2, lambda t: yr_hi[:, bass.ds(h * 2 + t, 1)].rearrange("p a s -> p (a s)"))
                with c.loop(act, KT // 2) as i:
                    for j in range(2):
                        gate_unit(0, j, i * 2 + j)
                        step(1)
                        act.wait_ge(tmp_ready, c.next(tmp_ready))
                        then(act.activation(m_hi[:, bass.ds(i * 2 + j, 1)].rearrange("p a s -> p (a s)"),
                                            t2[:, 0], ACT.Copy, scale=0.5), hi_tile)
                with c.loop(act, KT // 2):
                    for j in range(2):
                        step(j)
                full_norm(mem, MEM, None, mem_hi)
                full_norm(x, S, x_tile, u_hi)
                with c.loop(act, 4) as h:
                    for j in range(2):
                        def before():
                            then(act.activation(xk[:, j], acc[j][:, 0:MEM], ACT.Copy), xa_ready)
                        step(j, before)
                    for j in range(2):
                        def before():
                            then(act.activation(xv[:, j], acc[j][:, 0:MEM], ACT.Copy), v_ready)
                        step(j, before)
                    for j in range(2):
                        def before():
                            then(act.activation(xq[:, j], acc[j][:], ACT.Copy, scale=(2 * P) ** -0.5), xa_ready)
                        step(j, before)
                    for i in range(NBLK):
                        act.wait_ge(max_ready, c.next(max_ready))
                        then(act.activation(prob[:, i % 2], pr[i % 2][:, 0:MEM], ACT.Exp,
                                            bias=small[:, i % 2:i % 2 + 1], accum_out=small[:, 2 + i % 2:3 + i % 2]), prob_raw)
                    act.wait_ge(head_y, c.next(head_y))
                    for t in range(2):
                        then(act.activation(o_hi[:, bass.ds(h * 2 + t, 1)].rearrange("p a s -> p (a s)"), yp[t][:], ACT.Copy), hi_tile)
                with c.loop(act, KT // 2):
                    for j in range(2):
                        step(j)
                full_norm(x, S, x_tile, u_hi)
                with c.loop(act, FFQ):
                    with c.loop(act, KT // 2) as i:
                        for j in range(2):
                            def before():
                                then(act.activation(t2[:, j], acc[j][:], ACT.Relu), relu_ready)

                            def after():
                                act.wait_ge(tmp_ready, c.next(tmp_ready))
                                then(act.activation(h_hi[:, bass.ds(i * 2 + j, 1)].rearrange("p a s -> p (a s)"), e2[:, j], ACT.Copy), hi_tile)
                            step(j, before, after)
                    with c.loop(act, KT // 2):
                        for j in range(2):
                            step(j)
                c.next(x_tile, (FFQ - 1) * KT)
            full_norm(x, S, x_tile, None)
            act.wait_ge(final_ready, 1)
            act.dma_start(a["out"], x[:]).then_inc(out_done, 16)
            act.wait_ge(out_done, 16)

        @block.vector
        def _(dve):
            c = Counts("dve", per, passed)

            def then(ins, signal=dve_step):
                ins.then_inc(signal, 1)
                dve.wait_ge(signal, c.next(signal))

            def split(s):
                dve.wait_ge(hi_ready, c.next(hi_ready))
                then(dve.tensor_tensor(w_lo[:, s], raw[:, s], w_hi[:, s].bitcast(F32), ALU.subtract), lo_ready)

            def step(s, before=None, after=None):
                dve.wait_ge(unit_done, c.next(unit_done))
                if before:
                    before()
                split(s)
                if after:
                    after()

            def low_parts(n, make, hi, lo, width=S):
                for k in range(n + 1):
                    if k < n:
                        make(k)
                    if k:
                        dve.wait_ge(hi_tile, c.next(hi_tile))
                        then(dve.tensor_tensor(lo(k - 1), t2[:, (k - 1) % 2, 0:width], hi(k - 1).bitcast(F32), ALU.subtract), pair_ready)

            def full_norm(src, width, col, hi, lo, out=None):
                for k in range(KT):
                    dve.wait_ge(sq_ready, c.next(sq_ready))
                    s_ = t2[:, k % 2, 0:width]
                    if k == 0:
                        then(dve.tensor_copy(acc_sq[:, 0:width], s_), gated)
                        if width < S:
                            then(dve.memset(acc_sq[:, width:S], 0.0))
                    else:
                        then(dve.tensor_tensor(acc_sq[:, 0:width], acc_sq[:, 0:width], s_, ALU.add),
                             sum_ready if k == KT - 1 else gated if k < KT - 2 else dve_step)
                dve.wait_ge(rstd_ready, c.next(rstd_ready))
                if out is not None:
                    for k in range(KT):
                        then(dve.scalar_tensor_tensor(out[:, k], src[:, k], col(k), rstd[:], ALU.mult, ALU.mult))
                    return

                def make(k):
                    then(dve.scalar_tensor_tensor(t2[:, k % 2, 0:width], src[:, k], col(k), rstd[:, 0:width], ALU.mult, ALU.mult), tmp_ready)
                low_parts(KT, make, lambda k: hi[:, k, 0:width], lambda k: lo[:, k, 0:width], width)
                dve.sem_inc(gated, 2)
                c.next(gated, 2)

            dve.wait_ge(consts_ready, 1)
            dve.wait_ge(pool_step, 2)
            ang, n_hi, n_lo, tmp = t2[:, 0], t2[:, 1], acc_sq[:], e2[:, 1]
            then(dve.tensor_copy(tmp, e2[:, 0].bitcast(I32)))
            then(dve.tensor_scalar(ang, tmp, freq[:, 0:1], None, ALU.mult))
            then(dve.tensor_scalar(tmp, ang, 1.0 / TWO_PI, freq[:, 1:2], ALU.mult, ALU.add))
            then(dve.tensor_scalar(tmp, tmp, MAGIC, None, ALU.add))
            then(dve.tensor_scalar(tmp, tmp, MAGIC, None, ALU.subtract))
            then(dve.tensor_scalar(n_hi, tmp, 4096.0 * MAGIC, None, ALU.add))
            then(dve.tensor_scalar(n_hi, n_hi, 4096.0 * MAGIC, None, ALU.subtract))
            then(dve.tensor_tensor(n_lo, tmp, n_hi, ALU.subtract))
            for n, const in ((n_hi, C1), (n_lo, C1), (n_hi, C2), (n_lo, C2), (tmp, C3)):
                then(dve.scalar_tensor_tensor(ang, n, -const, ang, ALU.mult, ALU.add))
            then(dve.tensor_scalar(ang, ang, freq[:, 2:3], None, ALU.add))
            then(dve.tensor_scalar(ang, ang, 3.1415925, -3.1415925, ALU.min, ALU.max), angle_ready)
            dve.wait_ge(trig_ready, 1)
            dve.wait_ge(x_in, 32)
            dve.sem_inc(x_tile, KT)
            c.next(x_tile, KT)
            dve.sem_inc(gated, 2)
            dve.wait_ge(gated, c.next(gated, 2))
            for s_, n in ((ss_free, 1), (tp_free, 1), (cb_free, 1), (y_free, 1), (row_free, 2), (sc_free, 2), (gp_free, 1), (lp_free, 1), (silu_ready, 2), (e_free, 2),
                          (acc_free[0], 1), (acc_free[1], 1)):
                dve.sem_inc(s_, n)
            for s_, n in ((tp_free, 1), (cb_free, 1), (y_free, 1), (row_free, 2), (sc_free, 2), (gp_free, 1), (lp_free, 1), (silu_ready, 2), (e_free, 2),
                          (acc_free[0], 1), (acc_free[1], 1)):
                c.next(s_, n)
            for s in range(2):
                split(s)

            def conv_unit(s, j, dst):
                def before():
                    dve.wait_ge(lin_ready, c.next(lin_ready))
                    for i in (2, 1, 0):
                        far = 3 - i
                        w = gp_half[:, G_TAP + 4 * j + i:G_TAP + 4 * j + i + 1]
                        if i == 0:
                            ins = dve.scalar_tensor_tensor(t2[:, s, far:S], acc[s][:, 0:S - far], w, t2[:, s, far:S], ALU.mult, ALU.add)
                            then(ins, act_ready)
                            dve.sem_inc(acc_free[s], 1)
                            c.next(acc_free[s])
                        else:
                            then(dve.scalar_tensor_tensor(t2[:, s, far:S], acc[s][:, 0:S - far], w, t2[:, s, far:S], ALU.mult, ALU.add))

                def after():
                    dve.wait_ge(gate_ready, c.next(gate_ready))
                    then(dve.scalar_tensor_tensor(dst, e2[:, s], 1.0, t2[:, s], ALU.add, ALU.mult), silu_ready)
                step(s, before, after)

            def silu_unit(s, dst):
                def after():
                    dve.wait_ge(gate_ready, c.next(gate_ready))
                    then(dve.scalar_tensor_tensor(dst, e2[:, s], 1.0, acc[s][:], ALU.add, ALU.mult), silu_ready)
                    dve.sem_inc(acc_free[s], 1)
                    c.next(acc_free[s])
                step(s, None, after)

            def free(s):
                dve.sem_inc(acc_free[s], 1)
                c.next(acc_free[s])

            with c.loop(dve, DEPTH):
                dve.wait_ge(lp_in, c.next(lp_in, 16))
                then(dve.tensor_scalar(half_gate[:], lp[:, L_GATE:L_GATE + 2 * KT], 0.5, None, ALU.mult), lp_ready)
                full_norm(x, S, lambda k: lp[:, L_MIX + k:L_MIX + k + 1], u_hi, u_lo)

                def dt_part():
                    then(dve.tensor_scalar(dt_w[:, 0], acc[0][0:SSM_HEADS, :], lp[0:SSM_HEADS, L_DTB:L_DTB + 1], None, ALU.add), dt_abs)
                    free(0)
                step(0, dt_part)
                v, s1, s2, p, e = dt_w[:, 0], dt_w[:, 3], dt_w[:, 1], dt_w[:, 4], dt_w[:, 2]
                dve.wait_ge(dt_exp, c.next(dt_exp))
                then(dve.tensor_scalar(s2, e, 2.0, None, ALU.add))
                then(dve.reciprocal(s1, s2))
                then(dve.tensor_tensor(s1, s1, e, ALU.mult))
                then(dve.tensor_tensor(s2, s1, s1, ALU.mult))
                then(dve.tensor_scalar(p, s2, 1.0 / 15, None, ALU.mult))
                for n in (13, 11, 9, 7, 5, 3):
                    then(dve.scalar_tensor_tensor(p, p, 1.0 / n, s2, ALU.add, ALU.mult))
                then(dve.scalar_tensor_tensor(p, p, 1.0, s1, ALU.add, ALU.mult))
                then(dve.tensor_scalar(v, v, 0.0, None, ALU.max))
                then(dve.scalar_tensor_tensor(v, p, 2.0, v, ALU.mult, ALU.add), dt_done)
                step(1, lambda: free(1))
                dve.wait_ge(dt_turned, c.next(dt_turned))
                then(dve.tensor_copy(tok[:, 0].rearrange("p b h -> p (b h)"), tp[:, 0:P]), tp_free)
                dve.wait_ge(tok_part, c.next(tok_part))
                then(dve.scalar_tensor_tensor(t2[:, 0, 0:P].rearrange("p (b h) -> p b h", b=NBLK), tok[:, 0], -1.0,
                                              a_pos[:].unsqueeze(1).broadcast_to([P, NBLK, SSM_HEADS]), ALU.mult, ALU.mult), dta_ready)
                dve.wait_ge(cum_ready, c.next(cum_ready))
                then(dve.tensor_copy(tok[:, 1].rearrange("p b h -> p (b h)"), pr[0][:, 0:P]))
                then(dve.tensor_tensor(tok[:, 2].rearrange("p b h -> p (b h)"), pr[0][:, P:2 * P],
                                       tok[:, 1].rearrange("p b h -> p (b h)"), ALU.subtract))
                then(dve.tensor_copy(tok[:, 3].rearrange("p b h -> p (b h)"), pr[0][:, P:2 * P]), tok_ready)
                dve.wait_ge(tok_part, c.next(tok_part))
                dve.wait_ge(cum_rows, c.next(cum_rows))

                with c.loop(dve, GROUPS) as g:
                    dve.wait_ge(gp_in, c.next(gp_in, 16))
                    then(dve.tensor_scalar(gp_half[:], gp[:, 0:G_SKIP], 0.5, None, ALU.mult), lp_ready)
                    for j, dst in enumerate((b_t[:], c_t[:], xs_t[:, 0], xs_t[:, 1])):
                        conv_unit(j % 2, j, dst)
                    for j in range(2):
                        silu_unit(j, z_t[:, j])

                    def heads(kind, b, n):
                        return tok[:, kind, b, bass.ds(g * HPG, HPG)].unsqueeze(2).broadcast_to([P, HPG, n])

                    for b in range(NBLK):
                        at = slice(b * P, (b + 1) * P)
                        dve.wait_ge(row_in[b % 2], c.next(row_in[b % 2], 16))
                        then(dve.tensor_tensor(seg[:], row[:, b % 2], heads(1, b, P), ALU.subtract), diff_ready)
                        dve.wait_ge(turned, c.next(turned))
                        then(dve.tensor_tensor(xdt[:], tp[:, P:3 * P].rearrange("p (h d) -> p h d", h=HPG), heads(0, b, HD), ALU.mult))
                        then(dve.tensor_copy(b_tok[:], tp[:, 0:P]), tp_free)
                        dve.wait_ge(cb_ready, c.next(cb_ready))
                        then(dve.tensor_tensor(cb_m[:], pr[0][:, 0:P], mask[:], ALU.mult), cb_free)
                        dve.wait_ge(seg_ready, c.next(seg_ready))
                        then(dve.tensor_tensor(seg[:], seg[:], cb_m[:].unsqueeze(1).broadcast_to([P, HPG, P]), ALU.mult), blk_ready)
                        if b:
                            then(dve.tensor_tensor(c_dec[:], c_dec[:], c_t[:, at].unsqueeze(1).broadcast_to([P, HPG, P]), ALU.mult), cdec_ready)
                        dve.sem_inc(row_free, 1)
                        c.next(row_free)
                        if b < NBLK - 1:
                            then(dve.tensor_tensor(xdt_dec[:], xdt[:], heads(2, b, HD), ALU.mult), dec_ready)
                        dve.wait_ge(y_blk, c.next(y_blk))
                        if b < NBLK - 1:
                            dve.wait_ge(st_sum, c.next(st_sum))
                            new = pr[1][:, 0:HPG * HD].rearrange("p (h d) -> p h d", h=HPG)
                            if b == 0:
                                then(dve.tensor_copy(state[:], new), st_ready)
                            else:
                                then(dve.tensor_tensor(state[:], state[:], heads(3, b, HD), ALU.mult))
                                then(dve.tensor_tensor(state[:], state[:], new, ALU.add), st_ready)
                    for t in range(2):
                        then(dve.scalar_tensor_tensor(xs_t[:, t], xs_t[:, t], gp[:, G_SKIP + t:G_SKIP + t + 1], yp[t][:], ALU.mult, ALU.add))
                        then(dve.scalar_tensor_tensor(xs_t[:, t], xs_t[:, t], 0.5, z_t[:, t], ALU.mult, ALU.mult),
                             (out_ready if t else y_free))
                    dve.wait_ge(sq_ready, c.next(sq_ready, 2))
                    then(dve.tensor_tensor(acc_sq[:], z_t[:, 0], z_t[:, 1], ALU.add), sum_ready)
                    dve.wait_ge(rstd_ready, c.next(rstd_ready))

                    def make(t):
                        then(dve.scalar_tensor_tensor(t2[:, t], xs_t[:, t], gp[:, G_NORM + t:G_NORM + t + 1], rstd[:], ALU.mult, ALU.mult), tmp_ready)
                    low_parts(2, make, lambda t: ys_hi[:, bass.ds(g * 2 + t, 1)].rearrange("p a s -> p (a s)"),
                              lambda t: ys_lo[:, bass.ds(g * 2 + t, 1)].rearrange("p a s -> p (a s)"))
                    dve.sem_inc(gp_free, 1)
                    c.next(gp_free)

                with c.loop(dve, KT // 2) as i:
                    for j in range(2):
                        step(j)
                        dve.wait_ge(gate_ready, c.next(gate_ready))
                        free(0)
                        step(1 - j)

                        def before():
                            then(dve.scalar_tensor_tensor(merge[:, bass.ds(i * 2 + j, 1)].rearrange("p a s -> p (a s)"), e2[:, j], 1.0,
                                                          acc[1][:], ALU.add, ALU.mult), e_free)
                            free(1)
                        step(j, before)
                with c.loop(dve, RET_HEADS) as h:
                    for j, dst in enumerate((q_t, k_t)):
                        def before():
                            then(dve.tensor_tensor(dst[:], acc[j][:], cos_sb[:], ALU.mult))
                            then(dve.tensor_tensor(t2[64:128, j], acc[j][0:64], sin_sb[0:64], ALU.mult))
                            then(dve.tensor_tensor(t2[0:64, j], acc[j][64:128], sin_sb[64:128], ALU.mult))
                            free(j)
                            then(dve.tensor_tensor(dst[:], dst[:], t2[:, j], ALU.add))
                        step(j, before)
                    for t in range(2):
                        step(t)
                        dve.wait_ge(v_ready, c.next(v_ready))
                        free(t)
                    for t in range(2):
                        silu_unit(t, g_t[:, t])
                    for t in range(2):
                        dve.wait_ge(turned, c.next(turned))
                        then(dve.tensor_copy(v_tok[:, :, t * P:(t + 1) * P], tp[:].rearrange("p (b e) -> p b e", b=NBLK)), vtok_ready)
                        dve.sem_inc(tp_free, 1)
                        c.next(tp_free)
                    for i in range(NBLK):
                        n = S - i * P
                        dve.wait_ge(sc_ready, c.next(sc_ready))
                        then(dve.tensor_tensor(score[:, i, 0:n], pr[i % 2][:, 0:n], decay[:, bass.ds(h, 1), 0:n].rearrange("p a s -> p (a s)"), ALU.mult), sc_done)
                        dve.sem_inc(sc_free, 1)
                        c.next(sc_free)
                    dve.wait_ge(sq_ready, c.next(sq_ready, 2))
                    dve.sem_inc(y_free, 1)
                    c.next(y_free)
                    then(dve.tensor_tensor(acc_sq[:], t2[:, 0], t2[:, 1], ALU.add), sum_ready)
                    dve.wait_ge(rstd_ready, c.next(rstd_ready))

                    def make(t):
                        then(dve.scalar_tensor_tensor(t2[:, t], v_t[:, t], 0.5, rstd[:], ALU.mult, ALU.mult))
                        then(dve.tensor_tensor(t2[:, t], t2[:, t], g_t[:, t], ALU.mult), tmp_ready)
                    low_parts(2, make, lambda t: yr_hi[:, bass.ds(h * 2 + t, 1)].rearrange("p a s -> p (a s)"),
                              lambda t: yr_lo[:, bass.ds(h * 2 + t, 1)].rearrange("p a s -> p (a s)"))
                with c.loop(dve, KT // 2) as i:
                    for j in range(2):
                        n = bass.ds(i * 2 + j, 1)
                        step(0)
                        dve.wait_ge(gate_ready, c.next(gate_ready))
                        free(0)

                        def before():
                            then(dve.scalar_tensor_tensor(t2[:, 1], e2[:, j], 1.0, acc[1][:], ALU.add, ALU.mult), e_free)
                            free(1)
                            then(dve.tensor_tensor(t2[:, 0], t2[:, 1], merge[:, n].rearrange("p a s -> p (a s)"), ALU.add), tmp_ready)

                        def after():
                            dve.wait_ge(hi_tile, c.next(hi_tile))
                            then(dve.scalar_tensor_tensor(m_lo[:, n].rearrange("p a s -> p (a s)"), t2[:, 0], 0.5,
                                                          m_hi[:, n].rearrange("p a s -> p (a s)").bitcast(F32), ALU.mult, ALU.subtract), pair_ready)
                        step(1, before, after)

                def add_to_x():
                    with c.loop(dve, KT // 2) as i:
                        for j in range(2):
                            def before():
                                n = bass.ds(i * 2 + j, 1)
                                xn = x[:, n].rearrange("p a s -> p (a s)")
                                then(dve.tensor_tensor(xn, xn, acc[j][:], ALU.add), x_tile)
                                free(j)
                            step(j, before)

                c.next(x_tile, KT) if 0 else None
                add_to_x()
                full_norm(mem, MEM, lambda k: lp[:, L_MEM + k:L_MEM + k + 1], mem_hi, mem_lo)
                full_norm(x, S, lambda k: lp[:, L_XA + k:L_XA + k + 1], u_hi, u_lo)
                with c.loop(dve, 4) as h:
                    for j in range(2):
                        step(j)
                        dve.wait_ge(xa_ready, c.next(xa_ready))
                        free(j)
                    for j in range(2):
                        step(j)
                        dve.wait_ge(v_ready, c.next(v_ready))
                        free(j)
                    for j in range(2):
                        step(j)
                        dve.wait_ge(xa_ready, c.next(xa_ready))
                        free(j)
                    for t in range(2):
                        dve.wait_ge(turned, c.next(turned))
                        then(dve.tensor_copy(xv_tok[:, :, t * P:(t + 1) * P], tp[:, 0:2 * P].rearrange("p (m e) -> p m e", m=2)), vtok_ready)
                        dve.sem_inc(tp_free, 1)
                        c.next(tp_free)
                    for i in range(NBLK + 1):
                        if i < NBLK:
                            dve.wait_ge(sc_ready, c.next(sc_ready))
                            then(dve.tensor_reduce(small[:, 4:5], pr[i % 2][:, 0:MEM], AX, ALU.max))
                            then(dve.tensor_scalar(small[:, i % 2:i % 2 + 1], small[:, 4:5], -1.0, None, ALU.mult), max_ready)
                            dve.wait_ge(prob_raw, c.next(prob_raw))
                            dve.sem_inc(sc_free, 1)
                            c.next(sc_free)
                            then(dve.reciprocal(small[:, 5:6], small[:, 2 + i % 2:3 + i % 2]))
                            then(dve.tensor_scalar(prob[:, i % 2], prob[:, i % 2], small[:, 5:6], None, ALU.mult), prob_ready)
                        if i:
                            dve.wait_ge(turned, c.next(turned))
                            then(dve.tensor_copy(prob_t[:, :, (i - 1) * P:i * P], tp[:, 0:2 * P].rearrange("p (m s) -> p m s", m=2)), probt_ready)
                            dve.sem_inc(tp_free, 1)
                            c.next(tp_free)
                    for t in range(2):
                        n = bass.ds(h * 2 + t, 1)
                        dve.wait_ge(hi_tile, c.next(hi_tile))
                        then(dve.tensor_tensor(o_lo[:, n].rearrange("p a s -> p (a s)"), yp[t][:],
                                               o_hi[:, n].rearrange("p a s -> p (a s)").bitcast(F32), ALU.subtract), pair_ready)
                    dve.sem_inc(y_free, 1)
                    c.next(y_free)
                add_to_x()
                full_norm(x, S, lambda k: lp[:, L_MLP + k:L_MLP + k + 1], u_hi, u_lo)
                dve.sem_inc(lp_free, 1)
                c.next(lp_free)
                with c.loop(dve, FFQ):
                    with c.loop(dve, KT // 2) as i:
                        for j in range(2):
                            n = bass.ds(i * 2 + j, 1)

                            def before():
                                dve.wait_ge(relu_ready, c.next(relu_ready))
                                free(j)
                                then(dve.tensor_tensor(e2[:, j], t2[:, j], t2[:, j], ALU.mult), tmp_ready)

                            def after():
                                dve.wait_ge(hi_tile, c.next(hi_tile))
                                then(dve.tensor_tensor(h_lo[:, n].rearrange("p a s -> p (a s)"), e2[:, j],
                                                       h_hi[:, n].rearrange("p a s -> p (a s)").bitcast(F32), ALU.subtract), pair_ready)
                            step(j, before, after)
                    add_to_x()
            full_norm(x, S, lambda k: fin_w[:, k:k + 1], None, None, out=x)
            dve.sem_inc(final_ready, 1)


def _layout(x, mem, positions, norm_mix, w_in, b_gate, conv_w, conv_b, dt_bias, a_log, d_skip, ssm_norm,
            w_br_ret, w_br_ssm, w_out, norm_xa, norm_mem, xa_wq, xa_wkv, xa_wo, norm_mlp, mlp_w1, mlp_w2, norm_final):
    f = np.float32

    def units(w):
        r, n = w.shape
        return w.reshape(r // D, KT, P, n // P, P).transpose(3, 0, 2, 1, 4)

    stream = np.zeros((DEPTH * UNITS + AHEAD, P, KT, P), f)
    lps = np.zeros((DEPTH, P, LPN), f)
    gps = np.zeros((DEPTH * GROUPS, P, GPN), f)

    def cols(v):
        return v.reshape(-1, P).T

    for l in range(DEPTH):
        at = l * UNITS

        def put(u, at):
            stream[at:at + len(u)] = u
            return at + len(u)

        wi = w_in[l]
        stream[at, :, :, 0:SSM_HEADS] = wi[:, O_DT:O_DT + SSM_HEADS].reshape(KT, P, SSM_HEADS).transpose(1, 0, 2)
        at += 2

        def part(o, n):
            return units(wi[:, o:o + n * P])[:, 0]

        for g in range(GROUPS):
            for o, n in ((O_B + g * P, 1), (O_C + g * P, 1), (O_XS + g * 2 * P, 2), (O_Z + g * 2 * P, 2)):
                at = put(part(o, n), at)
        br, gates = units(w_br_ssm[l]), part(O_GATE, 2 * KT)
        for n in range(KT):
            at = put(gates[KT + n:KT + n + 1], at)
            at = put(br[n], at)
        for h in range(RET_HEADS):
            for o, n in ((O_Q + h * P, 1), (O_K + h * P, 1), (O_V + h * 2 * P, 2), (O_G + h * 2 * P, 2)):
                at = put(part(o, n), at)
        br = units(w_br_ret[l])
        for n in range(KT):
            at = put(gates[n:n + 1], at)
            at = put(br[n], at)
        at = put(units(w_out[l])[:, 0], at)
        q, kv = units(xa_wq[l])[:, 0], units(xa_wkv[l])[:, 0]
        for h in range(4):
            at = put(kv[2 * h:2 * h + 2], at)
            at = put(kv[KT + 2 * h:KT + 2 * h + 2], at)
            at = put(q[2 * h:2 * h + 2], at)
        at = put(units(xa_wo[l])[:, 0], at)
        w1, w2 = units(mlp_w1[l])[:, 0], units(mlp_w2[l])
        for q4 in range(FFQ):
            at = put(w1[q4 * KT:(q4 + 1) * KT], at)
            at = put(w2[:, q4], at)
        assert at == (l + 1) * UNITS

        for o, v in ((L_MIX, norm_mix), (L_XA, norm_xa), (L_MEM, norm_mem), (L_MLP, norm_mlp), (L_GATE, b_gate)):
            lps[l, :, o:o + v.shape[1] // P] = cols(v[l])
        lps[l, :, L_ALOG:L_ALOG + SSM_HEADS] = a_log[l][None, :]
        lps[l, 0:SSM_HEADS, L_DTB] = dt_bias[l]
        skip = np.repeat(d_skip[l], HD)
        for g in range(GROUPS):
            gpt = gps[l * GROUPS + g]
            for j, o in enumerate((SSM_INNER + g * P, SSM_INNER + BC + g * P, g * 2 * P, g * 2 * P + P)):
                gpt[:, G_TAP + 4 * j:G_TAP + 4 * j + 4] = conv_w[l][:, o:o + P].T
                gpt[:, G_BIAS + j] = conv_b[l][o:o + P]
            gpt[:, G_SKIP:G_SKIP + 2] = cols(skip[g * 2 * P:(g + 1) * 2 * P])
            gpt[:, G_NORM:G_NORM + 2] = cols(ssm_norm[l][g * 2 * P:(g + 1) * 2 * P])

    i = np.arange(P)
    upto = (i[:, None] <= i[None, :]).astype(f)
    mask = (i[:, None] // CHUNK <= i[None, :] // CHUNK).astype(f)
    lg = np.log1p(-(2.0 ** (-5.0 - np.arange(RET_HEADS))))
    m, l_ = np.arange(P)[:, None], np.arange(S)[None, :]
    decay = np.exp(lg[None, :, None] * np.abs(l_ - m)[:, None, :]) * (m // CHUNK <= l_ // CHUNK)[:, None, :] * P ** -0.5
    freq = np.zeros((P, 4), f)
    freq[:, 0] = np.tile(10000.0 ** (-np.arange(0, P, 2) / P), 2)
    freq[64:, 1] = 0.25
    freq[64:, 2] = np.pi / 2
    return {
        "stream": stream, "lp": lps, "gp": gps,
        "x": np.ascontiguousarray(x[0].T.reshape(KT, P, S).transpose(1, 0, 2)),
        "mem": np.ascontiguousarray(mem[0].T.reshape(KT, P, MEM).transpose(1, 0, 2)),
        "pos": np.ascontiguousarray(positions[0]),
        "fin_w": np.ascontiguousarray(cols(norm_final)),
        "ident": np.eye(P, dtype=f), "upto": upto, "mask": mask,
        "decay": decay.astype(f), "freq": freq,
    }


def kernel(**inputs):
    import concourse.bacc as bacc
    from concourse.bass_utils import run_bass_kernel_spmd

    arrays = _layout(**{k: np.asarray(v) for k, v in inputs.items()})

    def build(per):
        nc = bacc.Bacc("TRN2", target_bir_lowering=False, num_devices=1)
        a = {n: nc.dram_tensor(f"in_{n}", v.shape, mybir.dt.from_np(v.dtype), kind="ExternalInput").ap() for n, v in arrays.items()}
        a["out"] = nc.dram_tensor("out_0", [P, KT, S], F32, kind="ExternalOutput").ap()
        program(nc, a, per)
        return nc

    per = {}
    build(per)
    nc = build(per)
    r = run_bass_kernel_spmd(nc, [{f"in_{n}": v for n, v in arrays.items()}], core_ids=[0])
    out = r.results[0]["out_0"]
    return np.ascontiguousarray(out.transpose(1, 0, 2).reshape(D, S).T)[None]
```

```python
from contextlib import ExitStack, contextmanager

import numpy as np

import concourse.bass as bass
from concourse import mybir

F32 = mybir.dt.float32
F32R = mybir.dt.float32r
I32 = mybir.dt.int32
ALU = mybir.AluOpType
ACT = mybir.ActivationFunctionType
AX = mybir.AxisListType.X

P = 128
D = 1024
S = 512
KT = D // P
DEPTH = 2
MEM = 256
CHUNK = 64
NBLK = S // P
EPS = 1e-6
RET_HEADS = 4
RET_QK = 512
RET_V = 1024
SSM_INNER = 2048
SSM_HEADS = 32
GROUPS = 8
HPG = SSM_HEADS // GROUPS
HD = SSM_INNER // SSM_HEADS
BC = 1024
D_FF = 4096
FFQ = D_FF // D

O_Q = 0
O_K = O_Q + RET_QK
O_V = O_K + RET_QK
O_G = O_V + RET_V
O_Z = O_G + RET_V
O_XS = O_Z + SSM_INNER
O_B = O_XS + SSM_INNER
O_C = O_B + BC
O_DT = O_C + BC
O_GATE = O_DT + SSM_HEADS

UNITS = 2 + GROUPS * 6 + KT * 3 + RET_HEADS * 6 + KT * 2 + KT + 4 * 6 + KT + FFQ * 2 * KT
AHEAD = 2

L_MIX, L_XA, L_MEM, L_MLP, L_GATE, L_ALOG, L_DTB = 0, 8, 16, 24, 32, 48, 80
LPN = 81
G_TAP, G_BIAS, G_SKIP, G_NORM = 0, 16, 20, 22
GPN = 24

TWO_PI = 2 * np.pi
C1 = 6.28125
C2 = float(np.float32(np.round((TWO_PI - C1) * 2**21) / 2**21))
C3 = float(np.float32(TWO_PI - C1 - C2))
MAGIC = 1.5 * 2.0**23


class Counts:

    def __init__(self, engine, per, always):
        self.engine, self.per, self.always = engine, per, always
        self.n, self.active, self.loops = {}, [], 0

    def now(self, sem):
        value = self.n.get(sem.name, 0)
        for index, counts in self.active:
            if counts.get(sem.name, 0):
                value = index * counts[sem.name] + value
        return value

    def next(self, sem, by=1):
        self.n[sem.name] = self.n.get(sem.name, 0) + by
        return self.now(sem)

    @contextmanager
    def loop(self, eng, times):
        self.loops += 1
        label = (self.engine, self.loops)
        before = dict(self.n)
        if self.active:
            eng.sem_inc(self.always, 1)
        with eng.Fori(0, times) as index:
            self.active.append((index, self.per.get(label, {})))
            yield index
            self.active.pop()
        once = {s: v - before.get(s, 0) for s, v in self.n.items()}
        self.per[label] = once
        self.n = {s: before.get(s, 0) + times * v for s, v in once.items()}


def program(nc, a, per):
    with ExitStack() as ctx:
        def sb(name, shape, dt=F32, stack=ctx):
            return stack.enter_context(nc.sbuf_tensor(name, shape, dt))

        def sem(name):
            return ctx.enter_context(nc.semaphore(name))

        x = sb("x", [P, KT, S])
        u_hi, u_lo = sb("u_hi", [P, KT, S], F32R), sb("u_lo", [P, KT, S], F32R)
        raw = sb("raw", [P, 2, KT, P])
        w_hi, w_lo = sb("w_hi", [P, 2, KT, P], F32R), sb("w_lo", [P, 2, KT, P], F32R)
        cos_sb, sin_sb = sb("cos_sb", [P, S]), sb("sin_sb", [P, S])
        decay = sb("decay", [P, RET_HEADS, S])
        ident, upto, mask = sb("ident", [P, P]), sb("upto", [P, P]), sb("mask", [P, P])
        ones = sb("ones", [P, P])
        eps_t = sb("eps_t", [P, 1])
        lp = sb("lp", [P, LPN])
        fin_w = sb("fin_w", [P, KT])
        half_gate = sb("half_gate", [P, 2 * KT])
        a_pos = sb("a_pos", [P, SSM_HEADS])
        gp = [sb(f"gp{i}", [P, GPN]) for i in range(2)]
        gp_half = [sb(f"gp_half{i}", [P, G_SKIP]) for i in range(2)]
        freq = sb("freq", [P, 4])
        t2, e2 = sb("t2", [P, 2, S]), sb("e2", [P, 2, S])
        rstd, acc_sq = sb("rstd", [P, S]), sb("acc_sq", [P, S])
        tok = sb("tok", [P, 4, NBLK, SSM_HEADS])
        small = sb("small", [P, 8])

        with ExitStack() as ssm:
            b_t, c_t, xs_t, z_t = {}, {}, {}, {}

            def group_buffer(p):
                b_t[p], c_t[p] = sb(f"b_t{p}", [P, S], F32, ssm), sb(f"c_t{p}", [P, S], F32, ssm)
                xs_t[p], z_t[p] = sb(f"xs_t{p}", [P, 2, S], F32, ssm), sb(f"z_t{p}", [P, 2, S], F32, ssm)

            group_buffer(0)
            sb("under_merge", [P, 4 * 256], F32, ssm)
            group_buffer(1)
            b_tok = sb("b_tok", [P, P], F32, ssm)
            xdt, xdt_dec = sb("xdt", [P, HPG, HD], F32, ssm), sb("xdt_dec", [P, HPG, HD], F32, ssm)
            row = sb("row", [P, 2, HPG, P], F32, ssm)
            seg, c_dec = sb("seg", [P, HPG, P], F32, ssm), sb("c_dec", [P, HPG, P], F32, ssm)
            cb_m = sb("cb_m", [P, P], F32, ssm)
            state = sb("state", [P, HPG, HD], F32, ssm)
            with ExitStack() as early:
                dt_v, dt_rows_sb = sb("dt_v", [SSM_HEADS, S], F32, early), sb("dt_rows_sb", [SSM_HEADS, S], F32, early)
                dt_w = sb("dt_w", [P, 5, P], F32, early)
            ys_hi, ys_lo = sb("ys_hi", [P, 2 * KT, S], F32R, ssm), sb("ys_lo", [P, 2 * KT, S], F32R, ssm)
        with ExitStack() as mix:
            merge = sb("merge", [P, KT, S], F32, mix)
            yr_hi, yr_lo = sb("yr_hi", [P, KT, S], F32R, mix), sb("yr_lo", [P, KT, S], F32R, mix)
            with ExitStack() as ret:
                q_t, k_t, v_t, g_t = {}, {}, {}, {}

                def head_buffer(p):
                    q_t[p], k_t[p] = sb(f"q_t{p}", [P, S], F32, ret), sb(f"k_t{p}", [P, S], F32, ret)
                    v_t[p], g_t[p] = sb(f"v_t{p}", [P, 2, S], F32, ret), sb(f"g_t{p}", [P, 2, S], F32, ret)

                head_buffer(0)
                sb("under_gate", [P, 4 * 256], F32, ret)
                head_buffer(1)
                v_tok = sb("v_tok", [P, NBLK, 2 * P], F32, ret)
                score = [sb(f"score{i}", [P, S - i * P], F32, ret) for i in range(NBLK)]
            gate_r = sb("gate_r", [P, KT, S], F32, mix)
            m_hi, m_lo = sb("m_hi", [P, KT, S], F32R, mix), sb("m_lo", [P, KT, S], F32R, mix)
            mem = sb("mem_t", [P, KT, MEM], F32, mix)
        with ExitStack() as xa:
            mem_hi, mem_lo = sb("mem_hi", [P, KT, MEM], F32R, xa), sb("mem_lo", [P, KT, MEM], F32R, xa)
            o_hi, o_lo = sb("o_hi", [P, KT, S], F32R, xa), sb("o_lo", [P, KT, S], F32R, xa)
            sb("under_m", [P, 16 * 256], F32, xa)
            xk, xv = [sb(f"xk{p}", [P, 2, MEM], F32, xa) for p in range(2)], [sb(f"xv{p}", [P, 2, MEM], F32, xa) for p in range(2)]
            xq = [sb(f"xq{p}", [P, 2, S], F32, xa) for p in range(2)]
            xv_tok = sb("xv_tok", [P, 2, 2 * P], F32, xa)
            prob = sb("prob", [P, 2, MEM], F32, xa)
            prob_t = sb("prob_t", [P, 2, S], F32, xa)
        h_hi, h_lo = sb("h_hi", [P, KT, S], F32R), sb("h_lo", [P, KT, S], F32R)

        acc = [ctx.enter_context(nc.psum_tensor(f"acc{i}", [P, S], F32)) for i in range(2)]
        tp = ctx.enter_context(nc.psum_tensor("tp", [P, S], F32))
        pr = [ctx.enter_context(nc.psum_tensor(f"pr{i}", [P, S], F32)) for i in range(2)]
        yp = [ctx.enter_context(nc.psum_tensor(f"yp{i}", [P, S], F32)) for i in range(2)]
        ss = ctx.enter_context(nc.psum_tensor("ss", [P, S], F32))
        cum_dram = nc.dram_tensor("cum_scratch", [GROUPS, HPG, S], F32, kind="Internal").ap()

        passed = sem("passed")
        const_in, angle_in = sem("const_in"), sem("angle_in")
        x_in, mem_in, mem_free = sem("x_in"), sem("mem_in"), sem("mem_free")
        lp_in, gp_in = sem("lp_in"), [sem("gp_in0"), sem("gp_in1")]
        raw_in = [sem("raw_in0"), sem("raw_in1")]
        hi_ready, lo_ready, unit_done = sem("hi_ready"), sem("lo_ready"), sem("unit_done")
        acc_free = [sem("acc_free0"), sem("acc_free1")]
        dve_step, act_step, pool_step = sem("dve_step"), sem("act_step"), sem("pool_step")
        x_tile = sem("x_tile")
        sq_ready, sq_free, sum_ready = sem("sq_ready"), sem("sq_free"), sem("sum_ready")
        ss_ready, ss_free, rstd_ready = sem("ss_ready"), sem("ss_free"), sem("rstd_ready")
        tmp_ready, hi_tile, pair_ready = sem("tmp_ready"), sem("hi_tile"), sem("pair_ready")
        consts_ready = sem("consts_ready")
        angle_ready, trig_ready = sem("angle_ready"), sem("trig_ready")
        lp_ready, lp_free, a_ready = sem("lp_ready"), sem("lp_free"), sem("a_ready")
        gp_ready, gp_free = sem("gp_ready"), sem("gp_free")
        dt_in, dt_turned, dt_copied, dt_exp = sem("dt_in"), sem("dt_turned"), sem("dt_copied"), sem("dt_exp")
        dta_ready, cum_ready, dec_in, dec_out = sem("dta_ready"), sem("cum_ready"), sem("dec_in"), sem("dec_out")
        cum_rows, cum_out = sem("cum_rows"), sem("cum_out")
        row_in, row_free = [sem("row_in0"), sem("row_in1")], sem("row_free")
        lin_ready, conv_ready, tanh_ready, silu_ready = sem("lin_ready"), sem("conv_ready"), sem("tanh_ready"), sem("silu_ready")
        turned, tp_free = sem("turned"), sem("tp_free")
        cb_ready, cb_free = sem("cb_ready"), sem("cb_free")
        seg_ready, edec_ready, cdec_ready = sem("seg_ready"), sem("edec_ready"), sem("cdec_ready")
        blk_ready, y_blk = sem("blk_ready"), sem("y_blk")
        dec_ready, st_sum, st_ready = sem("dec_ready"), sem("st_sum"), sem("st_ready")
        y_free, out_ready = sem("y_free"), sem("out_ready")
        gate_ready = sem("gate_ready")
        v_ready, sc_ready, sc_free, sc_done = sem("v_ready"), sem("sc_ready"), sem("sc_free"), sem("sc_done")
        vtok_ready, head_y, y_copied = sem("vtok_ready"), sem("head_y"), sem("y_copied")
        q_ready, xa_ready = sem("q_ready"), sem("xa_ready")
        max_ready, prob_raw, prob_ready = sem("max_ready"), sem("prob_raw"), sem("prob_ready")
        probt_ready = sem("probt_ready")
        relu_ready = sem("relu_ready")
        mem_sq, mem_tmp, mem_hi_ready, mem_tile, mem_slot = sem("mem_sq"), sem("mem_tmp"), sem("mem_hi_ready"), sem("mem_tile"), sem("mem_slot")
        final_ready, out_done = sem("final_ready"), sem("out_done")

        def tile(t, n):
            return t[:, bass.ds(n, 1)].rearrange("p a s -> p (a s)")

        block = ctx.enter_context(nc.Block())

        @block.sync
        def _(sp):
            sp.dma_start(x[:, 0:KT // 2], a["x"][:, 0:KT // 2]).then_inc(x_in, 16)
            sp.dma_start(x[:, KT // 2:KT], a["x"][:, KT // 2:KT]).then_inc(x_in, 16)
            for s in range(2):
                sp.dma_start(raw[:, s], a["stream"][s]).then_inc(raw_in[s], 16)
            with sp.Fori(1, (DEPTH * UNITS + AHEAD) // 2) as i:
                for s in range(2):
                    sp.wait_ge(lo_ready, i * 2 + (s - 1))
                    sp.dma_start(raw[:, s], a["stream"][bass.ds(i * 2 + s, 1)].rearrange("a p k c -> p (a k) c")).then_inc(raw_in[s], 16)

        @block.gpsimd
        def _(pool):
            c = Counts("pool", per, passed)
            pool.dma_start(freq[:], a["freq"]).then_inc(angle_in, 16)
            pool.dma_start(e2[:, 0].bitcast(I32), a["pos"].partition_broadcast(P)).then_inc(angle_in, 16)
            pool.memset(ones[:], 1.0).then_inc(pool_step, 1)
            pool.memset(eps_t[:], EPS).then_inc(pool_step, 1)
            pool.wait_ge(pool_step, c.next(pool_step, 2))

            def layer_parameters(l):
                pool.wait_ge(lp_free, c.next(lp_free))
                pool.sem_inc(passed, 1)
                pool.dma_start(lp[:], a["lp"][bass.ds(l, 1)].rearrange("a p n -> p (a n)")).then_inc(lp_in, 16)

            pool.dma_start(ident[:], a["ident"]).then_inc(const_in, 16)
            pool.dma_start(upto[:], a["upto"]).then_inc(const_in, 16)
            pool.dma_start(mask[:], a["mask"]).then_inc(const_in, 16)
            pool.dma_start(fin_w[:], a["fin_w"]).then_inc(const_in, 16)
            pool.dma_start(decay[:], a["decay"]).then_inc(const_in, 16)
            with c.loop(pool, DEPTH) as l:
                layer_parameters(l)

                def group(g, p):
                    pool.wait_ge(gp_free, c.next(gp_free))
                    pool.sem_inc(passed, 1)
                    pool.dma_start(gp[p][:], a["gp"][bass.ds(l * GROUPS + g, 1)].rearrange("a p n -> p (a n)")).then_inc(gp_in[p], 16)

                def rows(g):
                    for b in range(NBLK):
                        pool.wait_ge(row_free, c.next(row_free))
                        pool.sem_inc(passed, 1)
                        pool.dma_start(row[:, b % 2], cum_dram[bass.ds(g, 1), :, b * P:(b + 1) * P]
                                       .rearrange("a h s -> (a h) s").partition_broadcast(P)).then_inc(row_in[b % 2], 16)

                group(0, 0)
                with c.loop(pool, GROUPS // 2 - 1) as i:
                    group(i * 2 + 1, 1)
                    pool.wait_ge(cum_out, l * 16 + 16)
                    rows(i * 2)
                    group(i * 2 + 2, 0)
                    rows(i * 2 + 1)
                group(GROUPS - 1, 1)
                rows(GROUPS - 2)
                rows(GROUPS - 1)
                pool.wait_ge(mem_free, c.next(mem_free))
                pool.sem_inc(passed, 1)
                pool.dma_start(mem[:], a["mem"]).then_inc(mem_in, 16)

        @block.tensor
        def _(pe):
            c = Counts("pe", per, passed)

            def unit(s, bank, hi, lo, first=True, last=True, width=S, tiles=None):
                pe.wait_ge(hi_ready, c.next(hi_ready))
                if first:
                    pe.wait_ge(acc_free[bank], c.next(acc_free[bank]))
                out = acc[bank][:, 0:width]
                for k in range(KT):
                    if tiles is not None:
                        pe.wait_ge(tiles[0], tiles[1] + (k + 1))
                    pe.matmul(out, w_hi[:, s, k], hi[:, k, 0:width], start=first and k == 0, stop=False)
                    pe.matmul(out, w_hi[:, s, k], lo[:, k, 0:width], start=False, stop=False)
                pe.wait_ge(lo_ready, c.next(lo_ready))
                for k in range(KT):
                    mm = pe.matmul(out, w_lo[:, s, k], hi[:, k, 0:width], start=False, stop=last and k == KT - 1)
                mm.then_inc(unit_done, 1)

            def expect(signal, n=KT):
                base = c.now(signal)
                c.next(signal, n)
                return signal, base

            def sum_of_squares():
                pe.wait_ge(sum_ready, c.next(sum_ready))
                pe.wait_ge(ss_free, c.next(ss_free))
                pe.matmul(ss[:], ones[:], acc_sq[:], start=True, stop=True).then_inc(ss_ready, 1)

            def in_unit(j, tiles=None):
                unit(j % 2, j % 2, u_hi, u_lo, tiles=tiles)

            def dt_turn():
                pe.wait_ge(dt_in, c.next(dt_in))
                pe.wait_ge(tp_free, c.next(tp_free))
                pe.sem_inc(passed, 1)
                for b in range(NBLK):
                    t = pe.transpose(tp[:, b * SSM_HEADS:(b + 1) * SSM_HEADS], dt_v[:, b * P:(b + 1) * P],
                                     ident[0:SSM_HEADS, 0:SSM_HEADS])
                t.then_inc(dt_turned, 1)

            def dt_sums():
                pe.wait_ge(dta_ready, c.next(dta_ready))
                dta = dt_w[:, 4]
                pe.matmul(pr[0][:, 0:P], upto[:], dta, start=True, stop=True)
                pe.matmul(pr[0][:, P:2 * P], ones[:], dta, start=True, stop=True)
                for b in range(NBLK):
                    mm = pe.matmul(pr[1][0:SSM_HEADS, b * P:(b + 1) * P], dta[:, b * SSM_HEADS:(b + 1) * SSM_HEADS], upto[:],
                                   start=True, stop=True)
                mm.then_inc(cum_ready, 1)

            def scan_stage(j, p):
                if j == 0:
                    pe.wait_ge(silu_ready, c.next(silu_ready, 6))
                if 1 <= j <= NBLK:
                    b = j - 1
                    at = slice(b * P, (b + 1) * P)
                    pe.wait_ge(blk_ready, c.next(blk_ready))
                    if b == 0:
                        pe.wait_ge(y_free, c.next(y_free))
                    else:
                        pe.wait_ge(cdec_ready, c.next(cdec_ready))
                        pe.wait_ge(st_ready, c.next(st_ready))
                    for h in range(HPG):
                        out = yp[h // 2][h % 2 * HD:(h % 2 + 1) * HD, at]
                        mm = pe.matmul(out, xdt[:, h], seg[:, h], start=True, stop=b == 0)
                        if b:
                            mm = pe.matmul(out, state[:, h], c_dec[:, h], start=False, stop=True)
                    mm.then_inc(y_blk, 1)
                    if b < NBLK - 1:
                        pe.wait_ge(dec_ready, c.next(dec_ready))
                        pe.matmul(pr[1][:, 0:HPG * HD], b_tok[:], xdt_dec[:].rearrange("p h d -> p (h d)"),
                                  start=True, stop=True).then_inc(st_sum, 1)
                if j < NBLK:
                    at = slice(j * P, (j + 1) * P)
                    pe.wait_ge(tp_free, c.next(tp_free))
                    pe.transpose(tp[:, 0:P], b_t[p][:, at], ident[:])
                    pe.transpose(tp[:, P:2 * P], xs_t[p][:, 0, at], ident[:])
                    pe.transpose(tp[:, 2 * P:3 * P], xs_t[p][:, 1, at], ident[:]).then_inc(turned, 1)
                    pe.wait_ge(cb_free, c.next(cb_free))
                    pe.matmul(pr[0][:, 0:P], b_t[p][:, at], c_t[p][:, at], start=True, stop=True).then_inc(cb_ready, 1)
                if j == NBLK + 1:
                    sum_of_squares()

            def head_stage(j, p):
                if j < 2:
                    if j == 0:
                        c.next(silu_ready, 2)
                        pe.wait_ge(q_ready, c.next(q_ready, 2))
                        pe.wait_ge(v_ready, c.next(v_ready, 2))
                    pe.wait_ge(tp_free, c.next(tp_free))
                    for b in range(NBLK):
                        mm = pe.transpose(tp[:, b * P:(b + 1) * P], v_t[p][:, j, b * P:(b + 1) * P], ident[:])
                    mm.then_inc(turned, 1)
                    for i in (2 * j, 2 * j + 1):
                        pe.wait_ge(sc_free, c.next(sc_free))
                        pe.matmul(pr[i % 2][:, 0:S - i * P], k_t[p][:, i * P:(i + 1) * P], q_t[p][:, i * P:S],
                                  start=True, stop=True).then_inc(sc_ready, 1)
                if j == 2:
                    pe.wait_ge(vtok_ready, c.next(vtok_ready, 2))
                    pe.wait_ge(y_free, c.next(y_free))
                    for i in range(NBLK):
                        pe.wait_ge(sc_done, c.next(sc_done))
                        for t in range(2):
                            mm = pe.matmul(yp[t][:, i * P:S], v_tok[:, i, t * P:(t + 1) * P], score[i][:],
                                           start=i == 0, stop=i == NBLK - 1)
                    mm.then_inc(head_y, 1)
                if j == 4:
                    sum_of_squares()

            def attention_stage(j, p):
                if j == 0:
                    pe.wait_ge(xa_ready, c.next(xa_ready, 4))
                    pe.wait_ge(v_ready, c.next(v_ready, 2))
                if j < 2:
                    pe.wait_ge(tp_free, c.next(tp_free))
                    for m in range(2):
                        mm = pe.transpose(tp[:, m * P:(m + 1) * P], xv[p][:, j, m * P:(m + 1) * P], ident[:])
                    mm.then_inc(turned, 1)
                if j < NBLK:
                    pe.wait_ge(sc_free, c.next(sc_free))
                    for k in range(2):
                        mm = pe.matmul(pr[j % 2][:, 0:MEM], xq[p][:, k, j * P:(j + 1) * P], xk[p][:, k],
                                       start=k == 0, stop=k == 1)
                    mm.then_inc(sc_ready, 1)
                if 2 <= j < NBLK + 2:
                    pe.wait_ge(prob_ready, c.next(prob_ready))
                    pe.wait_ge(tp_free, c.next(tp_free))
                    for m in range(2):
                        mm = pe.transpose(tp[:, m * P:(m + 1) * P], prob[:, j % 2, m * P:(m + 1) * P], ident[:])
                    mm.then_inc(turned, 1)

            def attention_out():
                pe.wait_ge(probt_ready, c.next(probt_ready, NBLK))
                pe.wait_ge(vtok_ready, c.next(vtok_ready, 2))
                pe.wait_ge(y_free, c.next(y_free))
                for t in range(2):
                    for m in range(2):
                        mm = pe.matmul(yp[t][:], xv_tok[:, m, t * P:(t + 1) * P], prob_t[:, m], start=m == 0, stop=m == 1)
                mm.then_inc(head_y, 1)

            def xa_unit(j, mem_tiles, tiles):
                if j < 4:
                    unit(j % 2, j % 2, mem_hi, mem_lo, width=MEM, tiles=mem_tiles)
                else:
                    unit(j % 2, j % 2, u_hi, u_lo, tiles=tiles)

            def plain_units(hi, lo, tiles):
                with c.loop(pe, KT // 2):
                    unit(0, 0, hi, lo, tiles=tiles)
                    unit(1, 1, hi, lo)

            pe.wait_ge(pool_step, 2)
            c.next(silu_ready, 2)
            with c.loop(pe, DEPTH):
                sum_of_squares()
                unit(0, 0, u_hi, u_lo, tiles=expect(pair_ready))
                pe.wait_ge(hi_ready, c.next(hi_ready))
                pe.wait_ge(lo_ready, c.next(lo_ready))
                pe.wait_ge(acc_free[1], c.next(acc_free[1]))
                pe.matmul(acc[1][:, 0:P], w_hi[:, 1, 0], w_lo[:, 1, 0], start=True, stop=True).then_inc(unit_done, 1)
                pe.wait_ge(consts_ready, 1)
                for j in range(6):
                    in_unit(j)
                    if j == 0:
                        dt_turn()
                    if j == 2:
                        dt_sums()
                with c.loop(pe, GROUPS // 2 - 1):
                    for p in range(2):
                        for j in range(6):
                            scan_stage(j, p)
                            in_unit(j)
                for j in range(6):
                    scan_stage(j, 0)
                    in_unit(j)
                for j in range(KT):
                    scan_stage(j, 1)
                    in_unit(j)
                tiles = expect(pair_ready, 2 * KT)
                with c.loop(pe, KT // 2):
                    for j in range(2):
                        unit(0, j, ys_hi[:, 0:KT], ys_lo[:, 0:KT], last=False, tiles=tiles)
                        unit(1, j, ys_hi[:, KT:2 * KT], ys_lo[:, KT:2 * KT], first=False, tiles=(tiles[0], tiles[1] + KT))
                for j in range(6):
                    in_unit(j)
                with c.loop(pe, RET_HEADS // 2 - 1):
                    for p in range(2):
                        for j in range(6):
                            head_stage(j, p)
                            in_unit(j)
                for j in range(6):
                    head_stage(j, 0)
                    in_unit(j)
                for j in range(KT):
                    head_stage(j, 1)
                    in_unit(j)
                plain_units(yr_hi, yr_lo, expect(pair_ready))
                sum_of_squares()
                plain_units(m_hi, m_lo, expect(pair_ready))
                sum_of_squares()
                mem_tiles, tiles = expect(mem_tile), expect(pair_ready)
                for j in range(6):
                    xa_unit(j, mem_tiles, tiles)
                with c.loop(pe, 1):
                    for p in range(2):
                        for j in range(6):
                            attention_stage(j, p)
                            xa_unit(j, None, None)
                        attention_out()
                for j in range(6):
                    attention_stage(j, 0)
                    xa_unit(j, None, None)
                attention_out()
                for j in range(6):
                    attention_stage(j, 1)
                attention_out()
                plain_units(o_hi, o_lo, expect(pair_ready))
                sum_of_squares()
                tiles = expect(pair_ready)
                with c.loop(pe, FFQ):
                    plain_units(u_hi, u_lo, tiles)
                    plain_units(h_hi, h_lo, expect(pair_ready))
            sum_of_squares()

        @block.scalar
        def _(act):
            c = Counts("act", per, passed)

            def then(ins, signal=act_step):
                ins.then_inc(signal, 1)
                act.wait_ge(signal, c.next(signal))

            def split(s):
                act.wait_ge(raw_in[s], c.next(raw_in[s], 16))
                then(act.activation(w_hi[:, s], raw[:, s], ACT.Copy), hi_ready)

            def step(s, before=None, after=None):
                act.wait_ge(unit_done, c.next(unit_done))
                if before:
                    before()
                split(s)
                if after:
                    after()

            def rms(scale):
                act.wait_ge(ss_ready, c.next(ss_ready))
                then(act.activation(acc_sq[:], ss[:], ACT.Ln, bias=eps_t[:], scale=scale), ss_free)
                then(act.activation(rstd[:], acc_sq[:], ACT.Exp, scale=-0.5), rstd_ready)

            def high_parts(n, dst):
                for k in range(n):
                    act.wait_ge(tmp_ready, c.next(tmp_ready))
                    then(act.activation(dst(k), t2[:, k % 2], ACT.Copy), hi_tile)

            def square_of_x(k, j):
                act.wait_ge(x_tile, c.next(x_tile))
                act.wait_ge(sq_free, c.next(sq_free))
                then(act.activation(t2[:, j], tile(x, k), ACT.Square), sq_ready)

            def make_u():
                rms(1.0 / D)
                high_parts(KT, lambda k: u_hi[:, k])

            c.next(ss_free)
            act.wait_ge(pool_step, 2)
            for s in range(2):
                split(s)
            act.wait_ge(angle_ready, 1)
            then(act.activation(e2[:, 1], e2[:, 0], ACT.Sin))
            then(act.activation(sin_sb[0:64], e2[0:64, 1], ACT.Copy))
            then(act.activation(sin_sb[64:128], e2[0:64, 1], ACT.Copy, scale=-1.0))
            then(act.activation(cos_sb[0:64], e2[64:128, 1], ACT.Copy))
            then(act.activation(cos_sb[64:128], e2[64:128, 1], ACT.Copy), trig_ready)
            with c.loop(act, KT // 2) as i:
                for j in range(2):
                    square_of_x(i * 2 + j, j)

            def conv_unit(s, j, p):
                def before():
                    act.wait_ge(silu_ready, c.next(silu_ready))
                    if j == 0:
                        act.wait_ge(gp_ready, c.next(gp_ready))
                    then(act.activation(t2[:, s], acc[s][:], ACT.Identity, bias=gp_half[p][:, G_BIAS + j:G_BIAS + j + 1],
                                        scale=gp_half[p][:, G_TAP + 4 * j + 3:G_TAP + 4 * j + 4]), lin_ready)

                def after():
                    act.wait_ge(conv_ready, c.next(conv_ready))
                    then(act.activation(e2[:, s], t2[:, s], ACT.Tanh), tanh_ready)
                step(s, before, after)

            def silu_unit(s):
                def before():
                    act.wait_ge(silu_ready, c.next(silu_ready))
                    then(act.activation(e2[:, s], acc[s][:], ACT.Tanh, scale=0.5), tanh_ready)
                step(s, before)

            def group_unit(j, p):
                if j < 4:
                    conv_unit(j % 2, j, p)
                else:
                    silu_unit(j % 2)

            def gate_unit(j, dst, col):
                def before():
                    act.activation(dst[:, j], acc[j % 2][:], ACT.Tanh, bias=half_gate[:, col:col + 1], scale=0.5).then_inc(acc_free[j % 2], 1)
                step(j % 2, before)

            def scan_stage(j, p, g):
                if j < NBLK:
                    act.wait_ge(row_in[j % 2], c.next(row_in[j % 2], 16))
                    if j:
                        act.wait_ge(y_blk, c.next(y_blk))
                    for h in range(HPG):
                        ins = act.activation(seg[:, h], row[:, j % 2, h], ACT.Abs, bias=tile(tok[:, 1, j:j + 1].rearrange("p a n -> p n a"), g * HPG + h))
                    then(ins)
                    then(act.activation(seg[:], seg[:], ACT.Exp, scale=-1.0), seg_ready)
                    if j:
                        then(act.activation(c_dec[:], row[:, j % 2], ACT.Exp), edec_ready)
                if j == NBLK:
                    act.wait_ge(y_blk, c.next(y_blk))
                    act.wait_ge(out_ready, c.next(out_ready))
                    for t in range(2):
                        then(act.activation(z_t[p][:, t], xs_t[p][:, t], ACT.Square), sq_ready)
                if j == NBLK + 1:
                    rms(1.0 / (SSM_INNER // GROUPS))

            def scan_out(g):
                high_parts(2, lambda t: tile(ys_hi, g * 2 + t))

            def head_unit(j, p):
                if j < 2:
                    step(j)
                elif j < 4:
                    def before():
                        then(act.activation(v_t[p][:, j - 2], acc[j % 2][:], ACT.Copy), v_ready)
                    step(j % 2, before)
                else:
                    silu_unit(j % 2)

            def head_stage(j, p):
                if j == 3:
                    act.wait_ge(head_y, c.next(head_y))
                    for t in range(2):
                        then(act.activation(v_t[p][:, t], yp[t][:], ACT.Copy), y_copied)
                        act.wait_ge(sq_free, c.next(sq_free))
                        then(act.activation(q_t[p][:] if t else k_t[p][:], v_t[p][:, t], ACT.Square), sq_ready)
                if j == 5:
                    rms(1.0 / (RET_V // RET_HEADS))

            def head_out(h):
                high_parts(2, lambda t: tile(yr_hi, h * 2 + t))

            def xa_unit(j, p):
                def before():
                    if j < 2:
                        then(act.activation(xk[p][:, j], acc[j][:, 0:MEM], ACT.Copy), xa_ready)
                    elif j < 4:
                        then(act.activation(xv[p][:, j - 2], acc[j % 2][:, 0:MEM], ACT.Copy), v_ready)
                    else:
                        then(act.activation(xq[p][:, j - 4], acc[j % 2][:], ACT.Copy, scale=(2 * P) ** -0.5), xa_ready)
                    act.sem_inc(acc_free[j % 2], 1)
                step(j % 2, before)

            def attention_stage(j):
                if j < NBLK:
                    act.wait_ge(max_ready, c.next(max_ready))
                    then(act.activation(prob[:, j % 2], pr[j % 2][:, 0:MEM], ACT.Exp,
                                        bias=small[:, j % 2:j % 2 + 1], accum_out=small[:, 2 + j % 2:3 + j % 2]), prob_raw)

            def attention_out(h):
                act.wait_ge(head_y, c.next(head_y))
                for t in range(2):
                    then(act.activation(tile(o_hi, h * 2 + t), yp[t][:], ACT.Copy), hi_tile)

            def added_units():
                with c.loop(act, KT // 2) as i:
                    for j in range(2):
                        step(j, None, lambda: square_of_x(i * 2 + j, j))

            with c.loop(act, DEPTH):
                act.wait_ge(lp_ready, c.next(lp_ready))
                then(act.activation(a_pos[:], lp[:, L_ALOG:L_ALOG + SSM_HEADS], ACT.Exp), a_ready)
                make_u()
                step(0)
                step(1)
                for j in range(6):
                    group_unit(j, 0)
                    if j == 0:
                        act.wait_ge(dt_copied, c.next(dt_copied))
                        then(act.activation(dt_w[:, 1], dt_w[:, 0], ACT.Abs))
                        then(act.activation(dt_w[:, 2], dt_w[:, 1], ACT.Exp, scale=-1.0), dt_exp)
                    if j == 2:
                        act.wait_ge(cum_ready, c.next(cum_ready))
                        then(act.activation(dt_rows_sb[:], pr[1][0:SSM_HEADS, :], ACT.Copy), cum_rows)
                        act.dma_start(cum_dram.rearrange("g h s -> (g h) s"), dt_rows_sb[:]).then_inc(cum_out, 16)
                        act.wait_ge(dec_in, c.next(dec_in))
                        then(act.activation(tok[:, 2:4], tok[:, 2:4], ACT.Exp), dec_out)
                        act.wait_ge(cum_out, c.next(cum_out, 16))
                with c.loop(act, GROUPS // 2 - 1) as i:
                    for p in range(2):
                        for j in range(6):
                            scan_stage(j, p, i * 2 + p)
                            group_unit(j, 1 - p)
                        scan_out(i * 2 + p)
                for j in range(6):
                    scan_stage(j, 0, GROUPS - 2)
                    group_unit(j, 1)
                scan_out(GROUPS - 2)
                for j in range(KT):
                    scan_stage(j, 1, GROUPS - 1)
                    gate_unit(j, merge, KT + j)
                scan_out(GROUPS - 1)
                with c.loop(act, KT):
                    step(0)
                    step(1)
                for j in range(6):
                    head_unit(j, 0)
                with c.loop(act, RET_HEADS // 2 - 1) as i:
                    for p in range(2):
                        for j in range(6):
                            head_stage(j, p)
                            head_unit(j, 1 - p)
                        head_out(i * 2 + p)
                for j in range(6):
                    head_stage(j, 0)
                    head_unit(j, 1)
                head_out(RET_HEADS - 2)
                for j in range(KT):
                    head_stage(j, 1)
                    gate_unit(j, gate_r, j)
                head_out(RET_HEADS - 1)
                act.wait_ge(mem_in, c.next(mem_in, 16))
                with c.loop(act, KT // 2) as i:
                    for j in range(2):
                        step(j)
                        act.wait_ge(tmp_ready, c.next(tmp_ready))
                        then(act.activation(tile(m_hi, i * 2 + j), t2[:, 0], ACT.Copy, scale=0.5), hi_tile)
                        act.wait_ge(mem_slot, c.next(mem_slot))
                        then(act.activation(e2[:, j, 0:MEM], tile(mem, i * 2 + j), ACT.Square), mem_sq)
                rms(1.0 / D)
                with c.loop(act, KT // 2) as i:
                    for j in range(2):
                        def after():
                            square_of_x(i * 2 + j, j)
                            act.wait_ge(mem_tmp, c.next(mem_tmp))
                            then(act.activation(tile(mem_hi, i * 2 + j), e2[:, j, 0:MEM], ACT.Copy), mem_hi_ready)
                        step(j, None, after)
                make_u()
                for j in range(6):
                    xa_unit(j, 0)
                with c.loop(act, 1) as i:
                    for p in range(2):
                        for j in range(6):
                            attention_stage(j)
                            xa_unit(j, 1 - p)
                        attention_out(i * 2 + p)
                for j in range(6):
                    attention_stage(j)
                    xa_unit(j, 1)
                attention_out(2)
                for j in range(6):
                    attention_stage(j)
                attention_out(3)
                added_units()
                make_u()

                def inner_units():
                    with c.loop(act, KT // 2) as i:
                        for j in range(2):
                            def before():
                                then(act.activation(t2[:, j], acc[j][:], ACT.Relu), relu_ready)

                            def after():
                                act.wait_ge(tmp_ready, c.next(tmp_ready))
                                then(act.activation(tile(h_hi, i * 2 + j), e2[:, j], ACT.Copy), hi_tile)
                            step(j, before, after)

                with c.loop(act, FFQ - 1):
                    inner_units()
                    with c.loop(act, KT // 2):
                        step(0)
                        step(1)
                inner_units()
                c.next(x_tile, (FFQ - 1) * KT)
                added_units()
            rms(1.0 / D)
            act.wait_ge(final_ready, 1)
            act.dma_start(a["out"], x[:]).then_inc(out_done, 16)
            act.wait_ge(out_done, 16)

        @block.vector
        def _(dve):
            c = Counts("dve", per, passed)

            def mark(ins, signal=dve_step):
                ins.then_inc(signal, 1)
                return c.next(signal)

            def then(ins, signal=dve_step):
                dve.wait_ge(signal, mark(ins, signal))

            def split(s):
                dve.wait_ge(hi_ready, c.next(hi_ready))
                then(dve.tensor_tensor(w_lo[:, s], raw[:, s], w_hi[:, s].bitcast(F32), ALU.subtract), lo_ready)

            def step(s, before=None, after=None):
                dve.wait_ge(unit_done, c.next(unit_done))
                if before:
                    before()
                split(s)
                if after:
                    after()

            def low_parts(n, make, hi, lo):
                for k in range(n + 1):
                    if k < n:
                        make(k)
                    if k:
                        dve.wait_ge(hi_tile, c.next(hi_tile))
                        then(dve.tensor_tensor(lo(k - 1), t2[:, (k - 1) % 2], hi(k - 1).bitcast(F32), ALU.subtract), pair_ready)

            def add_square(j):
                dve.wait_ge(sq_ready, c.next(sq_ready))
                then(dve.tensor_tensor(acc_sq[:], acc_sq[:], t2[:, j], ALU.add), sq_free)

            def make_u(col):
                dve.sem_inc(sum_ready, 1)
                dve.wait_ge(rstd_ready, c.next(rstd_ready))

                def make(k):
                    then(dve.scalar_tensor_tensor(t2[:, k % 2], x[:, k], lp[:, col + k:col + k + 1], rstd[:], ALU.mult, ALU.mult), tmp_ready)
                low_parts(KT, make, lambda k: u_hi[:, k], lambda k: u_lo[:, k])

            def free(bank):
                dve.sem_inc(acc_free[bank], 1)

            dve.wait_ge(angle_in, 32)
            ang, n_hi, n_lo, tmp = e2[:, 0], rstd[:], acc_sq[:], e2[:, 1]
            then(dve.tensor_copy(tmp, e2[:, 0].bitcast(I32)))
            then(dve.tensor_scalar(ang, tmp, freq[:, 0:1], None, ALU.mult))
            then(dve.tensor_scalar(tmp, ang, 1.0 / TWO_PI, freq[:, 1:2], ALU.mult, ALU.add))
            then(dve.tensor_scalar(tmp, tmp, MAGIC, None, ALU.add))
            then(dve.tensor_scalar(tmp, tmp, MAGIC, None, ALU.subtract))
            then(dve.tensor_scalar(n_hi, tmp, 4096.0 * MAGIC, None, ALU.add))
            then(dve.tensor_scalar(n_hi, n_hi, 4096.0 * MAGIC, None, ALU.subtract))
            then(dve.tensor_tensor(n_lo, tmp, n_hi, ALU.subtract))
            for n, const in ((n_hi, C1), (n_lo, C1), (n_hi, C2), (n_lo, C2), (tmp, C3)):
                then(dve.scalar_tensor_tensor(ang, n, -const, ang, ALU.mult, ALU.add))
            then(dve.tensor_scalar(ang, ang, freq[:, 2:3], None, ALU.add))
            then(dve.tensor_scalar(ang, ang, 3.1415925, -3.1415925, ALU.min, ALU.max), angle_ready)
            then(dve.memset(acc_sq[:], 0.0))
            dve.wait_ge(x_in, 32)
            for s_, n in ((x_tile, KT), (sq_free, 2), (silu_ready, 2), (ss_free, 1), (tp_free, 1), (cb_free, 1), (y_free, 1),
                          (row_free, 2), (sc_free, 2), (gp_free, 2), (lp_free, 1), (mem_slot, 2), (acc_free[0], 1), (acc_free[1], 1)):
                dve.sem_inc(s_, n)
                c.next(s_, n)
            for s in range(2):
                split(s)
            with c.loop(dve, KT // 2):
                for j in range(2):
                    add_square(j)
            dve.wait_ge(const_in, 5 * 16)
            dve.sem_inc(consts_ready, 1)
            dve.wait_ge(trig_ready, 1)

            def conv_unit(s, j, p, dst):
                def before():
                    dve.wait_ge(lin_ready, c.next(lin_ready))
                    for i in (2, 1, 0):
                        far = 3 - i
                        w = gp_half[p][:, G_TAP + 4 * j + i:G_TAP + 4 * j + i + 1]
                        then(dve.scalar_tensor_tensor(t2[:, s, far:S], acc[s][:, 0:S - far], w, t2[:, s, far:S], ALU.mult, ALU.add),
                             dve_step if i else conv_ready)
                    free(s)

                def after():
                    dve.wait_ge(tanh_ready, c.next(tanh_ready))
                    then(dve.scalar_tensor_tensor(dst, e2[:, s], 1.0, t2[:, s], ALU.add, ALU.mult), silu_ready)
                step(s, before, after)

            def silu_unit(s, dst):
                def after():
                    dve.wait_ge(tanh_ready, c.next(tanh_ready))
                    then(dve.scalar_tensor_tensor(dst, e2[:, s], 1.0, acc[s][:], ALU.add, ALU.mult), silu_ready)
                    free(s)
                step(s, None, after)

            def group_unit(j, p):
                if j == 0:
                    dve.wait_ge(gp_in[p], c.next(gp_in[p], 16))
                    then(dve.tensor_scalar(gp_half[p][:], gp[p][:, 0:G_SKIP], 0.5, None, ALU.mult), gp_ready)
                if j < 4:
                    conv_unit(j % 2, j, p, (b_t[p][:], c_t[p][:], xs_t[p][:, 0], xs_t[p][:, 1])[j])
                else:
                    silu_unit(j % 2, z_t[p][:, j - 4])

            def scan_stage(j, p, g):
                def heads(kind, b, n):
                    return tok[:, kind, b, bass.ds(g * HPG, HPG)].unsqueeze(2).broadcast_to([P, HPG, n])

                if 1 <= j < NBLK:
                    b = j - 1
                    new = pr[1][:, 0:HPG * HD].rearrange("p (h d) -> p h d", h=HPG)
                    if b:
                        dve.wait_ge(y_blk, c.next(y_blk))
                        then(dve.tensor_tensor(state[:], state[:], heads(3, b, HD), ALU.mult))
                        dve.wait_ge(st_sum, c.next(st_sum))
                        mark(dve.tensor_tensor(state[:], state[:], new, ALU.add), st_ready)
                    else:
                        dve.wait_ge(y_blk, c.next(y_blk))
                        dve.wait_ge(st_sum, c.next(st_sum))
                        mark(dve.tensor_copy(state[:], new), st_ready)
                if j < NBLK:
                    b = j
                    at = slice(b * P, (b + 1) * P)
                    dve.wait_ge(turned, c.next(turned))
                    weighted = mark(dve.tensor_tensor(xdt[:], tp[:, P:3 * P].rearrange("p (h d) -> p h d", h=HPG), heads(0, b, HD), ALU.mult))
                    then(dve.tensor_copy(b_tok[:], tp[:, 0:P]), tp_free)
                    dve.wait_ge(cb_ready, c.next(cb_ready))
                    mark(dve.tensor_tensor(cb_m[:], pr[0][:, 0:P], mask[:], ALU.mult), cb_free)
                    if b < NBLK - 1:
                        dve.wait_ge(dve_step, weighted)
                        mark(dve.tensor_tensor(xdt_dec[:], xdt[:], heads(2, b, HD), ALU.mult), dec_ready)
                    dve.wait_ge(cb_free, c.now(cb_free))
                    dve.wait_ge(seg_ready, c.next(seg_ready))
                    then(dve.tensor_tensor(seg[:], seg[:], cb_m[:].unsqueeze(1).broadcast_to([P, HPG, P]), ALU.mult), blk_ready)
                    if b:
                        dve.wait_ge(edec_ready, c.next(edec_ready))
                        then(dve.tensor_tensor(c_dec[:], c_dec[:], c_t[p][:, at].unsqueeze(1).broadcast_to([P, HPG, P]), ALU.mult), cdec_ready)
                    dve.sem_inc(row_free, 1)
                if j == NBLK:
                    dve.wait_ge(y_blk, c.next(y_blk, 1))
                    for t in range(2):
                        then(dve.scalar_tensor_tensor(xs_t[p][:, t], xs_t[p][:, t], gp[p][:, G_SKIP + t:G_SKIP + t + 1], yp[t][:], ALU.mult, ALU.add))
                        then(dve.scalar_tensor_tensor(xs_t[p][:, t], xs_t[p][:, t], 0.5, z_t[p][:, t], ALU.mult, ALU.mult),
                             (out_ready if t else y_free))
                    dve.wait_ge(sq_ready, c.next(sq_ready, 2))
                    then(dve.tensor_tensor(acc_sq[:], z_t[p][:, 0], z_t[p][:, 1], ALU.add), sum_ready)

            def scan_out(p, g):
                dve.wait_ge(rstd_ready, c.next(rstd_ready))

                def make(t):
                    then(dve.scalar_tensor_tensor(t2[:, t], xs_t[p][:, t], gp[p][:, G_NORM + t:G_NORM + t + 1], rstd[:], ALU.mult, ALU.mult), tmp_ready)
                low_parts(2, make, lambda t: tile(ys_hi, g * 2 + t), lambda t: tile(ys_lo, g * 2 + t))
                dve.sem_inc(gp_free, 1)

            def head_unit(j, p):
                if j < 2:
                    dst = (q_t, k_t)[j][p]

                    def before():
                        mark(dve.tensor_tensor(dst[:], acc[j][:], cos_sb[:], ALU.mult))
                        mark(dve.tensor_tensor(t2[64:128, j], acc[j][0:64], sin_sb[0:64], ALU.mult))
                        then(dve.tensor_tensor(t2[0:64, j], acc[j][64:128], sin_sb[64:128], ALU.mult))
                        free(j)
                        then(dve.tensor_tensor(dst[:], dst[:], t2[:, j], ALU.add), q_ready)
                    step(j, before)
                elif j < 4:
                    step(j % 2)
                    dve.wait_ge(v_ready, c.next(v_ready))
                    free(j % 2)
                else:
                    silu_unit(j % 2, g_t[p][:, j - 4])

            def head_stage(j, p, h):
                if j < 2:
                    dve.wait_ge(turned, c.next(turned))
                    then(dve.tensor_copy(v_tok[:, :, j * P:(j + 1) * P], tp[:].rearrange("p (b e) -> p b e", b=NBLK)), vtok_ready)
                    dve.sem_inc(tp_free, 1)
                    for i in (2 * j, 2 * j + 1):
                        n = S - i * P
                        dve.wait_ge(sc_ready, c.next(sc_ready))
                        then(dve.tensor_tensor(score[i][:], pr[i % 2][:, 0:n], decay[:, bass.ds(h, 1), 0:n].rearrange("p a s -> p (a s)"), ALU.mult), sc_done)
                        dve.sem_inc(sc_free, 1)
                if j == 3:
                    dve.wait_ge(y_copied, c.next(y_copied, 2))
                    dve.sem_inc(y_free, 1)
                    dve.wait_ge(sq_ready, c.next(sq_ready, 2))
                    then(dve.tensor_tensor(acc_sq[:], k_t[p][:], q_t[p][:], ALU.add), sum_ready)
                    dve.sem_inc(sq_free, 2)
                    c.next(sq_free, 2)

            def head_out(p, h):
                dve.wait_ge(rstd_ready, c.next(rstd_ready))

                def make(t):
                    then(dve.scalar_tensor_tensor(t2[:, t], v_t[p][:, t], 0.5, rstd[:], ALU.mult, ALU.mult))
                    then(dve.tensor_tensor(t2[:, t], t2[:, t], g_t[p][:, t], ALU.mult), tmp_ready)
                low_parts(2, make, lambda t: tile(yr_hi, h * 2 + t), lambda t: tile(yr_lo, h * 2 + t))

            def attention_stage(j):
                if j < 2:
                    dve.wait_ge(turned, c.next(turned))
                    then(dve.tensor_copy(xv_tok[:, :, j * P:(j + 1) * P], tp[:, 0:2 * P].rearrange("p (m e) -> p m e", m=2)), vtok_ready)
                    dve.sem_inc(tp_free, 1)
                if 1 <= j <= NBLK:
                    i = (j - 1) % 2
                    dve.wait_ge(prob_raw, c.next(prob_raw))
                    dve.sem_inc(sc_free, 1)
                    then(dve.reciprocal(small[:, 5:6], small[:, 2 + i:3 + i]))
                    mark(dve.tensor_scalar(prob[:, i], prob[:, i], small[:, 5:6], None, ALU.mult), prob_ready)
                if j < NBLK:
                    dve.wait_ge(sc_ready, c.next(sc_ready))
                    then(dve.tensor_reduce(small[:, 4:5], pr[j % 2][:, 0:MEM], AX, ALU.max))
                    if j >= 2:
                        dve.wait_ge(turned, c.next(turned))
                    then(dve.tensor_scalar(small[:, j % 2:j % 2 + 1], small[:, 4:5], -1.0, None, ALU.mult), max_ready)
                if 2 <= j < NBLK + 2:
                    if j >= NBLK:
                        dve.wait_ge(turned, c.next(turned))
                    then(dve.tensor_copy(prob_t[:, :, (j - 2) * P:(j - 1) * P], tp[:, 0:2 * P].rearrange("p (m s) -> p m s", m=2)), probt_ready)
                    dve.sem_inc(tp_free, 1)

            def attention_out(h):
                for t in range(2):
                    dve.wait_ge(hi_tile, c.next(hi_tile))
                    then(dve.tensor_tensor(tile(o_lo, h * 2 + t), yp[t][:], tile(o_hi, h * 2 + t).bitcast(F32), ALU.subtract), pair_ready)
                dve.sem_inc(y_free, 1)

            def add_units(squares):
                if squares:
                    then(dve.memset(acc_sq[:], 0.0))
                with c.loop(dve, KT // 2) as i:
                    for j in range(2):
                        def before():
                            then(dve.tensor_tensor(tile(x, i * 2 + j), tile(x, i * 2 + j), acc[j][:], ALU.add), x_tile)
                            free(j)
                        step(j, before, (lambda: add_square(j)) if squares else None)

            with c.loop(dve, DEPTH):
                dve.wait_ge(lp_in, c.next(lp_in, 16))
                then(dve.tensor_scalar(half_gate[:], lp[:, L_GATE:L_GATE + 2 * KT], 0.5, None, ALU.mult), lp_ready)
                make_u(L_MIX)

                def dt_part():
                    then(dve.tensor_scalar(dt_v[:], acc[0][0:SSM_HEADS, :], lp[0:SSM_HEADS, L_DTB:L_DTB + 1], None, ALU.add), dt_in)
                    free(0)
                step(0, dt_part)
                step(1, lambda: free(1))
                v, e, s1, s2, p_, dta = dt_w[:, 0], dt_w[:, 2], dt_w[:, 3], dt_w[:, 1], dt_w[:, 4], dt_w[:, 4]
                by_head = lambda t: t.rearrange("p (b h) -> p b h", b=NBLK)
                flat = lambda t: t.rearrange("p b h -> p (b h)")
                for j in range(6):
                    if j == 1:
                        dve.wait_ge(dt_turned, c.next(dt_turned))
                        then(dve.tensor_copy(v, tp[:, 0:P]), dt_copied)
                        dve.sem_inc(tp_free, 1)
                        c.next(tp_free)
                    group_unit(j, 0)
                    if j == 1:
                        dve.wait_ge(dt_exp, c.next(dt_exp))
                        then(dve.tensor_scalar(s2, e, 2.0, None, ALU.add))
                        then(dve.reciprocal(s1, s2))
                        then(dve.tensor_tensor(s1, s1, e, ALU.mult))
                        then(dve.tensor_tensor(s2, s1, s1, ALU.mult))
                        then(dve.tensor_scalar(p_, s2, 1.0 / 15, None, ALU.mult))
                        for n in (13, 11, 9, 7, 5, 3):
                            then(dve.scalar_tensor_tensor(p_, p_, 1.0 / n, s2, ALU.add, ALU.mult))
                        then(dve.scalar_tensor_tensor(p_, p_, 1.0, s1, ALU.add, ALU.mult))
                        then(dve.tensor_scalar(v, v, 0.0, None, ALU.max))
                        then(dve.scalar_tensor_tensor(flat(tok[:, 0]), p_, 2.0, v, ALU.mult, ALU.add))
                        dve.wait_ge(a_ready, c.next(a_ready))
                        then(dve.scalar_tensor_tensor(by_head(dta), tok[:, 0], -1.0,
                                                      a_pos[:].unsqueeze(1).broadcast_to([P, NBLK, SSM_HEADS]), ALU.mult, ALU.mult), dta_ready)
                    if j == 2:
                        dve.wait_ge(cum_ready, c.next(cum_ready))
                        then(dve.tensor_scalar(flat(tok[:, 1]), pr[0][:, 0:P], -1.0, None, ALU.mult))
                        mark(dve.tensor_tensor(flat(tok[:, 2]), pr[0][:, P:2 * P], flat(tok[:, 1]), ALU.add))
                        then(dve.tensor_copy(flat(tok[:, 3]), pr[0][:, P:2 * P]), dec_in)
                dve.wait_ge(dec_out, c.next(dec_out))
                dve.wait_ge(cum_rows, c.next(cum_rows))
                with c.loop(dve, GROUPS // 2 - 1) as i:
                    for p in range(2):
                        for j in range(6):
                            scan_stage(j, p, i * 2 + p)
                            group_unit(j, 1 - p)
                        scan_out(p, i * 2 + p)
                for j in range(6):
                    scan_stage(j, 0, GROUPS - 2)
                    group_unit(j, 1)
                scan_out(0, GROUPS - 2)
                for j in range(KT):
                    scan_stage(j, 1, GROUPS - 1)
                    step(j % 2)
                scan_out(1, GROUPS - 1)
                with c.loop(dve, KT // 2) as i:
                    for j in range(2):
                        step(0)

                        def before():
                            then(dve.scalar_tensor_tensor(tile(merge, i * 2 + j), tile(merge, i * 2 + j), 1.0, acc[j][:], ALU.add, ALU.mult))
                            free(j)
                        step(1, before)
                dve.sem_inc(mem_free, 1)
                for j in range(6):
                    head_unit(j, 0)
                with c.loop(dve, RET_HEADS // 2 - 1) as i:
                    for p in range(2):
                        for j in range(6):
                            head_stage(j, p, i * 2 + p)
                            head_unit(j, 1 - p)
                        head_out(p, i * 2 + p)
                for j in range(6):
                    head_stage(j, 0, RET_HEADS - 2)
                    head_unit(j, 1)
                head_out(0, RET_HEADS - 2)
                for j in range(KT):
                    head_stage(j, 1, RET_HEADS - 1)
                    step(j % 2)
                head_out(1, RET_HEADS - 1)
                then(dve.memset(acc_sq[:], 0.0))
                with c.loop(dve, KT // 2) as i:
                    for j in range(2):
                        def before():
                            then(dve.scalar_tensor_tensor(t2[:, 1], tile(gate_r, i * 2 + j), 1.0, acc[j][:], ALU.add, ALU.mult))
                            free(j)
                            then(dve.tensor_tensor(t2[:, 0], t2[:, 1], tile(merge, i * 2 + j), ALU.add), tmp_ready)

                        def after():
                            dve.wait_ge(hi_tile, c.next(hi_tile))
                            then(dve.scalar_tensor_tensor(tile(m_lo, i * 2 + j), t2[:, 0], 0.5, tile(m_hi, i * 2 + j).bitcast(F32),
                                                          ALU.mult, ALU.subtract), pair_ready)
                            dve.wait_ge(mem_sq, c.next(mem_sq))
                            then(dve.tensor_tensor(acc_sq[:, 0:MEM], acc_sq[:, 0:MEM], e2[:, j, 0:MEM], ALU.add), mem_slot)
                        step(j, before, after)
                dve.sem_inc(sum_ready, 1)
                dve.wait_ge(rstd_ready, c.next(rstd_ready))
                then(dve.memset(acc_sq[:], 0.0))
                with c.loop(dve, KT // 2) as i:
                    for j in range(2):
                        def before():
                            then(dve.tensor_tensor(tile(x, i * 2 + j), tile(x, i * 2 + j), acc[j][:], ALU.add), x_tile)
                            free(j)
                            then(dve.scalar_tensor_tensor(e2[:, j, 0:MEM], tile(mem, i * 2 + j), lp[:, bass.ds(i * 2 + (L_MEM + j), 1)],
                                                          rstd[:, 0:MEM], ALU.mult, ALU.mult), mem_tmp)

                        def after():
                            add_square(j)
                            dve.wait_ge(mem_hi_ready, c.next(mem_hi_ready))
                            then(dve.tensor_tensor(tile(mem_lo, i * 2 + j), e2[:, j, 0:MEM], tile(mem_hi, i * 2 + j).bitcast(F32), ALU.subtract), mem_tile)
                        step(j, before, after)
                make_u(L_XA)
                for j in range(6):
                    step(j % 2)
                with c.loop(dve, 1) as i:
                    for p in range(2):
                        for j in range(6):
                            attention_stage(j)
                            step(j % 2)
                        attention_out(i * 2 + p)
                for j in range(6):
                    attention_stage(j)
                    step(j % 2)
                attention_out(2)
                for j in range(6):
                    attention_stage(j)
                attention_out(3)
                add_units(True)
                make_u(L_MLP)
                dve.sem_inc(lp_free, 1)

                def inner_units():
                    with c.loop(dve, KT // 2) as i:
                        for j in range(2):
                            def before():
                                dve.wait_ge(relu_ready, c.next(relu_ready))
                                free(j)
                                then(dve.tensor_tensor(e2[:, j], t2[:, j], t2[:, j], ALU.mult), tmp_ready)

                            def after():
                                dve.wait_ge(hi_tile, c.next(hi_tile))
                                then(dve.tensor_tensor(tile(h_lo, i * 2 + j), e2[:, j], tile(h_hi, i * 2 + j).bitcast(F32), ALU.subtract), pair_ready)
                            step(j, before, after)

                with c.loop(dve, FFQ - 1):
                    inner_units()
                    add_units(False)
                inner_units()
                add_units(True)
            dve.sem_inc(sum_ready, 1)
            dve.wait_ge(rstd_ready, c.next(rstd_ready))
            for k in range(KT):
                then(dve.scalar_tensor_tensor(x[:, k], x[:, k], fin_w[:, k:k + 1], rstd[:], ALU.mult, ALU.mult))
            dve.sem_inc(final_ready, 1)


def _layout(x, mem, positions, norm_mix, w_in, b_gate, conv_w, conv_b, dt_bias, a_log, d_skip, ssm_norm,
            w_br_ret, w_br_ssm, w_out, norm_xa, norm_mem, xa_wq, xa_wkv, xa_wo, norm_mlp, mlp_w1, mlp_w2, norm_final):
    f = np.float32

    def units(w):
        r, n = w.shape
        return w.reshape(r // D, KT, P, n // P, P).transpose(3, 0, 2, 1, 4)

    stream = np.zeros((DEPTH * UNITS + AHEAD, P, KT, P), f)
    lps = np.zeros((DEPTH, P, LPN), f)
    gps = np.zeros((DEPTH * GROUPS, P, GPN), f)

    def cols(v):
        return v.reshape(-1, P).T

    for l in range(DEPTH):
        at = l * UNITS

        def put(u, at):
            stream[at:at + len(u)] = u
            return at + len(u)

        wi = w_in[l]
        stream[at, :, :, 0:SSM_HEADS] = wi[:, O_DT:O_DT + SSM_HEADS].reshape(KT, P, SSM_HEADS).transpose(1, 0, 2)
        at += 2

        def part(o, n):
            return units(wi[:, o:o + n * P])[:, 0]

        for g in range(GROUPS):
            for o, n in ((O_B + g * P, 1), (O_C + g * P, 1), (O_XS + g * 2 * P, 2), (O_Z + g * 2 * P, 2)):
                at = put(part(o, n), at)
        br, gates = units(w_br_ssm[l]), part(O_GATE, 2 * KT)
        at = put(gates[KT:2 * KT], at)
        for n in range(KT):
            at = put(br[n], at)
        for h in range(RET_HEADS):
            for o, n in ((O_Q + h * P, 1), (O_K + h * P, 1), (O_V + h * 2 * P, 2), (O_G + h * 2 * P, 2)):
                at = put(part(o, n), at)
        at = put(gates[0:KT], at)
        at = put(units(w_br_ret[l])[:, 0], at)
        at = put(units(w_out[l])[:, 0], at)
        q, kv = units(xa_wq[l])[:, 0], units(xa_wkv[l])[:, 0]
        for h in range(4):
            at = put(kv[2 * h:2 * h + 2], at)
            at = put(kv[KT + 2 * h:KT + 2 * h + 2], at)
            at = put(q[2 * h:2 * h + 2], at)
        at = put(units(xa_wo[l])[:, 0], at)
        w1, w2 = units(mlp_w1[l])[:, 0], units(mlp_w2[l])
        for q4 in range(FFQ):
            at = put(w1[q4 * KT:(q4 + 1) * KT], at)
            at = put(w2[:, q4], at)
        assert at == (l + 1) * UNITS

        for o, v in ((L_MIX, norm_mix), (L_XA, norm_xa), (L_MEM, norm_mem), (L_MLP, norm_mlp), (L_GATE, b_gate)):
            lps[l, :, o:o + v.shape[1] // P] = cols(v[l])
        lps[l, :, L_ALOG:L_ALOG + SSM_HEADS] = a_log[l][None, :]
        lps[l, 0:SSM_HEADS, L_DTB] = dt_bias[l]
        skip = np.repeat(d_skip[l], HD)
        for g in range(GROUPS):
            gpt = gps[l * GROUPS + g]
            for j, o in enumerate((SSM_INNER + g * P, SSM_INNER + BC + g * P, g * 2 * P, g * 2 * P + P)):
                gpt[:, G_TAP + 4 * j:G_TAP + 4 * j + 4] = conv_w[l][:, o:o + P].T
                gpt[:, G_BIAS + j] = conv_b[l][o:o + P]
            gpt[:, G_SKIP:G_SKIP + 2] = cols(skip[g * 2 * P:(g + 1) * 2 * P])
            gpt[:, G_NORM:G_NORM + 2] = cols(ssm_norm[l][g * 2 * P:(g + 1) * 2 * P])

    i = np.arange(P)
    upto = (i[:, None] <= i[None, :]).astype(f)
    mask = (i[:, None] // CHUNK <= i[None, :] // CHUNK).astype(f)
    lg = np.log1p(-(2.0 ** (-5.0 - np.arange(RET_HEADS))))
    m, l_ = np.arange(P)[:, None], np.arange(S)[None, :]
    decay = np.exp(lg[None, :, None] * np.abs(l_ - m)[:, None, :]) * (m // CHUNK <= l_ // CHUNK)[:, None, :] * P ** -0.5
    freq = np.zeros((P, 4), f)
    freq[:, 0] = np.tile(10000.0 ** (-np.arange(0, P, 2) / P), 2)
    freq[64:, 1] = 0.25
    freq[64:, 2] = np.pi / 2
    return {
        "stream": stream, "lp": lps, "gp": gps,
        "x": np.ascontiguousarray(x[0].T.reshape(KT, P, S).transpose(1, 0, 2)),
        "mem": np.ascontiguousarray(mem[0].T.reshape(KT, P, MEM).transpose(1, 0, 2)),
        "pos": np.ascontiguousarray(positions[0]),
        "fin_w": np.ascontiguousarray(cols(norm_final)),
        "ident": np.eye(P, dtype=f), "upto": upto, "mask": mask,
        "decay": decay.astype(f), "freq": freq,
    }


def kernel(**inputs):
    import concourse.bacc as bacc
    from concourse.bass_utils import run_bass_kernel_spmd

    arrays = _layout(**{k: np.asarray(v) for k, v in inputs.items()})

    def build(per):
        nc = bacc.Bacc("TRN2", target_bir_lowering=False, num_devices=1)
        a = {n: nc.dram_tensor(f"in_{n}", v.shape, mybir.dt.from_np(v.dtype), kind="ExternalInput").ap() for n, v in arrays.items()}
        a["out"] = nc.dram_tensor("out_0", [P, KT, S], F32, kind="ExternalOutput").ap()
        program(nc, a, per)
        return nc

    per = {}
    build(per)
    nc = build(per)
    r = run_bass_kernel_spmd(nc, [{f"in_{n}": v for n, v in arrays.items()}], core_ids=[0])
    out = r.results[0]["out_0"]
    return np.ascontiguousarray(out.transpose(1, 0, 2).reshape(D, S).T)[None]
```

```python
from contextlib import ExitStack, contextmanager

import numpy as np

import concourse.bass as bass
from concourse import mybir

F32 = mybir.dt.float32
F32R = mybir.dt.float32r
I32 = mybir.dt.int32
ALU = mybir.AluOpType
ACT = mybir.ActivationFunctionType
AX = mybir.AxisListType.X

P = 128
D = 1024
S = 512
KT = D // P
DEPTH = 2
MEM = 256
CHUNK = 64
NBLK = S // P
EPS = 1e-6
RET_HEADS = 4
RET_QK = 512
RET_V = 1024
SSM_INNER = 2048
SSM_HEADS = 32
GROUPS = 8
HPG = SSM_HEADS // GROUPS
HD = SSM_INNER // SSM_HEADS
BC = 1024
D_FF = 4096
FFQ = D_FF // D

O_Q = 0
O_K = O_Q + RET_QK
O_V = O_K + RET_QK
O_G = O_V + RET_V
O_Z = O_G + RET_V
O_XS = O_Z + SSM_INNER
O_B = O_XS + SSM_INNER
O_C = O_B + BC
O_DT = O_C + BC
O_GATE = O_DT + SSM_HEADS

UNITS = 2 + GROUPS * 6 + KT * 3 + RET_HEADS * 6 + KT * 2 + KT + 4 * 6 + KT + FFQ * 2 * KT
AHEAD = 2

L_MIX, L_XA, L_MEM, L_MLP, L_GATE, L_ALOG, L_DTB = 0, 8, 16, 24, 32, 48, 80
LPN = 81
G_TAP, G_BIAS, G_SKIP, G_NORM = 0, 16, 20, 22
GPN = 24
PARN = LPN + GROUPS * GPN

TWO_PI = 2 * np.pi
C1 = 6.28125
C2 = float(np.float32(np.round((TWO_PI - C1) * 2**21) / 2**21))
C3 = float(np.float32(TWO_PI - C1 - C2))
MAGIC = 1.5 * 2.0**23


class Counts:

    def __init__(self, engine, per, always):
        self.engine, self.per, self.always = engine, per, always
        self.n, self.active, self.loops = {}, [], 0

    def now(self, sem):
        value = self.n.get(sem.name, 0)
        for index, counts in self.active:
            if counts.get(sem.name, 0):
                value = index * counts[sem.name] + value
        return value

    def next(self, sem, by=1):
        self.n[sem.name] = self.n.get(sem.name, 0) + by
        return self.now(sem)

    @contextmanager
    def loop(self, eng, times):
        self.loops += 1
        label = (self.engine, self.loops)
        before = dict(self.n)
        if self.active:
            eng.sem_inc(self.always, 1)
        with eng.Fori(0, times) as index:
            self.active.append((index, self.per.get(label, {})))
            yield index
            self.active.pop()
        once = {s: v - before.get(s, 0) for s, v in self.n.items()}
        self.per[label] = once
        self.n = {s: before.get(s, 0) + times * v for s, v in once.items()}


def program(nc, a, per):
    with ExitStack() as ctx:
        def sb(name, shape, dt=F32, stack=ctx):
            return stack.enter_context(nc.sbuf_tensor(name, shape, dt))

        def sem(name):
            return ctx.enter_context(nc.semaphore(name))

        x = sb("x", [P, KT, S])
        u_hi, u_lo = sb("u_hi", [P, KT, S], F32R), sb("u_lo", [P, KT, S], F32R)
        raw = sb("raw", [P, 2, KT, P])
        w_hi, w_lo = sb("w_hi", [P, 2, KT, P], F32R), sb("w_lo", [P, 2, KT, P], F32R)
        cos_sb, sin_sb = sb("cos_sb", [P, S]), sb("sin_sb", [P, S])
        decay = sb("decay", [P, RET_HEADS, S])
        ident, upto, mask = sb("ident", [P, P]), sb("upto", [P, P]), sb("mask", [P, P])
        ones = sb("ones", [P, P])
        eps_t = sb("eps_t", [P, 1])
        par = sb("par", [P, DEPTH * PARN])
        fin_w = sb("fin_w", [P, KT])
        half_gate = sb("half_gate", [P, 2 * KT])
        a_pos = sb("a_pos", [P, SSM_HEADS])
        gp = [sb(f"gp{i}", [P, GPN]) for i in range(2)]
        gp_half = [sb(f"gp_half{i}", [P, G_SKIP]) for i in range(2)]
        freq = sb("freq", [P, 4])
        t2, e2 = sb("t2", [P, 2, S]), sb("e2", [P, 2, S])
        rstd, acc_sq = sb("rstd", [P, S]), sb("acc_sq", [P, S])
        tok = sb("tok", [P, 4, NBLK, SSM_HEADS])
        small = sb("small", [P, 8])
        log_warm = sb("log_warm", [P, 1])

        with ExitStack() as ssm:
            b_t, c_t, xs_t, z_t = {}, {}, {}, {}

            def group_buffer(p):
                b_t[p], c_t[p] = sb(f"b_t{p}", [P, S], F32, ssm), sb(f"c_t{p}", [P, S], F32, ssm)
                xs_t[p], z_t[p] = sb(f"xs_t{p}", [P, 2, S], F32, ssm), sb(f"z_t{p}", [P, 2, S], F32, ssm)

            group_buffer(0)
            sb("under_merge", [P, 4 * 256], F32, ssm)
            group_buffer(1)
            b_tok = sb("b_tok", [P, P], F32, ssm)
            xdt, xdt_dec = sb("xdt", [P, HPG, HD], F32, ssm), sb("xdt_dec", [P, HPG, HD], F32, ssm)
            row = sb("row", [P, 2, HPG, P], F32, ssm)
            seg, c_dec = sb("seg", [P, HPG, P], F32, ssm), sb("c_dec", [P, HPG, P], F32, ssm)
            cb_m = sb("cb_m", [P, P], F32, ssm)
            state = sb("state", [P, HPG, HD], F32, ssm)
            with ExitStack() as early:
                dt_v, dt_rows_sb = sb("dt_v", [SSM_HEADS, S], F32, early), sb("dt_rows_sb", [SSM_HEADS, S], F32, early)
                dt_w = sb("dt_w", [P, 5, P], F32, early)
            ys_hi, ys_lo = sb("ys_hi", [P, 2 * KT, S], F32R, ssm), sb("ys_lo", [P, 2 * KT, S], F32R, ssm)
        with ExitStack() as mix:
            merge = sb("merge", [P, KT, S], F32, mix)
            yr_hi, yr_lo = sb("yr_hi", [P, KT, S], F32R, mix), sb("yr_lo", [P, KT, S], F32R, mix)
            with ExitStack() as ret:
                q_t, k_t, v_t, g_t = {}, {}, {}, {}

                def head_buffer(p):
                    q_t[p], k_t[p] = sb(f"q_t{p}", [P, S], F32, ret), sb(f"k_t{p}", [P, S], F32, ret)
                    v_t[p], g_t[p] = sb(f"v_t{p}", [P, 2, S], F32, ret), sb(f"g_t{p}", [P, 2, S], F32, ret)

                head_buffer(0)
                sb("under_gate", [P, 4 * 256], F32, ret)
                head_buffer(1)
                v_tok = sb("v_tok", [P, NBLK, 2 * P], F32, ret)
                score = [sb(f"score{i}", [P, S - i * P], F32, ret) for i in range(NBLK)]
            gate_r = sb("gate_r", [P, KT, S], F32, mix)
            m_hi, m_lo = sb("m_hi", [P, KT, S], F32R, mix), sb("m_lo", [P, KT, S], F32R, mix)
            mem = sb("mem_t", [P, KT, MEM], F32, mix)
        with ExitStack() as xa:
            mem_hi, mem_lo = sb("mem_hi", [P, KT, MEM], F32R, xa), sb("mem_lo", [P, KT, MEM], F32R, xa)
            o_hi, o_lo = sb("o_hi", [P, KT, S], F32R, xa), sb("o_lo", [P, KT, S], F32R, xa)
            sb("under_m", [P, 16 * 256], F32, xa)
            xk, xv = [sb(f"xk{p}", [P, 2, MEM], F32, xa) for p in range(2)], [sb(f"xv{p}", [P, 2, MEM], F32, xa) for p in range(2)]
            xq = [sb(f"xq{p}", [P, 2, S], F32, xa) for p in range(2)]
            xv_tok = sb("xv_tok", [P, 2, 2 * P], F32, xa)
            prob = sb("prob", [P, 2, MEM], F32, xa)
            prob_t = sb("prob_t", [P, 2, S], F32, xa)
        h_hi, h_lo = sb("h_hi", [P, KT, S], F32R), sb("h_lo", [P, KT, S], F32R)

        acc = [ctx.enter_context(nc.psum_tensor(f"acc{i}", [P, S], F32)) for i in range(2)]
        tp = ctx.enter_context(nc.psum_tensor("tp", [P, S], F32))
        pr = [ctx.enter_context(nc.psum_tensor(f"pr{i}", [P, S], F32)) for i in range(2)]
        yp = [ctx.enter_context(nc.psum_tensor(f"yp{i}", [P, S], F32)) for i in range(2)]
        ss = ctx.enter_context(nc.psum_tensor("ss", [P, S], F32))
        cum_dram = nc.dram_tensor("cum_scratch", [GROUPS, HPG, S], F32, kind="Internal").ap()

        passed = sem("passed")
        const_in, angle_in, pos_in = sem("const_in"), sem("angle_in"), sem("pos_in")
        x_in, mem_in, decay_in = [sem(f"x_in{n}") for n in range(KT // 2)], sem("mem_in"), sem("decay_in")
        par_in = sem("par_in")
        raw_in = [sem("raw_in0"), sem("raw_in1")]
        hi_ready, lo_ready, unit_done = sem("hi_ready"), sem("lo_ready"), sem("unit_done")
        acc_free = [sem("acc_free0"), sem("acc_free1")]
        dve_step, act_step, pool_step = sem("dve_step"), sem("act_step"), sem("pool_step")
        x_tile = sem("x_tile")
        sq_ready, sq_free, sum_ready = sem("sq_ready"), sem("sq_free"), sem("sum_ready")
        ss_ready, ss_free, rstd_ready = sem("ss_ready"), sem("ss_free"), sem("rstd_ready")
        tmp_ready, hi_tile, pair_ready = sem("tmp_ready"), sem("hi_tile"), sem("pair_ready")
        angle_ready, trig_ready = sem("angle_ready"), sem("trig_ready")
        half_ready, a_ready, gp_ready = sem("half_ready"), sem("a_ready"), sem("gp_ready")
        dt_in, dt_turned, dt_copied, dt_exp = sem("dt_in"), sem("dt_turned"), sem("dt_copied"), sem("dt_exp")
        dta_ready, cum_ready, dec_in, dec_out = sem("dta_ready"), sem("cum_ready"), sem("dec_in"), sem("dec_out")
        cum_rows, cum_out = sem("cum_rows"), sem("cum_out")
        row_in = [sem("row_in0"), sem("row_in1")]
        lin_ready, conv_ready, tanh_ready, silu_ready = sem("lin_ready"), sem("conv_ready"), sem("tanh_ready"), sem("silu_ready")
        turned, tp_free = sem("turned"), sem("tp_free")
        cb_ready, cb_free = sem("cb_ready"), sem("cb_free")
        seg_ready, edec_ready, cdec_ready = sem("seg_ready"), sem("edec_ready"), sem("cdec_ready")
        blk_ready, y_blk = sem("blk_ready"), sem("y_blk")
        dec_ready, st_sum, st_ready = sem("dec_ready"), sem("st_sum"), sem("st_ready")
        y_free, out_ready = sem("y_free"), sem("out_ready")
        v_ready, sc_ready, sc_free, sc_done = sem("v_ready"), sem("sc_ready"), sem("sc_free"), sem("sc_done")
        vtok_ready, head_y, y_copied = sem("vtok_ready"), sem("head_y"), sem("y_copied")
        q_ready, xa_ready = sem("q_ready"), sem("xa_ready")
        max_ready, prob_raw, prob_ready = sem("max_ready"), sem("prob_raw"), sem("prob_ready")
        probt_ready = sem("probt_ready")
        relu_ready = sem("relu_ready")
        mem_sq, mem_tmp, mem_hi_ready, mem_tile, mem_slot = sem("mem_sq"), sem("mem_tmp"), sem("mem_hi_ready"), sem("mem_tile"), sem("mem_slot")
        final_ready, out_done = sem("final_ready"), sem("out_done")

        def u_slot(k):
            return (t2 if k % 4 < 2 else e2)[:, k % 2]

        def layer_par(l, col, n=1, rows=slice(None)):
            return par[rows, bass.ds(l * PARN + col, n)]

        def tile(t, n):
            return t[:, bass.ds(n, 1)].rearrange("p a s -> p (a s)")

        block = ctx.enter_context(nc.Block())

        @block.sync
        def _(sp):
            for n in range(KT // 2):
                sp.dma_start(x[:, 2 * n:2 * n + 2], a["x"][:, 2 * n:2 * n + 2]).then_inc(x_in[n], 16)
            for s in range(2):
                sp.dma_start(raw[:, s], a["stream"][s]).then_inc(raw_in[s], 16)
            sp.dma_start(par[:], a["par"]).then_inc(par_in, 16)
            sp.dma_start(freq[:], a["freq"]).then_inc(angle_in, 16)
            for name, t in (("ident", ident), ("upto", upto), ("mask", mask), ("fin_w", fin_w)):
                sp.dma_start(t[:], a[name]).then_inc(const_in, 16)
            with sp.Fori(1, (DEPTH * UNITS + AHEAD) // 2) as i:
                for s in range(2):
                    sp.wait_ge(lo_ready, i * 2 + (s - 1))
                    sp.dma_start(raw[:, s], a["stream"][bass.ds(i * 2 + s, 1)].rearrange("a p k c -> p (a k) c")).then_inc(raw_in[s], 16)

        @block.gpsimd
        def _(pool):
            pool.memset(ones[:], 1.0).then_inc(pool_step, 1)
            pool.memset(eps_t[:], EPS).then_inc(pool_step, 1)
            with pool.Fori(0, (DEPTH * UNITS + AHEAD) // 2) as i:
                for s in range(2):
                    pool.wait_ge(hi_ready, i * 2 + (s + 1))
                    pool.sem_inc(passed, 1)
                    for k in range(0, KT, 2):
                        ins = pool.tensor_tensor(w_lo[:, s, k:k + 2], raw[:, s, k:k + 2], w_hi[:, s, k:k + 2].bitcast(F32), ALU.subtract)
                    ins.then_inc(lo_ready, 1)

        @block.tensor
        def _(pe):
            c = Counts("pe", per, passed)

            def unit(s, bank, hi, lo, first=True, last=True, width=S, tiles=None, between=None):
                pe.wait_ge(hi_ready, c.next(hi_ready))
                if first:
                    pe.wait_ge(acc_free[bank], c.next(acc_free[bank]))
                out = acc[bank][:, 0:width]
                for k in range(KT):
                    if tiles is not None:
                        pe.wait_ge(tiles[0], tiles[1] + (k + 1))
                    elif between and k == KT // 2 + 1:
                        between()
                    pe.matmul(out, w_hi[:, s, k], hi[:, k, 0:width], start=first and k == 0, stop=False)
                    pe.matmul(out, w_hi[:, s, k], lo[:, k, 0:width], start=False, stop=False)
                if between and tiles is not None:
                    between()
                pe.wait_ge(lo_ready, c.next(lo_ready))
                for k in range(KT):
                    mm = pe.matmul(out, w_lo[:, s, k], hi[:, k, 0:width], start=False, stop=last and k == KT - 1)
                mm.then_inc(unit_done, 1)

            def pair(s0, s1, hi, lo, tiles):
                for s in (s0, s1):
                    pe.wait_ge(hi_ready, c.next(hi_ready))
                    pe.wait_ge(acc_free[s], c.next(acc_free[s]))
                pe.wait_ge(lo_ready, c.next(lo_ready))
                for k in range(KT):
                    pe.wait_ge(tiles[0], tiles[1] + (k + 1))
                    for s in (s1, s0):
                        pe.matmul(acc[s][:], w_hi[:, s, k], hi[:, k], start=k == 0, stop=False)
                        pe.matmul(acc[s][:], w_hi[:, s, k], lo[:, k], start=False, stop=False)
                    mm = pe.matmul(acc[s0][:], w_lo[:, s0, k], hi[:, k], start=False, stop=k == KT - 1)
                mm.then_inc(unit_done, 1)
                pe.wait_ge(lo_ready, c.next(lo_ready))
                for k in range(KT):
                    mm = pe.matmul(acc[s1][:], w_lo[:, s1, k], hi[:, k], start=False, stop=k == KT - 1)
                mm.then_inc(unit_done, 1)

            def expect(signal, n=KT):
                base = c.now(signal)
                c.next(signal, n)
                return signal, base

            def sum_of_squares():
                pe.wait_ge(sum_ready, c.next(sum_ready))
                pe.wait_ge(ss_free, c.next(ss_free))
                pe.matmul(ss[:], ones[:], acc_sq[:], start=True, stop=True).then_inc(ss_ready, 1)

            def in_unit(j, between=None):
                unit(j % 2, j % 2, u_hi, u_lo, between=between)

            def dt_turn():
                pe.wait_ge(dt_in, c.next(dt_in))
                pe.wait_ge(tp_free, c.next(tp_free))
                pe.sem_inc(passed, 1)
                for b in range(NBLK):
                    t = pe.transpose(tp[:, b * SSM_HEADS:(b + 1) * SSM_HEADS], dt_v[:, b * P:(b + 1) * P],
                                     ident[0:SSM_HEADS, 0:SSM_HEADS])
                t.then_inc(dt_turned, 1)

            def dt_sums():
                pe.wait_ge(dta_ready, c.next(dta_ready))
                dta = dt_w[:, 4]
                pe.matmul(pr[0][:, 0:P], upto[:], dta, start=True, stop=True)
                pe.matmul(pr[0][:, P:2 * P], ones[:], dta, start=True, stop=True)
                for b in range(NBLK):
                    mm = pe.matmul(pr[1][0:SSM_HEADS, b * P:(b + 1) * P], dta[:, b * SSM_HEADS:(b + 1) * SSM_HEADS], upto[:],
                                   start=True, stop=True)
                mm.then_inc(cum_ready, 1)

            def scan_stage(j, p):
                if j == 0:
                    pe.wait_ge(silu_ready, c.next(silu_ready, 4))
                    c.next(silu_ready, 2)
                if 1 <= j <= NBLK:
                    b = j - 1
                    at = slice(b * P, (b + 1) * P)
                    pe.wait_ge(blk_ready, c.next(blk_ready))
                    if b == 0:
                        pe.wait_ge(y_free, c.next(y_free))
                    else:
                        pe.wait_ge(cdec_ready, c.next(cdec_ready))
                        pe.wait_ge(st_ready, c.next(st_ready))
                    for h in range(HPG):
                        out = yp[h // 2][h % 2 * HD:(h % 2 + 1) * HD, at]
                        mm = pe.matmul(out, xdt[:, h], seg[:, h], start=True, stop=b == 0)
                        if b:
                            mm = pe.matmul(out, state[:, h], c_dec[:, h], start=False, stop=True)
                    mm.then_inc(y_blk, 1)
                    if b < NBLK - 1:
                        pe.wait_ge(dec_ready, c.next(dec_ready))
                        pe.matmul(pr[1][:, 0:HPG * HD], b_tok[:], xdt_dec[:].rearrange("p h d -> p (h d)"),
                                  start=True, stop=True).then_inc(st_sum, 1)
                if j < NBLK:
                    at = slice(j * P, (j + 1) * P)
                    pe.wait_ge(tp_free, c.next(tp_free))
                    pe.transpose(tp[:, 0:P], b_t[p][:, at], ident[:])
                    pe.transpose(tp[:, P:2 * P], xs_t[p][:, 0, at], ident[:])
                    pe.transpose(tp[:, 2 * P:3 * P], xs_t[p][:, 1, at], ident[:]).then_inc(turned, 1)
                    pe.wait_ge(cb_free, c.next(cb_free))
                    pe.matmul(pr[0][:, 0:P], b_t[p][:, at], c_t[p][:, at], start=True, stop=True).then_inc(cb_ready, 1)

            def head_stage(j, p):
                if j < 2:
                    if j == 0:
                        c.next(silu_ready, 2)
                        pe.wait_ge(q_ready, c.next(q_ready, 2))
                        pe.wait_ge(v_ready, c.next(v_ready, 2))
                    pe.wait_ge(tp_free, c.next(tp_free))
                    for b in range(NBLK):
                        mm = pe.transpose(tp[:, b * P:(b + 1) * P], v_t[p][:, j, b * P:(b + 1) * P], ident[:])
                    mm.then_inc(turned, 1)
                    for i in (2 * j, 2 * j + 1):
                        pe.wait_ge(sc_free, c.next(sc_free))
                        pe.matmul(pr[i % 2][:, 0:S - i * P], k_t[p][:, i * P:(i + 1) * P], q_t[p][:, i * P:S],
                                  start=True, stop=True).then_inc(sc_ready, 1)
                if j == 2:
                    pe.wait_ge(vtok_ready, c.next(vtok_ready, 2))
                    pe.wait_ge(y_free, c.next(y_free))
                    for i in range(NBLK):
                        pe.wait_ge(sc_done, c.next(sc_done))
                        for t in range(2):
                            mm = pe.matmul(yp[t][:, i * P:S], v_tok[:, i, t * P:(t + 1) * P], score[i][:],
                                           start=i == 0, stop=i == NBLK - 1)
                    mm.then_inc(head_y, 1)

            def attention_stage(j, p):
                if j == 0:
                    pe.wait_ge(xa_ready, c.next(xa_ready, 2))
                    pe.wait_ge(q_ready, c.next(q_ready, 2))
                    pe.wait_ge(v_ready, c.next(v_ready, 2))
                if j < 2:
                    pe.wait_ge(tp_free, c.next(tp_free))
                    for m in range(2):
                        mm = pe.transpose(tp[:, m * P:(m + 1) * P], xv[p][:, j, m * P:(m + 1) * P], ident[:])
                    mm.then_inc(turned, 1)
                if j < NBLK:
                    pe.wait_ge(sc_free, c.next(sc_free))
                    for k in range(2):
                        mm = pe.matmul(pr[j % 2][:, 0:MEM], xq[p][:, k, j * P:(j + 1) * P], xk[p][:, k],
                                       start=k == 0, stop=k == 1)
                    mm.then_inc(sc_ready, 1)
                if 2 <= j < NBLK + 2:
                    pe.wait_ge(prob_ready, c.next(prob_ready))
                    pe.wait_ge(tp_free, c.next(tp_free))
                    for m in range(2):
                        mm = pe.transpose(tp[:, m * P:(m + 1) * P], prob[:, j % 2, m * P:(m + 1) * P], ident[:])
                    mm.then_inc(turned, 1)

            def attention_out():
                pe.wait_ge(probt_ready, c.next(probt_ready, NBLK))
                pe.wait_ge(vtok_ready, c.next(vtok_ready, 2))
                pe.wait_ge(y_free, c.next(y_free))
                for t in range(2):
                    for m in range(2):
                        mm = pe.matmul(yp[t][:], xv_tok[:, m, t * P:(t + 1) * P], prob_t[:, m], start=m == 0, stop=m == 1)
                mm.then_inc(head_y, 1)

            def xa_unit(j, mem_tiles, tiles):
                if j < 4:
                    unit(j % 2, j % 2, mem_hi, mem_lo, width=MEM, tiles=mem_tiles)
                else:
                    unit(j % 2, j % 2, u_hi, u_lo, tiles=tiles)

            def plain_units(hi, lo, tiles, between=None):
                if between:
                    unit(0, 0, hi, lo, tiles=tiles, between=between)
                    unit(1, 1, hi, lo)
                with c.loop(pe, KT // 2 - (1 if between else 0)):
                    unit(0, 0, hi, lo, tiles=tiles)
                    unit(1, 1, hi, lo)

            def unit_parts(s, ks, tiles, last):
                if ks[0] == 0:
                    pe.wait_ge(hi_ready, c.next(hi_ready))
                    pe.wait_ge(lo_ready, c.next(lo_ready))
                    pe.wait_ge(acc_free[s], c.next(acc_free[s]))
                for k in ks:
                    pe.wait_ge(tiles[0], tiles[1] + (k + 1))
                    pe.matmul(acc[s][:], w_hi[:, s, k], o_hi[:, k], start=k == 0, stop=False)
                    pe.matmul(acc[s][:], w_hi[:, s, k], o_lo[:, k], start=False, stop=False)
                    mm = pe.matmul(acc[s][:], w_lo[:, s, k], o_hi[:, k], start=False, stop=k == KT - 1)
                if last:
                    mm.then_inc(unit_done, 1)

            pe.wait_ge(pool_step, 2)
            c.next(silu_ready, 2)
            with c.loop(pe, DEPTH):
                pe.wait_ge(hi_ready, c.next(hi_ready))
                c.next(lo_ready)
                pe.wait_ge(acc_free[0], c.next(acc_free[0]))
                pe.matmul(acc[0][:, 0:P], w_hi[:, 0, 0], w_hi[:, 0, 1], start=True, stop=True).then_inc(unit_done, 1)
                sum_of_squares()
                pair(1, 0, u_hi, u_lo, expect(pair_ready))
                pe.wait_ge(const_in, 4 * 16)
                for j in range(1, 6):
                    in_unit(j)
                    if j == 1:
                        dt_turn()
                    if j == 4:
                        dt_sums()
                pe.wait_ge(dec_in, c.next(dec_in))
                pe.wait_ge(cum_rows, c.next(cum_rows))
                def group(p):
                    for j in range(6):
                        scan_stage(j, p)
                        in_unit(j, sum_of_squares if j == NBLK + 1 else None)

                group(0)
                with c.loop(pe, GROUPS // 2 - 1):
                    group(1)
                    group(0)
                for j in range(KT):
                    scan_stage(j, 1)
                    in_unit(j, sum_of_squares if j == NBLK + 1 else None)
                tiles = expect(pair_ready, 2 * KT)
                with c.loop(pe, KT // 2):
                    for j in range(2):
                        unit(0, j, ys_hi[:, 0:KT], ys_lo[:, 0:KT], last=False, tiles=tiles)
                        unit(1, j, ys_hi[:, KT:2 * KT], ys_lo[:, KT:2 * KT], first=False, tiles=(tiles[0], tiles[1] + KT))
                for j in range(6):
                    in_unit(j)
                with c.loop(pe, RET_HEADS // 2 - 1):
                    for p in range(2):
                        for j in range(6):
                            head_stage(j, p)
                            in_unit(j, sum_of_squares if j == 4 else None)
                for j in range(6):
                    head_stage(j, 0)
                    in_unit(j, sum_of_squares if j == 4 else None)
                for j in range(KT):
                    head_stage(j, 1)
                    in_unit(j, sum_of_squares if j == 4 else None)
                plain_units(yr_hi, yr_lo, expect(pair_ready))
                plain_units(m_hi, m_lo, expect(pair_ready), between=sum_of_squares)
                mem_tiles, tiles = expect(mem_tile), expect(pair_ready)
                for j in range(6):
                    xa_unit(j, mem_tiles, tiles)
                    if j == 0:
                        sum_of_squares()
                with c.loop(pe, 1):
                    for p in range(2):
                        for j in range(6):
                            attention_stage(j, p)
                            xa_unit(j, None, None)
                        attention_out()
                for j in range(6):
                    attention_stage(j, 0)
                    xa_unit(j, None, None)
                attention_out()
                tiles = expect(pair_ready)
                for j in range(6):
                    attention_stage(j, 1)
                    for s in range(2):
                        unit_parts(s, (j,), tiles, False)
                attention_out()
                for s in range(2):
                    unit_parts(s, (6, 7), tiles, True)
                with c.loop(pe, KT // 2 - 1):
                    unit(0, 0, o_hi, o_lo)
                    unit(1, 1, o_hi, o_lo)
                plain_units(u_hi, u_lo, expect(pair_ready), between=sum_of_squares)
                plain_units(h_hi, h_lo, expect(pair_ready))
                with c.loop(pe, FFQ - 1):
                    plain_units(u_hi, u_lo, None)
                    plain_units(h_hi, h_lo, expect(pair_ready))
            sum_of_squares()

        @block.scalar
        def _(act):
            c = Counts("act", per, passed)

            def mark(ins, signal):
                ins.then_inc(signal, 1)
                c.next(signal)

            def then(ins, signal=act_step):
                mark(ins, signal)
                act.wait_ge(signal, c.now(signal))

            def split(s):
                act.wait_ge(raw_in[s], c.next(raw_in[s], 16))
                mark(act.activation(w_hi[:, s], raw[:, s], ACT.Copy), hi_ready)

            def step(s, before=None, after=None):
                act.wait_ge(unit_done, c.next(unit_done))
                if before:
                    before()
                split(s)
                if after:
                    after()

            def rms(scale):
                then(act.activation(log_warm[:], eps_t[:], ACT.Ln))
                act.wait_ge(ss_ready, c.next(ss_ready))
                then(act.activation(acc_sq[:], ss[:], ACT.Ln, bias=eps_t[:], scale=scale), ss_free)
                mark(act.activation(rstd[:], acc_sq[:], ACT.Exp, scale=-0.5), rstd_ready)

            def high_parts(n, dst, src):
                for k in range(n):
                    act.wait_ge(tmp_ready, c.next(tmp_ready))
                    mark(act.activation(dst(k), src(k), ACT.Copy), hi_tile)

            def square_of_x(k, j):
                act.wait_ge(x_tile, c.next(x_tile))
                act.wait_ge(sq_free, c.next(sq_free))
                mark(act.activation(t2[:, j], tile(x, k), ACT.Square), sq_ready)

            def high_of_u(k, j):
                act.wait_ge(tmp_ready, c.next(tmp_ready))
                mark(act.activation(tile(u_hi, k), e2[:, j], ACT.Copy), hi_tile)

            def load_rows(g, b):
                act.dma_start(row[:, b % 2], cum_dram[bass.ds(g, 1), :, b * P:(b + 1) * P]
                              .rearrange("a h s -> (a h) s").partition_broadcast(P)).then_inc(row_in[b % 2], 16)

            def rotary_tables():
                act.wait_ge(angle_ready, c.next(angle_ready))
                then(act.activation(e2[:, 1], e2[:, 0], ACT.Sin))
                then(act.activation(sin_sb[0:64], e2[0:64, 1], ACT.Copy))
                then(act.activation(sin_sb[64:128], e2[0:64, 1], ACT.Copy, scale=-1.0))
                then(act.activation(cos_sb[0:64], e2[64:128, 1], ACT.Copy))
                then(act.activation(cos_sb[64:128], e2[64:128, 1], ACT.Copy), trig_ready)

            c.next(ss_free)
            act.wait_ge(pool_step, 2)
            for k in range(KT):
                if k % 2 == 0:
                    act.wait_ge(x_in[k // 2], 16)
                if k >= 4:
                    act.wait_ge(sq_free, 2 + (k - 3))
                mark(act.activation(u_slot(k), x[:, k], ACT.Square), sq_ready)
            c.next(x_tile, KT)
            c.next(sq_free, KT)
            split(0)
            split(1)
            act.dma_start(decay[:], a["decay"]).then_inc(decay_in, 16)

            def conv_unit(s, j, p):
                def before():
                    act.wait_ge(silu_ready, c.next(silu_ready))
                    if j == 0:
                        act.wait_ge(gp_ready, c.next(gp_ready))
                    mark(act.activation(t2[:, s], acc[s][:], ACT.Identity, bias=gp_half[p][:, G_BIAS + j:G_BIAS + j + 1],
                                        scale=gp_half[p][:, G_TAP + 4 * j + 3:G_TAP + 4 * j + 4]), lin_ready)

                def finish():
                    act.wait_ge(conv_ready, c.next(conv_ready))
                    mark(act.activation(e2[:, s], t2[:, s], ACT.Tanh), tanh_ready)
                step(s, before)
                return finish

            def silu_unit(s):
                def before():
                    act.wait_ge(silu_ready, c.next(silu_ready))
                    mark(act.activation(e2[:, s], acc[s][:], ACT.Tanh, scale=0.5), tanh_ready)
                step(s, before)

            def group_unit(j, p):
                if j < 4:
                    return conv_unit(j % 2, j, p)
                silu_unit(j % 2)
                return lambda: None

            def gate_unit(j, dst, col):
                def before():
                    act.activation(dst[:, j], acc[j % 2][:], ACT.Tanh, bias=half_gate[:, col:col + 1], scale=0.5).then_inc(acc_free[j % 2], 1)
                step(j % 2, before)

            def scan_stage(j, p, g, last=False):
                if j < NBLK:
                    act.wait_ge(row_in[j % 2], c.next(row_in[j % 2], 16))
                    if j:
                        act.wait_ge(y_blk, c.next(y_blk))
                    for h in range(HPG):
                        ins = act.activation(seg[:, h], row[:, j % 2, h], ACT.Abs, bias=tile(tok[:, 1, j:j + 1].rearrange("p a n -> p n a"), g * HPG + h))
                    then(ins)
                    mark(act.activation(seg[:], seg[:], ACT.Exp, scale=-1.0), seg_ready)
                    if j:
                        then(act.activation(c_dec[:], row[:, j % 2], ACT.Exp), edec_ready)
                    if j + 2 < NBLK:
                        load_rows(g, j + 2)
                    elif not last:
                        load_rows(g + 1, j + 2 - NBLK)
                if j == NBLK:
                    act.wait_ge(y_blk, c.next(y_blk))
                    act.wait_ge(out_ready, c.next(out_ready))
                    for t in range(2):
                        mark(act.activation(z_t[p][:, t], xs_t[p][:, t], ACT.Square), sq_ready)
                if j == NBLK + 1:
                    rms(1.0 / (SSM_INNER // GROUPS))

            def scan_out(p, g):
                high_parts(2, lambda t: tile(ys_hi, g * 2 + t), lambda t: z_t[p][:, t])

            def head_unit(j, p):
                if j < 2:
                    step(j)
                elif j < 4:
                    def before():
                        then(act.activation(v_t[p][:, j - 2], acc[j % 2][:], ACT.Copy), v_ready)
                    step(j % 2, before)
                else:
                    silu_unit(j % 2)

            def head_stage(j, p):
                if j == 3:
                    act.wait_ge(head_y, c.next(head_y))
                    for t in range(2):
                        then(act.activation(v_t[p][:, t], yp[t][:], ACT.Copy), y_copied)
                        act.wait_ge(sq_free, c.next(sq_free))
                        mark(act.activation(q_t[p][:] if t else k_t[p][:], v_t[p][:, t], ACT.Square), sq_ready)
                if j == 5:
                    rms(1.0 / (RET_V // RET_HEADS))

            def head_out(h):
                high_parts(2, lambda t: tile(yr_hi, h * 2 + t), lambda t: t2[:, t])

            def xa_unit(j, p):
                def before():
                    if j < 2:
                        mark(act.activation(xk[p][:, j], acc[j][:, 0:MEM], ACT.Copy), xa_ready)
                    elif j < 4:
                        then(act.activation(xv[p][:, j - 2], acc[j % 2][:, 0:MEM], ACT.Copy), v_ready)
                    if j < 4:
                        act.sem_inc(acc_free[j % 2], 1)
                step(j % 2, before)

            def attention_stage(j):
                if j < NBLK:
                    act.wait_ge(max_ready, c.next(max_ready))
                    mark(act.activation(prob[:, j % 2], pr[j % 2][:, 0:MEM], ACT.Exp,
                                        bias=small[:, j % 2:j % 2 + 1], accum_out=small[:, 2 + j % 2:3 + j % 2]), prob_raw)

            def attention_out(h):
                act.wait_ge(head_y, c.next(head_y))
                for t in range(2):
                    mark(act.activation(tile(o_hi, h * 2 + t), yp[t][:], ACT.Copy), hi_tile)

            def added_units(to_u):
                with c.loop(act, KT // 2) as i:
                    for j in range(2):
                        def after():
                            square_of_x(i * 2 + j, j)
                            if to_u:
                                high_of_u(i * 2 + j, j)
                        step(j, None, after)

            with c.loop(act, DEPTH) as l:
                rms(1.0 / D)
                step(0)
                high_parts(KT, lambda k: u_hi[:, k], u_slot)
                step(1)
                for j in range(6):
                    group_unit(j, 0)()
                    if j == 0:
                        act.wait_ge(half_ready, c.next(half_ready))
                        mark(act.activation(a_pos[:], layer_par(l, L_ALOG, SSM_HEADS), ACT.Exp), a_ready)
                    if j == 1:
                        act.wait_ge(dt_copied, c.next(dt_copied))
                        then(act.activation(dt_w[:, 1], dt_w[:, 0], ACT.Abs))
                        mark(act.activation(dt_w[:, 2], dt_w[:, 1], ACT.Exp, scale=-1.0), dt_exp)
                    if j == 4:
                        act.wait_ge(cum_ready, c.next(cum_ready))
                        then(act.activation(dt_rows_sb[:], pr[1][0:SSM_HEADS, :], ACT.Copy), cum_rows)
                        act.dma_start(cum_dram.rearrange("g h s -> (g h) s"), dt_rows_sb[:]).then_inc(cum_out, 16)
                        act.wait_ge(dec_in, c.next(dec_in))
                        then(act.activation(tok[:, 2:4], tok[:, 2:4], ACT.Exp), dec_out)
                        act.wait_ge(cum_out, c.next(cum_out, 16))
                        load_rows(0, 0)
                        load_rows(0, 1)

                def group(p, g, last_g=None):
                    for j in range(6):
                        scan_stage(j, p, g)
                        if j:
                            finish()
                        finish = group_unit(j, 1 - p)
                        if j == 0 and last_g is not None:
                            scan_out(1 - p, last_g)
                    finish()

                group(0, 0)
                with c.loop(act, GROUPS // 2 - 1) as i:
                    group(1, i * 2 + 1, i * 2)
                    group(0, i * 2 + 2, i * 2 + 1)
                for j in range(KT):
                    scan_stage(j, 1, GROUPS - 1, last=True)
                    gate_unit(j, merge, KT + j)
                    if j == 0:
                        scan_out(0, GROUPS - 2)
                scan_out(1, GROUPS - 1)
                act.dma_start(e2[:, 0].bitcast(I32), a["pos"].partition_broadcast(P)).then_inc(pos_in, 16)
                step(0)
                step(1)
                rotary_tables()
                with c.loop(act, KT - 1):
                    step(0)
                    step(1)
                act.dma_start(mem[:], a["mem"]).then_inc(mem_in, 16)
                for j in range(6):
                    head_unit(j, 0)
                with c.loop(act, RET_HEADS // 2 - 1) as i:
                    for p in range(2):
                        for j in range(6):
                            head_stage(j, p)
                            head_unit(j, 1 - p)
                        head_out(i * 2 + p)
                for j in range(6):
                    head_stage(j, 0)
                    head_unit(j, 1)
                head_out(RET_HEADS - 2)
                for j in range(KT):
                    head_stage(j, 1)
                    gate_unit(j, gate_r, j)
                head_out(RET_HEADS - 1)
                act.wait_ge(mem_in, c.next(mem_in, 16))
                with c.loop(act, KT // 2) as i:
                    for j in range(2):
                        step(j)
                        act.wait_ge(tmp_ready, c.next(tmp_ready))
                        mark(act.activation(tile(m_hi, i * 2 + j), t2[:, 0], ACT.Copy, scale=0.5), hi_tile)
                        act.wait_ge(mem_slot, c.next(mem_slot))
                        mark(act.activation(e2[:, j, 0:MEM], tile(mem, i * 2 + j), ACT.Square), mem_sq)
                rms(1.0 / D)
                with c.loop(act, KT // 2) as i:
                    for j in range(2):
                        def after():
                            square_of_x(i * 2 + j, j)
                            high_of_u(i * 2 + j, j)
                        act.wait_ge(mem_tmp, c.next(mem_tmp))
                        mark(act.activation(tile(mem_hi, i * 2 + j), gate_r[:, j, 0:MEM], ACT.Copy), mem_hi_ready)
                        step(j, None, after)
                for j in range(6):
                    xa_unit(j, 0)
                    if j == 0:
                        rms(1.0 / D)
                with c.loop(act, 1) as i:
                    for p in range(2):
                        for j in range(6):
                            attention_stage(j)
                            xa_unit(j, 1 - p)
                        attention_out(i * 2 + p)
                for j in range(6):
                    attention_stage(j)
                    xa_unit(j, 1)
                attention_out(2)
                for j in range(6):
                    attention_stage(j)
                attention_out(3)
                added_units(True)
                rms(1.0 / D)

                def inner_units():
                    with c.loop(act, KT // 2) as i:
                        for j in range(2):
                            def after():
                                act.wait_ge(relu_ready, c.next(relu_ready))
                                then(act.activation(e2[:, j], t2[:, j], ACT.Square))
                                mark(act.activation(tile(h_hi, i * 2 + j), e2[:, j], ACT.Copy), hi_tile)
                            step(j, None, after)

                with c.loop(act, FFQ - 1):
                    inner_units()
                    with c.loop(act, KT // 2):
                        step(0)
                        step(1)
                inner_units()
                c.next(x_tile, (FFQ - 1) * KT)
                added_units(False)
            rms(1.0 / D)
            for k in range(KT):
                act.wait_ge(final_ready, k + 1)
                act.dma_start(a["out"][:, k], x[:, k]).then_inc(out_done, 16)
            act.wait_ge(out_done, KT * 16)

        @block.vector
        def _(dve):
            c = Counts("dve", per, passed)

            def mark(ins, signal=dve_step):
                ins.then_inc(signal, 1)
                return c.next(signal)

            def then(ins, signal=dve_step):
                dve.wait_ge(signal, mark(ins, signal))

            def step(s, before=None, after=None):
                dve.wait_ge(unit_done, c.next(unit_done))
                if before:
                    before()
                if after:
                    after()

            def low_parts(n, make, hi, lo):
                for k in range(n + 1):
                    if k < n:
                        make(k)
                    if k:
                        dve.wait_ge(hi_tile, c.next(hi_tile))
                        then(dve.tensor_tensor(lo(k - 1), t2[:, (k - 1) % 2], hi(k - 1).bitcast(F32), ALU.subtract), pair_ready)

            def add_square(j):
                dve.wait_ge(sq_ready, c.next(sq_ready))
                then(dve.tensor_tensor(acc_sq[:], acc_sq[:], t2[:, j], ALU.add), sq_free)

            def make_u(l, col):
                dve.wait_ge(rstd_ready, c.next(rstd_ready))

                low = []
                for k in range(KT + 2):
                    if k < KT:
                        if k >= 4:
                            dve.wait_ge(pair_ready, low[k - 4])
                        mark(dve.scalar_tensor_tensor(u_slot(k), x[:, k], layer_par(l, col + k), rstd[:], ALU.mult, ALU.mult), tmp_ready)
                    if k >= 2:
                        dve.wait_ge(hi_tile, c.next(hi_tile))
                        low.append(mark(dve.tensor_tensor(u_lo[:, k - 2], u_slot(k - 2), u_hi[:, k - 2].bitcast(F32), ALU.subtract), pair_ready))
                dve.wait_ge(pair_ready, low[-1])

            def free(bank):
                dve.sem_inc(acc_free[bank], 1)

            def rotary_angles():
                dve.wait_ge(pos_in, c.next(pos_in, 16))
                ang, n_hi, n_lo, tmp = e2[:, 0], rstd[:], acc_sq[:], e2[:, 1]
                then(dve.tensor_copy(tmp, e2[:, 0].bitcast(I32)))
                then(dve.tensor_scalar(ang, tmp, freq[:, 0:1], None, ALU.mult))
                then(dve.tensor_scalar(tmp, ang, 1.0 / TWO_PI, freq[:, 1:2], ALU.mult, ALU.add))
                then(dve.tensor_scalar(tmp, tmp, MAGIC, None, ALU.add))
                then(dve.tensor_scalar(tmp, tmp, MAGIC, None, ALU.subtract))
                then(dve.tensor_scalar(n_hi, tmp, 4096.0 * MAGIC, None, ALU.add))
                then(dve.tensor_scalar(n_hi, n_hi, 4096.0 * MAGIC, None, ALU.subtract))
                then(dve.tensor_tensor(n_lo, tmp, n_hi, ALU.subtract))
                for n, const in ((n_hi, C1), (n_lo, C1), (n_hi, C2), (n_lo, C2), (tmp, C3)):
                    then(dve.scalar_tensor_tensor(ang, n, -const, ang, ALU.mult, ALU.add))
                then(dve.tensor_scalar(ang, ang, freq[:, 2:3], None, ALU.add))
                then(dve.tensor_scalar(ang, ang, 3.1415925, -3.1415925, ALU.min, ALU.max), angle_ready)

            then(dve.memset(acc_sq[:], 0.0))
            for s_, n in ((sq_free, 2), (silu_ready, 2), (ss_free, 1), (tp_free, 1), (cb_free, 1), (y_free, 1),
                          (sc_free, 2), (mem_slot, 2), (acc_free[0], 1), (acc_free[1], 1)):
                dve.sem_inc(s_, n)
                c.next(s_, n)
            for k in range(KT):
                dve.wait_ge(sq_ready, c.next(sq_ready))
                then(dve.tensor_tensor(acc_sq[:], acc_sq[:], u_slot(k), ALU.add), sq_free)
            dve.sem_inc(sum_ready, 1)
            dve.sem_inc(x_tile, KT)
            c.next(x_tile, KT)
            dve.wait_ge(par_in, 16)
            dve.wait_ge(angle_in, 16)

            def conv_unit(s, j, p, dst):
                def before():
                    dve.wait_ge(lin_ready, c.next(lin_ready))
                    for i in (2, 1, 0):
                        far = 3 - i
                        w = gp_half[p][:, G_TAP + 4 * j + i:G_TAP + 4 * j + i + 1]
                        then(dve.scalar_tensor_tensor(t2[:, s, far:S], acc[s][:, 0:S - far], w, t2[:, s, far:S], ALU.mult, ALU.add),
                             dve_step if i else conv_ready)
                    free(s)

                def finish():
                    dve.wait_ge(tanh_ready, c.next(tanh_ready))
                    mark(dve.scalar_tensor_tensor(dst, e2[:, s], 1.0, t2[:, s], ALU.add, ALU.mult), silu_ready)
                step(s, before)
                return finish

            def silu_unit(s, dst):
                def finish():
                    dve.wait_ge(tanh_ready, c.next(tanh_ready))
                    then(dve.scalar_tensor_tensor(dst, e2[:, s], 1.0, acc[s][:], ALU.add, ALU.mult), silu_ready)
                    free(s)
                step(s)
                return finish

            def group_taps(p, l, g):
                mark(dve.tensor_scalar(gp_half[p][:], layer_par(l, g * GPN + LPN, G_SKIP), 0.5, None, ALU.mult), gp_ready)

            def group_unit(j, p, l, g):
                if j == 0:
                    mark(dve.tensor_scalar(gp[p][:], layer_par(l, g * GPN + LPN, GPN), 1.0, None, ALU.mult))
                if j < 4:
                    return conv_unit(j % 2, j, p, (b_t[p][:], c_t[p][:], xs_t[p][:, 0], xs_t[p][:, 1])[j])
                return silu_unit(j % 2, z_t[p][:, j - 4])

            def scan_stage(j, p, g):
                def heads(kind, b, n):
                    return tok[:, kind, b, bass.ds(g * HPG, HPG)].unsqueeze(2).broadcast_to([P, HPG, n])

                if 1 <= j < NBLK:
                    b = j - 1
                    new = pr[1][:, 0:HPG * HD].rearrange("p (h d) -> p h d", h=HPG)
                    if b:
                        dve.wait_ge(y_blk, c.next(y_blk))
                        then(dve.tensor_tensor(state[:], state[:], heads(3, b, HD), ALU.mult))
                        dve.wait_ge(st_sum, c.next(st_sum))
                        mark(dve.tensor_tensor(state[:], state[:], new, ALU.add), st_ready)
                    else:
                        dve.wait_ge(y_blk, c.next(y_blk))
                        dve.wait_ge(st_sum, c.next(st_sum))
                        mark(dve.tensor_copy(state[:], new), st_ready)
                if j < NBLK:
                    b = j
                    at = slice(b * P, (b + 1) * P)
                    dve.wait_ge(turned, c.next(turned))
                    weighted = mark(dve.tensor_tensor(xdt[:], tp[:, P:3 * P].rearrange("p (h d) -> p h d", h=HPG), heads(0, b, HD), ALU.mult))
                    then(dve.tensor_copy(b_tok[:], tp[:, 0:P]), tp_free)
                    dve.wait_ge(cb_ready, c.next(cb_ready))
                    mark(dve.tensor_tensor(cb_m[:], pr[0][:, 0:P], mask[:], ALU.mult), cb_free)
                    if b < NBLK - 1:
                        dve.wait_ge(dve_step, weighted)
                        mark(dve.tensor_tensor(xdt_dec[:], xdt[:], heads(2, b, HD), ALU.mult), dec_ready)
                    dve.wait_ge(cb_free, c.now(cb_free))
                    dve.wait_ge(seg_ready, c.next(seg_ready))
                    mark(dve.tensor_tensor(seg[:], seg[:], cb_m[:].unsqueeze(1).broadcast_to([P, HPG, P]), ALU.mult), blk_ready)
                    if b:
                        dve.wait_ge(edec_ready, c.next(edec_ready))
                        mark(dve.tensor_tensor(c_dec[:], c_dec[:], c_t[p][:, at].unsqueeze(1).broadcast_to([P, HPG, P]), ALU.mult), cdec_ready)
                if j == NBLK:
                    dve.wait_ge(y_blk, c.next(y_blk, 1))
                    for t in range(2):
                        then(dve.scalar_tensor_tensor(xs_t[p][:, t], xs_t[p][:, t], gp[p][:, G_SKIP + t:G_SKIP + t + 1], yp[t][:], ALU.mult, ALU.add))
                        then(dve.scalar_tensor_tensor(xs_t[p][:, t], xs_t[p][:, t], 0.5, z_t[p][:, t], ALU.mult, ALU.mult),
                             (out_ready if t else y_free))
                    dve.wait_ge(sq_ready, c.next(sq_ready, 2))
                    then(dve.tensor_tensor(acc_sq[:], z_t[p][:, 0], z_t[p][:, 1], ALU.add), sum_ready)

            def scan_norm(p, g):
                dve.wait_ge(rstd_ready, c.next(rstd_ready))
                for t in range(2):
                    then(dve.scalar_tensor_tensor(z_t[p][:, t], xs_t[p][:, t], gp[p][:, G_NORM + t:G_NORM + t + 1], rstd[:], ALU.mult, ALU.mult), tmp_ready)

            def scan_low(p, g):
                for t in range(2):
                    dve.wait_ge(hi_tile, c.next(hi_tile))
                    then(dve.tensor_tensor(tile(ys_lo, g * 2 + t), z_t[p][:, t], tile(ys_hi, g * 2 + t).bitcast(F32), ALU.subtract), pair_ready)

            def head_unit(j, p):
                if j < 2:
                    dst = (q_t, k_t)[j][p]

                    def before():
                        mark(dve.tensor_tensor(dst[:], acc[j][:], cos_sb[:], ALU.mult))
                        mark(dve.tensor_tensor(t2[64:128, j], acc[j][0:64], sin_sb[0:64], ALU.mult))
                        then(dve.tensor_tensor(t2[0:64, j], acc[j][64:128], sin_sb[64:128], ALU.mult))
                        free(j)
                        then(dve.tensor_tensor(dst[:], dst[:], t2[:, j], ALU.add), q_ready)
                    step(j, before)
                elif j < 4:
                    step(j % 2)
                    dve.wait_ge(v_ready, c.next(v_ready))
                    free(j % 2)
                else:
                    silu_unit(j % 2, g_t[p][:, j - 4])()

            def head_stage(j, p, h):
                if j < 2:
                    dve.wait_ge(turned, c.next(turned))
                    then(dve.tensor_copy(v_tok[:, :, j * P:(j + 1) * P], tp[:].rearrange("p (b e) -> p b e", b=NBLK)), vtok_ready)
                    dve.sem_inc(tp_free, 1)
                    for i in (2 * j, 2 * j + 1):
                        n = S - i * P
                        dve.wait_ge(sc_ready, c.next(sc_ready))
                        then(dve.tensor_tensor(score[i][:], pr[i % 2][:, 0:n], decay[:, bass.ds(h, 1), 0:n].rearrange("p a s -> p (a s)"), ALU.mult), sc_done)
                        dve.sem_inc(sc_free, 1)
                if j == 3:
                    dve.wait_ge(y_copied, c.next(y_copied, 2))
                    dve.sem_inc(y_free, 1)
                    dve.wait_ge(sq_ready, c.next(sq_ready, 2))
                    then(dve.tensor_tensor(acc_sq[:], k_t[p][:], q_t[p][:], ALU.add), sum_ready)
                    dve.sem_inc(sq_free, 2)
                    c.next(sq_free, 2)

            def head_out(p, h):
                dve.wait_ge(rstd_ready, c.next(rstd_ready))

                def make(t):
                    then(dve.scalar_tensor_tensor(t2[:, t], v_t[p][:, t], 0.5, rstd[:], ALU.mult, ALU.mult))
                    then(dve.tensor_tensor(t2[:, t], t2[:, t], g_t[p][:, t], ALU.mult), tmp_ready)
                low_parts(2, make, lambda t: tile(yr_hi, h * 2 + t), lambda t: tile(yr_lo, h * 2 + t))

            def xa_unit(j, p):
                if j < 4:
                    step(j % 2)
                else:
                    def before():
                        then(dve.scalar_tensor_tensor(xq[p][:, j - 4], acc[j % 2][:], (2 * P) ** -0.5, rstd[:], ALU.mult, ALU.mult), q_ready)
                        free(j % 2)
                    step(j % 2, before)

            def attention_stage(j):
                if j < 2:
                    dve.wait_ge(turned, c.next(turned))
                    then(dve.tensor_copy(xv_tok[:, :, j * P:(j + 1) * P], tp[:, 0:2 * P].rearrange("p (m e) -> p m e", m=2)), vtok_ready)
                    dve.sem_inc(tp_free, 1)
                if 1 <= j <= NBLK:
                    i = (j - 1) % 2
                    dve.wait_ge(prob_raw, c.next(prob_raw))
                    dve.sem_inc(sc_free, 1)
                    then(dve.reciprocal(small[:, 5:6], small[:, 2 + i:3 + i]))
                    mark(dve.tensor_scalar(prob[:, i], prob[:, i], small[:, 5:6], None, ALU.mult), prob_ready)
                if j < NBLK:
                    dve.wait_ge(sc_ready, c.next(sc_ready))
                    then(dve.tensor_reduce(small[:, 4:5], pr[j % 2][:, 0:MEM], AX, ALU.max))
                    if j >= 2:
                        dve.wait_ge(turned, c.next(turned))
                    then(dve.tensor_scalar(small[:, j % 2:j % 2 + 1], small[:, 4:5], -1.0, None, ALU.mult), max_ready)
                if 2 <= j < NBLK + 2:
                    if j >= NBLK:
                        dve.wait_ge(turned, c.next(turned))
                    then(dve.tensor_copy(prob_t[:, :, (j - 2) * P:(j - 1) * P], tp[:, 0:2 * P].rearrange("p (m s) -> p m s", m=2)), probt_ready)
                    dve.sem_inc(tp_free, 1)

            def attention_out(h):
                for t in range(2):
                    dve.wait_ge(hi_tile, c.next(hi_tile))
                    then(dve.tensor_tensor(tile(o_lo, h * 2 + t), yp[t][:], tile(o_hi, h * 2 + t).bitcast(F32), ALU.subtract), pair_ready)
                dve.sem_inc(y_free, 1)

            def weighted(k, j, l, col):
                then(dve.tensor_scalar(e2[:, j], tile(x, k), layer_par(l, k + col), None, ALU.mult), tmp_ready)

            def low_of_u(k, j):
                dve.wait_ge(hi_tile, c.next(hi_tile))
                mark(dve.tensor_tensor(tile(u_lo, k), e2[:, j], tile(u_hi, k).bitcast(F32), ALU.subtract), pair_ready)

            def add_units(squares, next_norm=None):
                if squares:
                    then(dve.memset(acc_sq[:], 0.0))
                with c.loop(dve, KT // 2) as i:
                    for j in range(2):
                        def before():
                            then(dve.tensor_tensor(tile(x, i * 2 + j), tile(x, i * 2 + j), acc[j][:], ALU.add), x_tile)
                            free(j)
                            if next_norm:
                                weighted(i * 2 + j, j, *next_norm)

                        def after():
                            if squares:
                                add_square(j)
                            if next_norm:
                                low_of_u(i * 2 + j, j)
                        step(j, before, after)

            with c.loop(dve, DEPTH) as l:
                then(dve.tensor_scalar(half_gate[:], layer_par(l, L_GATE, 2 * KT), 0.5, None, ALU.mult), half_ready)
                step(0, lambda: free(0))
                make_u(l, L_MIX)

                def dt_part():
                    then(dve.tensor_scalar(dt_v[:], acc[1][0:SSM_HEADS, :], layer_par(l, L_DTB, rows=slice(0, SSM_HEADS)), None, ALU.add), dt_in)
                    free(1)
                step(1, dt_part)
                v, e, ratio, squared, series, dta = dt_w[:, 0], dt_w[:, 2], dt_w[:, 3], dt_w[:, 1], dt_w[:, 4], dt_w[:, 4]
                by_head = lambda t: t.rearrange("p (b h) -> p b h", b=NBLK)
                flat = lambda t: t.rearrange("p b h -> p (b h)")
                group_taps(0, l, 0)
                for j in range(6):
                    if j == 2:
                        dve.wait_ge(dt_turned, c.next(dt_turned))
                        then(dve.tensor_copy(v, tp[:, 0:P]), dt_copied)
                        dve.sem_inc(tp_free, 1)
                        c.next(tp_free)
                    group_unit(j, 0, l, 0)()
                    if j == 2:
                        dve.wait_ge(dt_exp, c.next(dt_exp))
                        then(dve.tensor_scalar(squared, e, 2.0, None, ALU.add))
                        then(dve.reciprocal(ratio, squared))
                        then(dve.tensor_tensor(ratio, ratio, e, ALU.mult))
                        then(dve.tensor_tensor(squared, ratio, ratio, ALU.mult))
                        then(dve.tensor_scalar(series, squared, 1.0 / 15, None, ALU.mult))
                        for n in (13, 11, 9, 7, 5, 3):
                            then(dve.scalar_tensor_tensor(series, series, 1.0 / n, squared, ALU.add, ALU.mult))
                        then(dve.scalar_tensor_tensor(series, series, 1.0, ratio, ALU.add, ALU.mult))
                        then(dve.tensor_scalar(v, v, 0.0, None, ALU.max))
                        then(dve.scalar_tensor_tensor(flat(tok[:, 0]), series, 2.0, v, ALU.mult, ALU.add))
                        dve.wait_ge(a_ready, c.next(a_ready))
                        then(dve.scalar_tensor_tensor(by_head(dta), tok[:, 0], -1.0,
                                                      a_pos[:].unsqueeze(1).broadcast_to([P, NBLK, SSM_HEADS]), ALU.mult, ALU.mult), dta_ready)
                    if j == 4:
                        dve.wait_ge(cum_ready, c.next(cum_ready))
                        then(dve.tensor_scalar(flat(tok[:, 1]), pr[0][:, 0:P], -1.0, None, ALU.mult))
                        mark(dve.tensor_tensor(flat(tok[:, 2]), pr[0][:, P:2 * P], flat(tok[:, 1]), ALU.add))
                        then(dve.tensor_copy(flat(tok[:, 3]), pr[0][:, P:2 * P]), dec_in)
                dve.wait_ge(dec_out, c.next(dec_out))
                dve.wait_ge(cum_rows, c.next(cum_rows))
                dve.wait_ge(const_in, 4 * 16)

                def group(p, g, last_g=None):
                    for j in range(6):
                        scan_stage(j, p, g)
                        if j == 0:
                            group_taps(1 - p, l, g + 1)
                        if last_g is not None:
                            if j == 0:
                                scan_norm(1 - p, last_g)
                            if j == 5:
                                scan_low(1 - p, last_g)
                        if j:
                            finish()
                        finish = group_unit(j, 1 - p, l, g + 1)
                    finish()

                group(0, 0)
                with c.loop(dve, GROUPS // 2 - 1) as i:
                    group(1, i * 2 + 1, i * 2)
                    group(0, i * 2 + 2, i * 2 + 1)
                for j in range(KT):
                    scan_stage(j, 1, GROUPS - 1)
                    if j == 0:
                        scan_norm(0, GROUPS - 2)
                    if j == 1:
                        scan_low(0, GROUPS - 2)
                    step(j % 2)
                scan_norm(1, GROUPS - 1)
                scan_low(1, GROUPS - 1)
                rotary_angles()
                with c.loop(dve, KT // 2) as i:
                    for j in range(2):
                        step(0)

                        def before():
                            then(dve.scalar_tensor_tensor(tile(merge, i * 2 + j), tile(merge, i * 2 + j), 1.0, acc[j][:], ALU.add, ALU.mult))
                            free(j)
                        step(1, before)
                dve.wait_ge(trig_ready, c.next(trig_ready))
                dve.wait_ge(decay_in, 16)
                for j in range(6):
                    head_unit(j, 0)
                with c.loop(dve, RET_HEADS // 2 - 1) as i:
                    for p in range(2):
                        for j in range(6):
                            head_stage(j, p, i * 2 + p)
                            head_unit(j, 1 - p)
                        head_out(p, i * 2 + p)
                for j in range(6):
                    head_stage(j, 0, RET_HEADS - 2)
                    head_unit(j, 1)
                head_out(0, RET_HEADS - 2)
                for j in range(KT):
                    head_stage(j, 1, RET_HEADS - 1)
                    step(j % 2)
                head_out(1, RET_HEADS - 1)
                then(dve.memset(acc_sq[:], 0.0))
                with c.loop(dve, KT // 2) as i:
                    for j in range(2):
                        def before():
                            then(dve.scalar_tensor_tensor(t2[:, 1], tile(gate_r, i * 2 + j), 1.0, acc[j][:], ALU.add, ALU.mult))
                            free(j)
                            then(dve.tensor_tensor(t2[:, 0], t2[:, 1], tile(merge, i * 2 + j), ALU.add), tmp_ready)

                        def after():
                            dve.wait_ge(hi_tile, c.next(hi_tile))
                            then(dve.scalar_tensor_tensor(tile(m_lo, i * 2 + j), t2[:, 0], 0.5, tile(m_hi, i * 2 + j).bitcast(F32),
                                                          ALU.mult, ALU.subtract), pair_ready)
                            dve.wait_ge(mem_sq, c.next(mem_sq))
                            then(dve.tensor_tensor(acc_sq[:, 0:MEM], acc_sq[:, 0:MEM], e2[:, j, 0:MEM], ALU.add), mem_slot)
                        step(j, before, after)
                dve.sem_inc(sum_ready, 1)
                dve.wait_ge(rstd_ready, c.next(rstd_ready))
                then(dve.memset(acc_sq[:], 0.0))
                with c.loop(dve, KT // 2) as i:
                    for j in range(2):
                        def before():
                            then(dve.tensor_tensor(tile(x, i * 2 + j), tile(x, i * 2 + j), acc[j][:], ALU.add), x_tile)
                            free(j)
                            weighted(i * 2 + j, j, l, L_XA)
                            dve.wait_ge(mem_hi_ready, c.next(mem_hi_ready))
                            then(dve.tensor_tensor(tile(mem_lo, i * 2 + j), gate_r[:, j, 0:MEM], tile(mem_hi, i * 2 + j).bitcast(F32), ALU.subtract), mem_tile)

                        def after():
                            add_square(j)
                            low_of_u(i * 2 + j, j)
                        mark(dve.scalar_tensor_tensor(gate_r[:, j, 0:MEM], tile(mem, i * 2 + j), layer_par(l, i * 2 + j + L_MEM),
                                                      rstd[:, 0:MEM], ALU.mult, ALU.mult), mem_tmp)
                        step(j, before, after)
                dve.sem_inc(sum_ready, 1)
                dve.wait_ge(rstd_ready, c.next(rstd_ready))
                for j in range(6):
                    xa_unit(j, 0)
                with c.loop(dve, 1) as i:
                    for p in range(2):
                        for j in range(6):
                            attention_stage(j)
                            xa_unit(j, 1 - p)
                        attention_out(i * 2 + p)
                for j in range(6):
                    attention_stage(j)
                    xa_unit(j, 1)
                attention_out(2)
                for j in range(6):
                    attention_stage(j)
                attention_out(3)
                add_units(True, (l, L_MLP))
                dve.sem_inc(sum_ready, 1)
                dve.wait_ge(rstd_ready, c.next(rstd_ready))

                def inner_units():
                    with c.loop(dve, KT // 2) as i:
                        for j in range(2):
                            def before():
                                then(dve.scalar_tensor_tensor(t2[:, j], acc[j][:], 0.0, rstd[:], ALU.max, ALU.mult), relu_ready)
                                free(j)

                            def after():
                                dve.wait_ge(hi_tile, c.next(hi_tile))
                                mark(dve.tensor_tensor(tile(h_lo, i * 2 + j), e2[:, j], tile(h_hi, i * 2 + j).bitcast(F32), ALU.subtract), pair_ready)
                            step(j, before, after)

                with c.loop(dve, FFQ - 1):
                    inner_units()
                    add_units(False)
                inner_units()
                add_units(True)
                dve.sem_inc(sum_ready, 1)
            dve.wait_ge(rstd_ready, c.next(rstd_ready))
            for k in range(KT):
                mark(dve.scalar_tensor_tensor(x[:, k], x[:, k], fin_w[:, k:k + 1], rstd[:], ALU.mult, ALU.mult), final_ready)


def _layout(x, mem, positions, norm_mix, w_in, b_gate, conv_w, conv_b, dt_bias, a_log, d_skip, ssm_norm,
            w_br_ret, w_br_ssm, w_out, norm_xa, norm_mem, xa_wq, xa_wkv, xa_wo, norm_mlp, mlp_w1, mlp_w2, norm_final):
    f = np.float32

    def units(w):
        r, n = w.shape
        return w.reshape(r // D, KT, P, n // P, P).transpose(3, 0, 2, 1, 4)

    stream = np.zeros((DEPTH * UNITS + AHEAD, P, KT, P), f)
    lps = np.zeros((DEPTH, P, LPN), f)
    gps = np.zeros((DEPTH * GROUPS, P, GPN), f)

    def cols(v):
        return v.reshape(-1, P).T

    for l in range(DEPTH):
        at = l * UNITS

        def put(u, at):
            stream[at:at + len(u)] = u
            return at + len(u)

        wi = w_in[l]
        stream[at + 1, :, :, 0:SSM_HEADS] = wi[:, O_DT:O_DT + SSM_HEADS].reshape(KT, P, SSM_HEADS).transpose(1, 0, 2)
        at += 2

        def part(o, n):
            return units(wi[:, o:o + n * P])[:, 0]

        for g in range(GROUPS):
            for o, n in ((O_B + g * P, 1), (O_C + g * P, 1), (O_XS + g * 2 * P, 2), (O_Z + g * 2 * P, 2)):
                at = put(part(o, n), at)
        br, gates = units(w_br_ssm[l]), part(O_GATE, 2 * KT)
        at = put(gates[KT:2 * KT], at)
        for n in range(KT):
            at = put(br[n], at)
        for h in range(RET_HEADS):
            for o, n in ((O_Q + h * P, 1), (O_K + h * P, 1), (O_V + h * 2 * P, 2), (O_G + h * 2 * P, 2)):
                at = put(part(o, n), at)
        at = put(gates[0:KT], at)
        at = put(units(w_br_ret[l])[:, 0], at)
        at = put(units(w_out[l])[:, 0], at)
        q, kv = units(xa_wq[l])[:, 0], units(xa_wkv[l])[:, 0]
        for h in range(4):
            at = put(kv[2 * h:2 * h + 2], at)
            at = put(kv[KT + 2 * h:KT + 2 * h + 2], at)
            at = put(q[2 * h:2 * h + 2], at)
        at = put(units(xa_wo[l])[:, 0], at)
        w1, w2 = units(mlp_w1[l])[:, 0], units(mlp_w2[l])
        for q4 in range(FFQ):
            at = put(w1[q4 * KT:(q4 + 1) * KT], at)
            at = put(w2[:, q4], at)
        assert at == (l + 1) * UNITS

        for o, v in ((L_MIX, norm_mix), (L_XA, norm_xa), (L_MEM, norm_mem), (L_MLP, norm_mlp), (L_GATE, b_gate)):
            lps[l, :, o:o + v.shape[1] // P] = cols(v[l])
        lps[l, :, L_ALOG:L_ALOG + SSM_HEADS] = a_log[l][None, :]
        lps[l, 0:SSM_HEADS, L_DTB] = dt_bias[l]
        skip = np.repeat(d_skip[l], HD)
        for g in range(GROUPS):
            gpt = gps[l * GROUPS + g]
            for j, o in enumerate((SSM_INNER + g * P, SSM_INNER + BC + g * P, g * 2 * P, g * 2 * P + P)):
                gpt[:, G_TAP + 4 * j:G_TAP + 4 * j + 4] = conv_w[l][:, o:o + P].T
                gpt[:, G_BIAS + j] = conv_b[l][o:o + P]
            gpt[:, G_SKIP:G_SKIP + 2] = cols(skip[g * 2 * P:(g + 1) * 2 * P])
            gpt[:, G_NORM:G_NORM + 2] = cols(ssm_norm[l][g * 2 * P:(g + 1) * 2 * P])

    par = np.concatenate([lps, gps.reshape(DEPTH, GROUPS, P, GPN).transpose(0, 2, 1, 3).reshape(DEPTH, P, GROUPS * GPN)], 2)

    i = np.arange(P)
    upto = (i[:, None] <= i[None, :]).astype(f)
    mask = (i[:, None] // CHUNK <= i[None, :] // CHUNK).astype(f)
    lg = np.log1p(-(2.0 ** (-5.0 - np.arange(RET_HEADS))))
    m, l_ = np.arange(P)[:, None], np.arange(S)[None, :]
    decay = np.exp(lg[None, :, None] * np.abs(l_ - m)[:, None, :]) * (m // CHUNK <= l_ // CHUNK)[:, None, :] * P ** -0.5
    freq = np.zeros((P, 4), f)
    freq[:, 0] = np.tile(10000.0 ** (-np.arange(0, P, 2) / P), 2)
    freq[64:, 1] = 0.25
    freq[64:, 2] = np.pi / 2
    return {
        "stream": stream, "par": np.ascontiguousarray(par.transpose(1, 0, 2).reshape(P, DEPTH * PARN)),
        "x": np.ascontiguousarray(x[0].T.reshape(KT, P, S).transpose(1, 0, 2)),
        "mem": np.ascontiguousarray(mem[0].T.reshape(KT, P, MEM).transpose(1, 0, 2)),
        "pos": np.ascontiguousarray(positions[0]),
        "fin_w": np.ascontiguousarray(cols(norm_final)),
        "ident": np.eye(P, dtype=f), "upto": upto, "mask": mask,
        "decay": decay.astype(f), "freq": freq,
    }


def kernel(**inputs):
    import concourse.bacc as bacc
    from concourse.bass_utils import run_bass_kernel_spmd

    arrays = _layout(**{k: np.asarray(v) for k, v in inputs.items()})

    def build(per):
        nc = bacc.Bacc("TRN2", target_bir_lowering=False, num_devices=1)
        a = {n: nc.dram_tensor(f"in_{n}", v.shape, mybir.dt.from_np(v.dtype), kind="ExternalInput").ap() for n, v in arrays.items()}
        a["out"] = nc.dram_tensor("out_0", [P, KT, S], F32, kind="ExternalOutput").ap()
        program(nc, a, per)
        return nc

    per = {}
    build(per)
    nc = build(per)
    r = run_bass_kernel_spmd(nc, [{f"in_{n}": v for n, v in arrays.items()}], core_ids=[0])
    out = r.results[0]["out_0"]
    return np.ascontiguousarray(out.transpose(1, 0, 2).reshape(D, S).T)[None]
```
